# Optimizing a Trainium2 kernel written in Bass

```python
import math, functools
import jax, jax.numpy as jnp
from jax import lax
import numpy as np

D_MODEL = 2048
BATCH = 1
SEQ = 256
DEPTH = 1

GRID_W = 64
CTX_LEN = 256

DN_HEADS = 16
DN_DK = 128
DN_DV = 128
DN_QK_W = DN_HEADS * DN_DK
DN_V_W = DN_HEADS * DN_DV
DN_CONV = 5
DN_CHUNK = 64
HY_W = D_MODEL
HY_ORDER = 2
HY_CONV = 3
HY_BANDS = 16
HY_EMB = 1 + 2 * HY_BANDS
HY_HIDDEN = 64
HY_FILTER_GAIN = 0.05
HY_DECAY_TARGET = 1e-2
HY_FAST_DECAY = 0.3
HY_SLOW_DECAY = 1.5
OFF_Q = 0
OFF_K = OFF_Q + DN_QK_W
OFF_V = OFF_K + DN_QK_W
OFF_Z = OFF_V + DN_V_W
OFF_AB = OFF_Z + DN_V_W
OFF_HY = OFF_AB + 4 * DN_HEADS
OFF_GATE = OFF_HY + 3 * HY_W
PROJ_W = OFF_GATE + 2 * D_MODEL
PEER_NKEYS = 128
PEER_EXPERTS = PEER_NKEYS * PEER_NKEYS
PEER_HEADS = 8
PEER_TOPK = 16
PEER_DKEY = 256
PEER_HALF = PEER_DKEY // 2
PEER_BLOCK = 128
DEEPNORM_ALPHA = (2 * DEPTH) ** 0.25
DEEPNORM_BETA = (8 * DEPTH) ** -0.25
LN_EPS = 1e-5
RMS_EPS = 1e-6

kernel_name = 'hybrid_gdn_hyena_peer_diffusion_block'

F32 = jnp.float32

def layer_norm(x, g, b):
    xf = x.astype(F32)
    mu = jnp.mean(xf, -1, keepdims=True)
    var = jnp.mean(jnp.square(xf - mu), -1, keepdims=True)
    return ((xf - mu) * lax.rsqrt(var + LN_EPS) * g.astype(F32) + b.astype(F32)).astype(x.dtype)

def rms_norm(x, w):
    xf = x.astype(F32)
    return xf * lax.rsqrt(jnp.mean(xf * xf, -1, keepdims=True) + RMS_EPS) * w.astype(F32)

def l2_normalize(x):
    xf = x.astype(F32)
    return xf * lax.rsqrt(jnp.sum(xf * xf, -1, keepdims=True) + 1e-6)

def dwconv_centered(x, w):
    k = w.shape[0]
    pad = k // 2
    n = x.shape[-2]
    xp = jnp.pad(x, [(0, 0)] * (x.ndim - 2) + [(pad, pad), (0, 0)])
    out = xp[..., 0:n, :] * w[0]
    for j in range(1, k):
        out = out + xp[..., j:j + n, :] * w[j]
    return out

def grid_row_conv(x, w, rows):
    b, n, ch = x.shape
    return dwconv_centered(x.reshape(b, rows, GRID_W, ch), w).reshape(b, n, ch)

def delta_inputs(proj, conv, conv_w, a_log, dt_bias):
    b, n, _ = proj.shape
    qkv = jax.nn.silu(conv(proj[..., OFF_Q:OFF_Z], conv_w).astype(F32))
    q = qkv[..., :DN_QK_W].reshape(b, n, DN_HEADS, DN_DK)
    k = qkv[..., DN_QK_W:2 * DN_QK_W].reshape(b, n, DN_HEADS, DN_DK)
    v = qkv[..., 2 * DN_QK_W:].reshape(b, n, DN_HEADS, DN_DV)
    q = l2_normalize(q) * (DN_DK ** -0.5)
    k = l2_normalize(k)
    ab = proj[..., OFF_AB:OFF_HY].astype(F32).reshape(b, n, 2, 2, DN_HEADS)
    g = -jnp.exp(a_log.astype(F32)) * jax.nn.softplus(ab[..., 0, :] + dt_bias.astype(F32))
    beta = jax.nn.sigmoid(ab[..., 1, :])
    bhn = lambda t: t.transpose(0, 2, 1, 3)
    return bhn(q), bhn(k), bhn(v), g.transpose(2, 0, 3, 1), beta.transpose(2, 0, 3, 1)

def gated_delta_chunked(q, k, v, g, beta, s0):
    b, h, t, dk = q.shape
    dv = v.shape[-1]
    c = DN_CHUNK
    nc = t // c
    chunks = lambda a: a.reshape(b, h, nc, c, *a.shape[3:])
    q, k, v = chunks(q), chunks(k), chunks(v)
    g = lax.cumsum(chunks(g), axis=3)
    beta = chunks(beta)
    kb = k * beta[..., None]
    vb = v * beta[..., None]
    tril = jnp.tril(jnp.ones((c, c), dtype=bool))
    strict = jnp.tril(jnp.ones((c, c), dtype=bool), -1)
    decay = jnp.exp(jnp.where(tril, g[..., :, None] - g[..., None, :], -jnp.inf))
    m = jnp.where(strict, jnp.einsum('bhncd,bhnmd->bhncm', kb, k) * decay, 0.0)
    a_mat = m + jnp.eye(c, dtype=F32)
    rhs = jnp.concatenate([vb, kb * jnp.exp(g)[..., None]], axis=-1)
    sol = lax.linalg.triangular_solve(a_mat, rhs, left_side=True, lower=True)
    u, w = sol[..., :dv], sol[..., dv:]
    attn = jnp.einsum('bhncd,bhnmd->bhncm', q, k) * decay

    def step(s, inp):
        q_i, k_i, u_i, w_i, g_i, a_i = inp
        v_new = u_i - jnp.einsum('bhcd,bhdv->bhcv', w_i, s)
        o = jnp.einsum('bhcd,bhdv->bhcv', q_i * jnp.exp(g_i)[..., None], s) + jnp.einsum('bhcm,bhmv->bhcv', a_i, v_new)
        g_last = g_i[..., -1]
        s = s * jnp.exp(g_last)[..., None, None] + jnp.einsum('bhcd,bhcv->bhdv', k_i * jnp.exp(g_last[..., None] - g_i)[..., None], v_new)
        return s, o

    xs = tuple(jnp.moveaxis(a, 2, 0) for a in (q, k, u, w, g, attn))
    s_final, o = lax.scan(step, s0, xs)
    return jnp.moveaxis(o, 0, 2).reshape(b, h, t, dv), s_final

def bidir_delta(q, k, v, g, beta, s0_fwd, s0_bwd):
    o_f, s_f = gated_delta_chunked(q, k, v, g[0], beta[0], s0_fwd)
    flip = lambda a: jnp.flip(a, axis=2)
    o_b, s_b = gated_delta_chunked(flip(q), flip(k), flip(v), flip(g[1]), flip(beta[1]), s0_bwd)
    return o_f + flip(o_b), s_f, s_b

def hyena_filters(n, w1, b1, w2, b2, w3, b3, freq):
    t = jnp.linspace(0.0, 1.0, n, dtype=F32)
    pos = jnp.arange(n, dtype=F32)
    bands = jnp.linspace(1e-4, HY_BANDS - 1, HY_BANDS, dtype=F32)
    ang = (2.0 * math.pi / n) * pos[:, None] * bands[None, :]
    z = jnp.concatenate([t[:, None], jnp.cos(ang), -jnp.sin(ang)], axis=-1)
    fr = freq.astype(F32)
    hid = jnp.sin(fr * (z @ w1.astype(F32) + b1.astype(F32)))
    hid = jnp.sin(fr * (hid @ w2.astype(F32) + b2.astype(F32)))
    filt = (hid @ w3.astype(F32) + b3.astype(F32)).reshape(n, 2, HY_ORDER, HY_W)
    deltas = jnp.abs(jnp.linspace(math.log(HY_DECAY_TARGET) / HY_SLOW_DECAY, math.log(HY_DECAY_TARGET) / HY_FAST_DECAY, HY_W, dtype=F32))
    filt = filt * jnp.exp(-t[:, None] * deltas[None, :])[:, None, None, :]
    circ = jnp.concatenate([filt[:, 0], jnp.zeros((1, HY_ORDER, HY_W), F32), filt[:0:-1, 1]], axis=0)
    return jnp.fft.rfft(circ, axis=0)

def long_conv(u, filt_f, skip):
    n = u.shape[1]
    y = jnp.fft.irfft(jnp.fft.rfft(u, n=2 * n, axis=1) * filt_f, n=2 * n, axis=1)[:, :n]
    return y + u * skip.astype(F32)

def hyena_mix(p, conv, conv_w, filt_f, skip):
    u = conv(p, conv_w).astype(F32)
    v, x1, x2 = u[..., :HY_W], u[..., HY_W:2 * HY_W], u[..., 2 * HY_W:]
    y = x1 * long_conv(v, filt_f[:, 0], skip[0])
    return x2 * long_conv(y, filt_f[:, 1], skip[1])

def merge_branches(o_dn, proj, y_hy, norm_w, w_pa, w_ph, w_out):
    b, n, _ = proj.shape
    dt = proj.dtype
    z = proj[..., OFF_Z:OFF_AB].astype(F32).reshape(b, n, DN_HEADS, DN_DV)
    o = (rms_norm(o_dn.transpose(0, 2, 1, 3), norm_w) * jax.nn.silu(z)).reshape(b, n, DN_V_W).astype(dt)
    gates = jax.nn.sigmoid(proj[..., OFF_GATE:].astype(F32))
    merged = gates[..., :D_MODEL] * (o @ w_pa) + gates[..., D_MODEL:] * (y_hy.astype(dt) @ w_ph)
    return merged.astype(dt) @ w_out

def peer_ffn(h, wq, subkeys, u_tab, v_tab):
    b, n, d = h.shape
    t = b * n
    hf = h.reshape(t, d)
    q = (hf @ wq).astype(F32).reshape(t, PEER_HEADS, 2, PEER_HALF)
    s = jnp.einsum('thpd,hpkd->thpk', q, subkeys.astype(F32))
    top_s, top_i = lax.top_k(s, PEER_TOPK)
    cand_s = (top_s[:, :, 0, :, None] + top_s[:, :, 1, None, :]).reshape(t, PEER_HEADS, PEER_TOPK * PEER_TOPK)
    cand_i = (top_i[:, :, 0, :, None] * PEER_NKEYS + top_i[:, :, 1, None, :]).reshape(t, PEER_HEADS, PEER_TOPK * PEER_TOPK)
    best_s, best_j = lax.top_k(cand_s, PEER_TOPK)
    idx = jnp.take_along_axis(cand_i, best_j, axis=-1).reshape(t, PEER_HEADS * PEER_TOPK)
    gate = jax.nn.softmax(best_s, axis=-1).reshape(t, PEER_HEADS * PEER_TOPK)
    nb = t // PEER_BLOCK

    def block(args):
        xb, ib, gb = args
        act = jax.nn.gelu(jnp.einsum('tkd,td->tk', u_tab[ib], xb).astype(F32), approximate=False)
        return jnp.einsum('tk,tkd->td', (gb * act).astype(xb.dtype), v_tab[ib])

    y = lax.map(block, (hf.reshape(nb, PEER_BLOCK, d), idx.reshape(nb, PEER_BLOCK, -1), gate.reshape(nb, PEER_BLOCK, -1)))
    return y.reshape(b, n, d)

def setup_inputs(seed: int = 0) -> dict:
    key = jax.random.key(seed)
    ks = jax.random.split(key, 40)
    nrm = lambda k, shape, s: jax.random.normal(k, shape, F32) * s
    L = DEPTH
    dt = jnp.exp(jax.random.uniform(ks[8], (L, 2, DN_HEADS), F32, math.log(1e-3), math.log(1e-1)))
    return {
        'x': nrm(ks[0], (BATCH, SEQ, D_MODEL), 1.0),
        'c': nrm(ks[1], (BATCH, D_MODEL), 1.0),
        'ctx': nrm(ks[2], (BATCH, CTX_LEN, D_MODEL), 1.0),
        'c_ctx': nrm(ks[3], (D_MODEL,), 1.0),
        'w_ada': nrm(ks[4], (L, D_MODEL, 6 * D_MODEL), D_MODEL ** -0.5),
        'b_ada': nrm(ks[5], (L, 6 * D_MODEL), 0.02),
        'w_in': nrm(ks[6], (L, D_MODEL, PROJ_W), D_MODEL ** -0.5),
        'dn_conv_w': nrm(ks[7], (L, DN_CONV, 2 * DN_QK_W + DN_V_W), DN_CONV ** -0.5),
        'dn_a_log': jnp.log(jax.random.uniform(ks[9], (L, 2, DN_HEADS), F32, 1.0, 16.0)),
        'dn_dt_bias': dt + jnp.log(-jnp.expm1(-dt)),
        'dn_norm_w': 1.0 + nrm(ks[10], (L, DN_DV), 0.02),
        'hy_conv_w': nrm(ks[11], (L, HY_CONV, 3 * HY_W), HY_CONV ** -0.5),
        'hy_w1': nrm(ks[12], (L, HY_EMB, HY_HIDDEN), HY_EMB ** -0.5),
        'hy_b1': nrm(ks[13], (L, HY_HIDDEN), 0.02),
        'hy_w2': nrm(ks[14], (L, HY_HIDDEN, HY_HIDDEN), HY_HIDDEN ** -0.5),
        'hy_b2': nrm(ks[15], (L, HY_HIDDEN), 0.02),
        'hy_w3': nrm(ks[16], (L, HY_HIDDEN, 2 * HY_ORDER * HY_W), HY_FILTER_GAIN * HY_HIDDEN ** -0.5),
        'hy_b3': nrm(ks[17], (L, 2 * HY_ORDER * HY_W), 0.005),
        'hy_freq': 1.0 + nrm(ks[18], (L, HY_HIDDEN), 0.02),
        'hy_skip': nrm(ks[19], (L, HY_ORDER, HY_W), 0.5),
        'w_branch_dn': nrm(ks[20], (L, DN_V_W, D_MODEL), DN_V_W ** -0.5),
        'w_branch_hy': nrm(ks[21], (L, HY_W, D_MODEL), HY_W ** -0.5),
        'w_out': nrm(ks[22], (L, D_MODEL, D_MODEL), DEEPNORM_BETA * D_MODEL ** -0.5),
        'ln1_g': 1.0 + nrm(ks[23], (L, D_MODEL), 0.02),
        'ln1_b': nrm(ks[24], (L, D_MODEL), 0.02),
        'peer_wq': nrm(ks[25], (L, D_MODEL, PEER_HEADS * PEER_DKEY), D_MODEL ** -0.5),
        'peer_subkeys': nrm(ks[26], (L, PEER_HEADS, 2, PEER_NKEYS, PEER_HALF), PEER_HALF ** -0.5),
        'peer_u': nrm(ks[27], (L, PEER_EXPERTS, D_MODEL), D_MODEL ** -0.5),
        'peer_v': nrm(ks[28], (L, PEER_EXPERTS, D_MODEL), DEEPNORM_BETA),
        'ln2_g': 1.0 + nrm(ks[29], (L, D_MODEL), 0.02),
        'ln2_b': nrm(ks[30], (L, D_MODEL), 0.02),
    }

def reference(x, c, ctx, c_ctx, w_ada, b_ada, w_in, dn_conv_w, dn_a_log, dn_dt_bias, dn_norm_w, hy_conv_w, hy_w1, hy_b1, hy_w2, hy_b2, hy_w3, hy_b3, hy_freq, hy_skip, w_branch_dn, w_branch_hy, w_out, ln1_g, ln1_b, peer_wq, peer_subkeys, peer_u, peer_v, ln2_g, ln2_b):
    b, n, _ = x.shape
    rows = n // GRID_W
    n_ctx = ctx.shape[1]
    lat_conv = functools.partial(grid_row_conv, rows=rows)
    xc = ctx
    for l in range(DEPTH):
        mod = jax.nn.silu(c) @ w_ada[l] + b_ada[l]
        mod_c = jax.nn.silu(c_ctx) @ w_ada[l] + b_ada[l]
        sh1, sc1, g1, sh2, sc2, g2 = jnp.split(mod[:, None, :], 6, axis=-1)
        sh1c, sc1c, g1c, sh2c, sc2c, g2c = jnp.split(mod_c, 6)

        h = x * (1.0 + sc1) + sh1
        hc = xc * (1.0 + sc1c) + sh1c
        proj = h @ w_in[l]
        proj_c = hc @ w_in[l]

        qc, kc, vc, gc, bc = delta_inputs(proj_c, dwconv_centered, dn_conv_w[l], dn_a_log[l], dn_dt_bias[l])
        zero = jnp.zeros((b, DN_HEADS, DN_DK, DN_DV), F32)
        o_c, s_fwd, s_bwd = bidir_delta(qc, kc, vc, gc, bc, zero, zero)
        ql, kl, vl, gl, bl = delta_inputs(proj, lat_conv, dn_conv_w[l], dn_a_log[l], dn_dt_bias[l])
        o_l, _, _ = bidir_delta(ql, kl, vl, gl, bl, s_fwd, s_bwd)

        filt_l = hyena_filters(n, hy_w1[l], hy_b1[l], hy_w2[l], hy_b2[l], hy_w3[l], hy_b3[l], hy_freq[l])
        y_hy = hyena_mix(proj[..., OFF_HY:OFF_GATE], lat_conv, hy_conv_w[l], filt_l, hy_skip[l])

        mix = merge_branches(o_l, proj, y_hy, dn_norm_w[l], w_branch_dn[l], w_branch_hy[l], w_out[l])
        x_new = layer_norm(DEEPNORM_ALPHA * x + g1 * mix, ln1_g[l], ln1_b[l])

        h2 = x_new * (1.0 + sc2) + sh2
        y_peer = peer_ffn(h2, peer_wq[l], peer_subkeys[l], peer_u[l], peer_v[l])
        x_new = layer_norm(DEEPNORM_ALPHA * x_new + g2 * y_peer, ln2_g[l], ln2_b[l])

        if l < DEPTH - 1:
            filt_c = hyena_filters(n_ctx, hy_w1[l], hy_b1[l], hy_w2[l], hy_b2[l], hy_w3[l], hy_b3[l], hy_freq[l])
            y_hy_c = hyena_mix(proj_c[..., OFF_HY:OFF_GATE], dwconv_centered, hy_conv_w[l], filt_c, hy_skip[l])
            mix_c = merge_branches(o_c, proj_c, y_hy_c, dn_norm_w[l], w_branch_dn[l], w_branch_hy[l], w_out[l])
            xc = layer_norm(DEEPNORM_ALPHA * xc + g1c * mix_c, ln1_g[l], ln1_b[l])
            hc2 = xc * (1.0 + sc2c) + sh2c
            xc = layer_norm(DEEPNORM_ALPHA * xc + g2c * peer_ffn(hc2, peer_wq[l], peer_subkeys[l], peer_u[l], peer_v[l]), ln2_g[l], ln2_b[l])
        x = x_new
    return x


_drawn_inputs = setup_inputs


def setup_inputs(seed=0):
    import zlib

    import numpy as np

    out = dict(_drawn_inputs(seed))
    spreads = {}
    factors = {'dn_norm_w': 4.639,
     'hy_b1': 4.627,
     'hy_b2': 3.564,
     'hy_freq': 8.0,
     'ln2_g': 2.848,
     'ln2_b': 2.77}
    for name, (base, spread) in spreads.items():
        noise = np.random.default_rng([zlib.crc32(name.encode()), seed]).standard_normal(out[name].shape)
        drawn = base * np.exp(spread * noise) if base else spread * noise
        out[name] = __import__('jax').numpy.asarray(drawn.astype(out[name].dtype))
    for name, factor in factors.items():
        out[name] = (out[name] * factor).astype(out[name].dtype)
    return out
```

```python
from contextlib import ExitStack

import concourse.bass as bass
from concourse import mybir
import numpy as np

F32 = mybir.dt.float32
U32 = mybir.dt.uint32
ALU = mybir.AluOpType
ACT = mybir.ActivationFunctionType
AX = mybir.AxisListType

P = 128
D = 2048
KT = D // P
SEQ = 256
TOK = 2 * SEQ
CH = 64
NCH = SEQ // CH
H = 16
DK = 128
HD = 2 * H
TAPS = 5
HTAPS = 3
PH = 8
TOPK = 16
NKEYS = 128
SLOTS = PH * TOPK
ALPHA = 2.0 ** 0.25
BIG = 1.0e30
N1 = 512

CONST_COLS = {}
_at = 0
for _n, _w in (("ident", 128), ("ones", 128), ("blockones", 128), ("low_half", 128), ("high_half", 128),
               ("cum_f", 128), ("cum_b", 128), ("tri_f", 64), ("tri_b", 64), ("mask_above", 64),
               ("mask_below", 64), ("cos", 512), ("sin", 512), ("icos", 512), ("isin", 512),
               ("iota16", 16), ("not_first", 1)):
    CONST_COLS[_n] = (_at, _at + _w)
    _at += _w
CONST_W = _at


def constant_table():
    t = np.zeros((P, CONST_W), np.float32)
    p = np.arange(P)[:, None]
    c = np.arange(P)[None, :]
    i = np.arange(CH)[None, :]
    same = (p // CH) == (c // CH)

    def put(name, a):
        lo, hi = CONST_COLS[name]
        t[:, lo:hi] = a

    put("ident", p == c)
    put("ones", 1.0)
    put("blockones", same)
    put("low_half", (p < CH) & (c >= 0))
    put("high_half", (p >= CH) & (c >= 0))
    put("cum_f", same & (p <= c))
    put("cum_b", same & (p >= c))
    put("tri_f", (p % CH) <= i)
    put("tri_b", (p % CH) >= i)
    put("mask_above", BIG * (i > p % CH))
    put("mask_below", BIG * (i < p % CH))
    n = np.arange(SEQ, dtype=np.float64)
    ang = 2 * np.pi * (n[:, None] * (n[None, :] + 0.5)) / (2 * SEQ)
    two = lambda a: a.reshape(2, P, SEQ).transpose(1, 0, 2).reshape(P, 2 * SEQ)
    put("cos", two(np.cos(ang)))
    put("sin", two(np.sin(ang)))
    put("icos", two(np.cos(ang.T) / SEQ))
    put("isin", two(np.sin(ang.T) / SEQ))
    put("iota16", np.arange(16)[None, :])
    put("not_first", p > 0)
    return t


def build(nc, a, out):
    with ExitStack() as ctx:
        made = {}

        def sem(name):
            if name not in made:
                made[name] = ctx.enter_context(nc.semaphore(name))
            return made[name]

        ARENA = 52640
        arena = ctx.enter_context(nc.sbuf_tensor("arena", [P, ARENA], F32))
        bank = [ctx.enter_context(nc.psum_tensor(f"bank{i}", [P, N1], F32)) for i in range(8)]

        def area(at, *shape):
            size = int(np.prod(shape))
            assert at + size <= ARENA, (at, shape)
            v = arena[:, at:at + size]
            if len(shape) == 2:
                v = v.rearrange("p (a b) -> p a b", a=shape[0])
            if len(shape) == 3:
                v = v.rearrange("p (a b c) -> p a b c", a=shape[0], b=shape[1])
            return v

        def dram(name, *shape):
            return nc.dram_tensor(name, shape, F32, kind="Internal").ap()

        mix_scr = dram("mix_scr", 2, P, CH * CH)
        inv_scr = dram("inv_scr", 2, P, CH * CH)
        beta_scr = dram("beta_scr", 2, HD, SEQ)
        rec_scr = dram("rec_scr", H, P, 2048)

        cst = area(0, CONST_W)

        def const(name):
            lo, hi = CONST_COLS[name]
            return cst[:, lo:hi]

        HT0 = 3600
        WR0 = HT0 + KT * TOK
        R0 = WR0 + 4 * KT * P
        assert CONST_W <= HT0
        hT = area(HT0, KT, TOK)
        wring = area(WR0, 4, KT * P).rearrange("p s (k n) -> p s k n", k=KT)
        ada_ring = area(R0, 4, 8 * N1).rearrange("p s (k n) -> p s k n", k=8)
        ada_row = area(R0 + 16384, 2 * D)
        cond = area(52600, KT, 2)
        cols = area(R0 + 20512, 2 * KT, 2)
        condb = area(R0 + 20576, KT, P)
        G0 = R0 + 12288
        w_ab = area(G0, KT, CH)
        ab = area(G0 + 1024, 4, 64)
        xs = area(G0 + 1280, 4, HD)
        sp_m = area(G0 + 1408, 4, HD)
        sp_e = area(G0 + 1536, 4, HD)
        gate_row = area(G0 + 1664, 2, HD)
        gx = area(G0 + 2048, HD, CH)
        xm = area(G0 + 4096, HD, CH)
        xm2 = area(G0 + 6144, H, CH)
        K0 = 50900
        g_tok = area(K0, 4, HD)
        beta = area(K0 + 128, 4, HD)
        gcum = area(K0 + 256, 4, HD)
        eg = area(K0 + 384, 4, HD)
        neg_eg = area(K0 + 512, 4, HD)
        etail = area(K0 + 640, 4, HD)
        etot = area(K0 + 768, 2, 4 * HD)
        dn_nw = area(K0 + 1024, 1)
        eps6 = area(K0 + 1025, 1)
        eps5 = area(K0 + 1026, 1)
        hyc = area(K0 + 1032, 48, HTAPS)
        n_e1f = area(R0, 4, H * CH).rearrange("p t (h i) -> p t h i", h=H)
        n_eb = area(R0 + 4096, 4, H * CH).rearrange("p t (h i) -> p t h i", h=H)
        a_e2f = area(R0 + 8192, 2, H * CH).rearrange("p t (h i) -> p t h i", h=H)
        a_eb = area(R0 + 10240, 2, H * CH).rearrange("p t (h i) -> p t h i", h=H)
        X0 = R0 + 12288
        PADL, PADC = CH + TAPS - 1, SEQ + TAPS - 1
        cw = NCH * PADL + PADC
        cbuf = area(X0, 3, cw)
        acc = area(X0 + 1600, 3, TOK)
        raw = area(X0 + 3200, 3, TOK)
        sq = area(X0 + 4800, 2, TOK)
        nrm = area(X0 + 5900, 2, TOK)
        rec = area(X0 + 7000, 2048)
        mt = area(X0 + 9100, 2, 4 * CH).rearrange("p d (t i) -> p d t i", t=4)
        dnc = area(X0 + 9700, 48, TAPS)
        r_kT = rec[:, 0:512]
        r_qT = rec[:, 512:768]
        r_k = rec[:, 768:1280]
        r_v = rec[:, 1280:1792]
        r_at = rec[:, 1792:2048].rearrange("p (d t i) -> p d t i", d=2, t=2)

        c_lat = [cbuf[:, t, 0:NCH * PADL].rearrange("p (r w) -> p r w", r=NCH) for t in range(3)]
        c_ctx = [cbuf[:, t, NCH * PADL:cw] for t in range(3)]

        zsT = area(R0, KT, SEQ)
        gT = area(R0 + 4096, 2 * KT, SEQ)
        yhT = area(R0 + 12288, KT, SEQ)
        uv = area(R0 + 16384, 2, 2 * D)
        sol = area(R0 + 16384, CH, CH)
        sol_o = area(R0 + 20480, CH, CH)
        sol_t = area(R0 + 12288, CH * CH // 4)
        sol_b = area(R0 + 13400, CH)
        hbuf = area(R0 + 24576, 4, NCH * (CH + 2)).rearrange("p s (r w) -> p s r w", r=NCH)
        hacc = area(R0 + 24576 + 1056, 4, SEQ)
        mixed = area(K0 + 1200, 6, 4 * H).rearrange("p m (t h) -> p m t h", t=4)
        w3c = area(HT0, 4, N1)
        win = area(HT0 + 2048, 2, N1)
        skipc = area(HT0 + 3072, 2, N1)
        fa = area(HT0 + 4096, 2, N1)
        fb = area(HT0 + 5120, 2, N1)
        Fr = area(HT0 + 6144, 2, N1)
        Fi = area(HT0 + 7168, 2, N1)
        t1 = area(HT0 + 8192, 2, N1)
        t2 = area(HT0 + 9216, 2, N1)
        Yr = area(HT0 + 10240, 2, N1)
        Yi = area(HT0 + 11264, 2, N1)
        yb = area(HT0 + 12288, 2, N1)
        zT = area(HT0 + 13312, SEQ)
        hid1 = area(HT0 + 13568, SEQ)
        hid2 = area(HT0 + 13824, SEQ)
        ang = area(HT0 + 14080, SEQ)
        turns = area(HT0 + 14336, SEQ)
        fw1 = area(HT0 + 14592, CH)
        fw2 = area(HT0 + 14656, CH)
        fcol = area(HT0 + 14720, 3)
        mods = area(R0 + 16384, 4, D)
        ada_ring2 = area(HT0, 4, 8 * N1).rearrange("p s (k n) -> p s k n", k=8)
        condb = area(R0 + 24576, KT, P)
        INV0, INV_BUFS, SC0 = R0 + 24576, 1, R0 + 26624
        recs = area(HT0, 8, 2048)
        invs = area(INV0, 4 * INV_BUFS, 512).rearrange("p s (q d t i) -> p s q d t i", q=2, d=2, t=2)
        state = area(SC0, 8, P)
        r_in = area(SC0 + 1024, 4, P)
        v_new = area(SC0 + 1536, 4, P)
        v_tail = area(SC0 + 2048, 4, P)
        o_acc = area(SC0 + 2560, 8, P)
        o_sq = area(SC0 + 3584, P)
        o_ss = area(SC0 + 3712, 8)
        tmp_g = area(R0 + 24576, 2, SEQ)
        wo_ring = area(HT0, 2, 8 * N1).rearrange("p s (k n) -> p s k n", k=8)
        tmp_m = area(R0 + 25600, 2, N1)
        xn = area(R0 + 12288, 2, D)
        lnp = area(R0, 2, D)
        h2 = area(R0 + 8192, 2, D)
        stats = area(K0 + 1200, 2, 24)
        aggr = area(K0 + 1250, 2, 2)
        rstd = area(K0 + 1256, 2)
        h2T = area(HT0, KT, SEQ)
        subk = area(R0 + 24576, KT, NKEYS)
        q_sb = area(R0 + 26624, 4, SEQ)
        sc = area(HT0 + 4096, 2, KT * NKEYS).rearrange("p t (c n) -> p t c n", c=KT)
        tv = area(R0 + 28672, 2, KT * TOPK).rearrange("p t (c n) -> p t c n", c=KT)
        ti = area(R0 + 29184, 2, KT * TOPK).rearrange("p t (c n) -> p t c n", c=KT)
        sc2 = area(WR0, 2, KT * NKEYS).rearrange("p t (c n) -> p t c n", c=KT)
        cand = area(WR0, PH, TOPK * TOPK)
        cand2 = area(WR0 + 2048, PH, TOPK * TOPK)
        onehot = area(WR0 + 4096, SLOTS, TOPK)
        bv = area(R0 + 29696, 2, SLOTS)
        bj = area(R0 + 29952, 2, SLOTS)
        bhi = area(R0 + 30208, 2, SLOTS)
        tf = area(R0 + 26624, 2, KT * TOPK).rearrange("p t (c n) -> p t c n", c=KT)
        i0 = area(R0 + 27136, SLOTS)
        i1 = area(R0 + 27264, SLOTS)
        idx = area(R0 + 30464, 2, SLOTS)  
        idx_all = area(R0 + 30464, 2 * SLOTS + TOPK)
        gate = area(K0, 2, SLOTS)
        esum = area(K0 + 256, PH)
        ring = area(HT0, 8, D)
        y_acc = area(R0 + 4096, 2, D)
        junk = area(R0 + 24576, D)
        idx_u = area(K0 + 300, TOPK)
        idx_v = area(K0 + 320, TOPK)
        dots = area(K0 + 340, TOPK)
        gelu = area(K0 + 360, TOPK)
        coef = area(K0 + 380, TOPK)
        assert K0 >= R0 + 30720

        block = ctx.enter_context(nc.Block())

        HF = (slice(0, CH), slice(CH, P))

        @block.sync
        def _(sp):
            sp.dma_start(cst, a["consts"]).then_inc(sem("consts_in"), 16)
            sp.dma_start(cond, a["cond"]).then_inc(sem("cond_in"), 16)
            sp.dma_start(ada_row[0:2, :], a["b_ada"][0:2 * D].rearrange("(o n) -> o n", o=1).broadcast_to([2, 2 * D])
                         ).then_inc(sem("bada_in"), 16)
            with sp.Fori(0, 4) as i:
                for s in range(4):
                    sp.wait_ge(sem("ada_used"), 1 + i * 4 + s)
                    sp.dma_start(ada_ring[:, s], a["w_ada"][bass.ds(i * 4 + s, 1)].rearrange("o p k n -> p (o k) n")
                                 ).then_inc(sem(f"slot_in{4 + s}"), 16)
            sp.dma_start(hT, a["xcT"]).then_inc(sem("x_in"), 16)
            sp.wait_ge(sem("ada_used"), 4 + 16)
            sp.dma_start(w_ab, a["w_ab"]).then_inc(sem("wab_in"), 16)
            sp.dma_start(gate_row[:, 0, :], a["dn_a_log"].partition_broadcast(P)).then_inc(sem("gate_in"), 16)
            sp.dma_start(gate_row[:, 1, :], a["dn_dt_bias"].partition_broadcast(P)).then_inc(sem("gate_in"), 16)
            sp.dma_start(hyc, a["hy_conv"]).then_inc(sem("hyc_in"), 16)
            sp.dma_start(dn_nw, a["dn_norm_w"]).then_inc(sem("hyc_in"), 16)
            sp.wait_ge(sem("decay_done"), 1)
            sp.dma_start(dnc, a["dn_conv"]).then_inc(sem("dnc_in"), 16)
            with sp.Fori(0, H) as h:
                for t in range(3):
                    sp.wait_ge(sem("proj"), 1 + 3 * h + t)
                    sp.dma_start(wring[:, t], a["w_in"][bass.ds(3 * h + t, 1)].rearrange("o p k n -> p (o k) n")
                                 ).then_inc(sem(f"slot_in{t}"), 16)
            sp.wait_ge(sem("proj"), 3 + 3 * H)
            with sp.Fori(0, 12) as i:
                for s in range(4):
                    sp.wait_ge(sem("zg_proj"), 1 + i * 4 + s)
                    sp.dma_start(wring[:, s], a["w_in"][bass.ds(i * 4 + (48 + s), 1)].rearrange("o p k n -> p (o k) n")
                                 ).then_inc(sem(f"slot_in{s}"), 16)
            sp.wait_ge(sem("zg_proj"), 4 + 48)
            with sp.Fori(0, 12) as i:
                for s in range(4):
                    sp.wait_ge(sem("hy_proj"), 1 + i * 4 + s)
                    sp.dma_start(wring[:, s], a["w_in"][bass.ds(i * 4 + (96 + s), 1)].rearrange("o p k n -> p (o k) n")
                                 ).then_inc(sem(f"slot_in{s}"), 16)
            sp.wait_ge(sem("hy_proj"), 4 + 48)
            sp.dma_start(zT[0:33, :], a["hy_z"]).then_inc(sem("hyf_in"), 16)
            sp.dma_start(fw1[0:33, :], a["hy_w1"]).then_inc(sem("hyf_in"), 16)
            sp.dma_start(fw2[0:CH, :], a["hy_w2"]).then_inc(sem("hyf_in"), 16)
            sp.dma_start(fcol[0:CH, :], a["hy_cols"]).then_inc(sem("hyf_in"), 16)
            with sp.Fori(0, 4) as n:
                sp.wait_ge(sem("fil_used"), 1 + 2 * n)
                sp.dma_start(w3c[0:65], a["hy_w3"][bass.ds(n, 1)].rearrange("o p k n -> p (o k) n")).then_inc(sem("w3_in"), 16)
                sp.dma_start(win, a["hy_win"][bass.ds(n, 1)].rearrange("o p k n -> p (o k) n")).then_inc(sem("w3_in"), 16)
                sp.dma_start(skipc[0:1], a["hy_skip"][bass.ds(n, 1)].rearrange("o (p k) n -> (o p) k n", p=1)).then_inc(sem("w3_in"), 16)
            sp.wait_ge(sem("hyena_done"), 1)
            sp.dma_start(mods.rearrange("p s n -> p (s n)"), a["b_ada"][2 * D:6 * D].partition_broadcast(P)).then_inc(sem("mods_in"), 16)
            with sp.Fori(0, 8) as i:
                for s in range(4):
                    sp.wait_ge(sem("ada2_used"), 1 + i * 4 + s)
                    sp.dma_start(ada_ring2[:, s], a["w_ada"][bass.ds(i * 4 + (16 + s), 1)].rearrange("o p k n -> p (o k) n")
                                 ).then_inc(sem(f"slot_in{4 + s}"), 16)
            sp.wait_ge(sem("ada2_used"), 4 + 32)
            sp.wait_ge(sem("inv_out"), 32)
            sp.wait_ge(sem("rec_out"), 16 * H)
            with sp.Fori(0, 2) as i:
                for r in range(2):
                    sp.wait_ge(sem("o_merged"), 1 + i * 8 + 4 * r)
                    for u in range(4):
                        h = i * 8 + (4 * r + u)
                        sp.dma_start(recs[:, 4 * r + u], rec_scr[bass.ds(h, 1)].rearrange("o p n -> p (o n)")).then_inc(sem(f"rec_in{r}"), 16)
                    if INV_BUFS == 1:
                        sp.wait_ge(sem("o_merged"), 5 + i * 8 + 4 * r)
                    for u in range(4):
                        h = i * 8 + (4 * r + u)
                        for q in range(2):
                            for d in range(2):
                                src = inv_scr[q].rearrange("(d h c) (a b) -> d h (c a) b", d=2, h=H, b=CH)[d, bass.ds(h, 1)]
                                src = src.rearrange("o (t p) b -> p (o t) b", p=P)
                                sp.dma_start(invs[:, (4 * r + u) % (4 * INV_BUFS), q, d], src).then_inc(sem(f"rec_in{r}"), 16)
            with sp.Fori(0, 8) as i:
                for s in range(4):
                    sp.wait_ge(sem("br_proj"), 1 + i * 4 + s)
                    sp.dma_start(wring[:, s], a["w_branch"][bass.ds(i * 4 + s, 1)].rearrange("o p k n -> p (o k) n")
                                 ).then_inc(sem(f"slot_in{s}"), 16)
            sp.wait_ge(sem("br_proj"), 4 + 32)
            sp.dma_start(xn, a["x"].rearrange("(t p) n -> p t n", p=P)).then_inc(sem("xres_in"), 16)
            sp.dma_start(lnp[:, 0, :], a["ln1_g"].partition_broadcast(P)).then_inc(sem("ln1_in"), 16)
            sp.dma_start(lnp[:, 1, :], a["ln1_b"].partition_broadcast(P)).then_inc(sem("ln1_in"), 16)
            with sp.Fori(0, 4) as i:
                for s in range(2):
                    sp.wait_ge(sem("wo_used"), 1 + i * 2 + s)
                    sp.dma_start(wo_ring[:, s], a["w_out"][bass.ds(i * 2 + s, 1)].rearrange("o p k n -> p (o k) n")
                                 ).then_inc(sem(f"wo_in{s}"), 16)
            sp.wait_ge(sem("o_merged"), 5 + 16)
            sp.wait_ge(sem("mix_added"), 9)
            sp.dma_start(subk, a["subkeys"]).then_inc(sem("subk_in"), 16)
            with sp.Fori(0, 4) as i:
                for s in range(4):
                    sp.wait_ge(sem("q_proj"), 1 + i * 4 + s)
                    sp.dma_start(wring[:, s], a["w_q"][bass.ds(i * 4 + s, 1)].rearrange("o p k n -> p (o k) n")
                                 ).then_inc(sem(f"slot_in{s}"), 16)
            sp.wait_ge(sem("ln1_done"), 1)
            sp.dma_start(lnp[:, 0, :], a["ln2_g"].partition_broadcast(P)).then_inc(sem("ln2_in"), 16)
            sp.dma_start(lnp[:, 1, :], a["ln2_b"].partition_broadcast(P)).then_inc(sem("ln2_in"), 16)
            for t in range(2):
                sp.wait_ge(sem("result"), t + 1)
                sp.dma_start(out[t * P:(t + 1) * P, :], xn[:, t, :]).then_inc(sem("out_done"), 16)
            sp.wait_ge(sem("out_done"), 32)

        @block.tensor
        def _(pe):
            mm = nc.tensor.matmul
            pe.sem_inc(sem("o_turned"), 1)
            pe.wait_ge(sem("consts_in"), 16)
            pe.sem_inc(sem("ada_used"), 4)
            pe.wait_ge(sem("cond_done"), 1)
            with pe.Fori(0, 4) as i:
                for s in range(4):
                    j, half = s // 2, s % 2
                    pe.wait_ge(sem(f"slot_in{4 + s}"), i * 16 + 16)
                    if half == 0:
                        pe.wait_ge(sem("row_done"), 1 + i * 2 + j)
                    for k in range(8):
                        m = mm(bank[j][0:2, :], cond[:, half * 8 + k, :], ada_ring[:, s, k, :],
                               start=(half == 0 and k == 0), stop=(half == 1 and k == 7))
                    m.then_inc(sem("ada_used"), 1)
            pe.wait_ge(sem("row_done"), 2 + 8)
            for t in range(2 * KT):
                m = mm(bank[2][:, 2 * t:2 * t + 2], ada_row[0:2, t * P:(t + 1) * P], const("ident")[0:2, 0:2],
                       start=True, stop=True)
            m.then_inc(sem("cols_ready"), 1)
            pe.wait_ge(sem("wab_in"), 16)
            pe.wait_ge(sem("h_done"), 32)
            for t in range(4):
                for half in range(2):
                    c0 = SEQ * (t // 2) + CH * ((0, 3), (1, 2))[t % 2][half]
                    for k in range(KT):
                        m = mm(bank[0][HF[half], t * 64:t * 64 + 64], hT[:, k, c0:c0 + CH], w_ab[:, k, :],
                               start=(k == 0), stop=(k == KT - 1))
            m.then_inc(sem("gating_mm"), 1)
            pe.wait_ge(sem("beta_done"), 1)
            for t in range(4):
                m = mm(bank[4][0:HD, t * P:(t + 1) * P], beta[:, t, :], const("ident"), start=True, stop=True)
            m.then_inc(sem("gating_mm"), 1)
            pe.wait_ge(sem("gating_step"), 6)
            gd = lambda d: g_tok[:, :, d * H:(d + 1) * H]
            cum = bank[1][:, 0:128].rearrange("p (t h) -> p t h", t=4)
            mm(cum[:, :, 0:H], const("cum_f"), gd(0), start=True, stop=True)
            m = mm(cum[:, :, H:HD], const("cum_b"), gd(1), start=True, stop=True)
            m.then_inc(sem("gating_mm"), 1)
            gall = g_tok.rearrange("p t h -> p (t h)")
            mm(bank[2][:, 0:128], const("blockones"), gall, start=True, stop=True)
            mm(bank[2][:, 128:256], const("low_half"), gall, start=True, stop=True)
            m = mm(bank[2][:, 256:384], const("high_half"), gall, start=True, stop=True)
            m.then_inc(sem("gating_mm"), 1)
            for t in range(4):
                pe.wait_ge(sem("gx_done"), t + 1)
                if t == 0:
                    pe.wait_ge(sem("gating_step"), 7)
                else:
                    pe.wait_ge(sem("xm_done"), 4 * t)
                for b in range(4):
                    m = mm(bank[4 + b][:, :], const("blockones"), gx.rearrange("p h i -> p (h i)")[:, b * N1:(b + 1) * N1],
                           start=True, stop=True)
                m.then_inc(sem("gb_ready"), 1)

            def project(h, t):
                n = SEQ if t == 0 else TOK
                pe.wait_ge(sem(f"slot_in{t}"), 16 * h + 16)
                pe.wait_ge(sem("proj_copied"), 3 * h + t)
                for k in range(KT):
                    m = mm(bank[t][:, 0:n], wring[:, t, k, :], hT[:, k, 0:n], start=(k == 0), stop=(k == KT - 1))
                m.then_inc(sem("proj"), 1)

            def norms(h):
                for j, n in ((0, SEQ), (1, TOK)):
                    pe.wait_ge(sem("squared"), 2 * h + j + 1)
                    pe.wait_ge(sem("rooted"), 1 + 2 * h)
                    mm((bank[3] if j == 0 else bank[7])[:, 0:n], const("ones"), sq[:, j, 0:n], start=True, stop=True
                       ).then_inc(sem("ssq"), 1)

            def turn(h):
                pe.wait_ge(sem("silued"), 3 * h + 3)
                pe.wait_ge(sem("v_copied"), 1 + h)
                for t in range(4):
                    m = nc.tensor.transpose(bank[5][:, t * P:(t + 1) * P], raw[:, 2, t * P:(t + 1) * P], const("ident"))
                m.then_inc(sem("v_turned"), 1)
                pe.wait_ge(sem("normed"), 1 + 2 * h + 2)
                pe.wait_ge(sem("k_copied"), 1 + h)
                for t in range(4):
                    m = nc.tensor.transpose(bank[4][:, t * P:(t + 1) * P], r_kT[:, t * P:(t + 1) * P], const("ident"))
                m.then_inc(sem("k_turned"), 1)
                pe.wait_ge(sem("gram_used"), 1 + 4 * h)
                for t in range(4):
                    for half in range(2):
                        cs = slice(t * P + half * CH, t * P + half * CH + CH)
                        mm(bank[6][HF[half], t * CH:(t + 1) * CH], r_kT[:, cs], r_kT[:, cs], start=True, stop=True)
                for t in range(2):
                    for half in range(2):
                        cs = slice(t * P + half * CH, t * P + half * CH + CH)
                        m = mm(bank[6][HF[half], 256 + t * CH:256 + (t + 1) * CH], r_kT[:, cs], r_qT[:, cs],
                               start=True, stop=True)
                m.then_inc(sem("gram"), 1)

            pe.wait_ge(sem("decay_done"), 1)
            pe.sem_inc(sem("proj"), 3)
            for t in range(3):
                project(0, t)
            with pe.Fori(1, H) as h:
                project(h, 0)
                norms(h - 1)
                project(h, 1)
                project(h, 2)
                turn(h - 1)
            norms(H - 1)
            turn(H - 1)

            def weights_in(slot, use):
                pe.wait_ge(sem(f"slot_in{slot}"), use * 16 + (16 * H * (slot < 3) + 16))

            def wide(slot, b, n_ap):
                for k in range(KT):
                    m = mm(bank[b][:, 0:SEQ], wring[:, slot, k, :], n_ap[:, k, 0:SEQ], start=(k == 0), stop=(k == KT - 1))
                return m

            pe.sem_inc(sem("zg_proj"), 4)
            with pe.Fori(0, 12) as i:
                for s in range(4):
                    weights_in(s, i)
                    pe.wait_ge(sem("zg_evac"), 1 + i * 4 + s)
                    wide(s, s, hT).then_inc(sem("zg_proj"), 1)
            pe.sem_inc(sem("hy_proj"), 4)
            pe.sem_inc(sem("hy_turned"), 4)
            pe.wait_ge(sem("zg_evac"), 4 + 48)

            def hy_project(i, s):
                weights_in(s, i + 12)
                pe.wait_ge(sem("hy_evac"), 1 + i * 4 + s)
                wide(s, s, hT).then_inc(sem("hy_proj"), 1)

            def hy_turn(i, s):
                pe.wait_ge(sem("hy_tap"), 10 + 3 * (i * 4 + s) + 3)
                pe.wait_ge(sem("hy_tcopied"), 1 + i * 4 + s)
                for t in range(2):
                    m = nc.tensor.transpose(bank[4 + s][:, t * P:(t + 1) * P], hacc[:, s, t * P:(t + 1) * P], const("ident"))
                m.then_inc(sem("hy_turned"), 1)

            with pe.Fori(0, 8) as i:
                hy_project(i, 0)
                hy_project(i, 1)
                hy_turn(i, 0)
                hy_project(i, 2)
                hy_turn(i, 1)
                hy_project(i, 3)
                hy_turn(i, 2)
                hy_turn(i, 3)
            with pe.Fori(8, 12) as i:
                for s in range(4):
                    hy_project(i, s)
            pe.wait_ge(sem("hyf_in"), 64)
            pe.wait_ge(sem("hy_evac"), 4 + 48)
            mm(bank[0][0:CH, 0:SEQ], fw1[0:33, :], zT[0:33, :], start=True, stop=True).then_inc(sem("hid_mm"), 1)
            pe.wait_ge(sem("hid_done"), 1)
            mm(bank[1][0:CH, 0:SEQ], fw2[0:CH, :], hid1[0:CH, :], start=True, stop=True).then_inc(sem("hid_mm"), 1)
            pe.wait_ge(sem("hid_done"), 3)
            pe.wait_ge(sem("hy_tcopied"), 4 + 32)

            def filters(n, o):
                pe.wait_ge(sem("w3_in"), 48 * n + 48)
                for t in range(2):
                    for d in range(2):
                        m = mm(bank[4 + 2 * d + t][:, :], hid2[0:65, t * P:(t + 1) * P], w3c[0:65, 2 * d + o, :], start=True, stop=True)
                m.then_inc(sem("fil_ready"), 1)

            def convolve(n, o, last):
                c = n * 2 + o
                pe.wait_ge(sem("fil_used"), c + 2)
                for f in range(2):
                    for src, w, b in ((fa, "cos", 4), (fb, "sin", 6)):
                        for t in range(2):
                            m = mm(bank[b + f][:, :], const(w)[:, t * SEQ + f * P:t * SEQ + (f + 1) * P], src[:, t, :],
                                   start=(t == 0), stop=(t == 1))
                    m.then_inc(sem("spec_ready"), 1)
                pe.wait_ge(sem("inv_used"), n * 6 + (1 + 2 * o))
                for f in range(2):
                    for w, b in (("cos", 0), ("sin", 2)):
                        for t in range(2):
                            rhs = yb[:, t, :] if o else uv[:, t, bass.ds(n * N1, N1)]
                            m = mm(bank[b + f][:, :], const(w)[:, t * SEQ + f * P:t * SEQ + (f + 1) * P], rhs,
                                   start=(t == 0), stop=(t == 1))
                    m.then_inc(sem("sig_ready"), 1)
                if not last:
                    pe.wait_ge(sem("spec_copied"), c * 4 + 4)
                    filters(n + o, 1 - o)
                pe.wait_ge(sem("prod_done"), c * 12 + 13)
                if o == 0:
                    for t in range(2):
                        for e, (y, w) in enumerate(((Yr, "icos"), (Yi, "isin"))):
                            for f in range(2):
                                m = mm(bank[t][:, :], const(w)[:, f * SEQ + t * P:f * SEQ + (t + 1) * P], y[:, f, :],
                                       start=(e == 0 and f == 0), stop=(e == 1 and f == 1))
                        m.then_inc(sem("inv_ready"), 1)
                else:
                    for b in range(4):
                        for e, (y, w) in enumerate(((Yr, "icos"), (Yi, "isin"))):
                            for f in range(2):
                                m = mm(bank[b][:, 0:SEQ], y[:, f, b * P:(b + 1) * P], const(w)[:, f * SEQ:(f + 1) * SEQ],
                                       start=(e == 0 and f == 0), stop=(e == 1 and f == 1))
                        m.then_inc(sem("inv_ready"), 1)

            filters(0, 0)
            with pe.Fori(0, 3) as n:
                convolve(n, 0, False)
                convolve(n, 1, False)
            convolve(3, 0, False)
            convolve(3, 1, True)
            pe.sem_inc(sem("ada2_used"), 4)
            pe.wait_ge(sem("condb_done"), 1)
            pe.wait_ge(sem("inv_used"), 25)
            with pe.Fori(0, 8) as i:
                for s in range(4):
                    j, half = s // 2, s % 2
                    pe.wait_ge(sem(f"slot_in{4 + s}"), i * 16 + 80)
                    if half == 0:
                        pe.wait_ge(sem("mods_done"), 1 + i * 2 + j)
                    for k in range(8):
                        m = mm(bank[j][:, :], condb[:, half * 8 + k, :], ada_ring2[:, s, k, :],
                               start=(half == 0 and k == 0), stop=(half == 1 and k == 7))
                    m.then_inc(sem("ada2_used"), 1)
            pe.wait_ge(sem("mods_done"), 2 + 16)
            with pe.Fori(0, 2) as i:
                for r in range(2):
                    grp = i * 2 + r
                    pe.wait_ge(sem(f"rec_in{r}"), 320 * i + 320)
                    kT = lambda u, c: recs[:, 4 * r + u, c:c + CH]
                    qT = lambda u, c: recs[:, 4 * r + u, 512 + c:512 + c + CH]
                    for g in range(8):
                        q, s = g // 4, g % 4
                        t = (0, 1, 1, 0)[s]
                        T = 2 * (1 - q) + t
                        hf = ((0, 1), (1, 0))[s // 2]
                        for u in range(4):
                            A = bank[2 * u]
                            if g == 0:
                                pe.wait_ge(sem("state_zero"), grp + 1)
                            else:
                                pe.wait_ge(sem("state_done"), grp * 56 + ((g - 1) * 8 + 2 * u + 2))
                            for d in range(2):
                                m = mm(A[HF[hf[d]], 0:P], kT(u, T * P + hf[d] * CH), state[:, 2 * u + d, :], start=True, stop=True)
                            if q:
                                for d in range(2):
                                    m = mm(A[HF[hf[d]], P:2 * P], qT(u, t * P + hf[d] * CH), state[:, 2 * u + d, :], start=True, stop=True)
                            m.then_inc(sem("ks_ready"), 1)
                        for u in range(4):
                            pe.wait_ge(sem("r_done"), grp * 32 + (g * 4 + u + 1))
                            pe.sem_inc(sem("pe_passed"), 1)
                            for d in range(2):
                                hh = HF[hf[d]]
                                m = mm(bank[2 * u + 1][hh, 0:P], invs[hh, (4 * r + u) % (4 * INV_BUFS), 1 - q, d, t, :], r_in[hh, u, :],
                                       start=True, stop=True)
                            m.then_inc(sem("vn_ready"), 1)
                        for u in range(4):
                            if q:
                                pe.wait_ge(sem("vn_done"), grp * 16 + ((g - 4) * 4 + u + 1))
                                pe.sem_inc(sem("pe_passed"), 1)
                                for d in range(2):
                                    hh = HF[hf[d]]
                                    at = recs[hh, 4 * r + u, 1792 + (2 * d + t) * CH:1792 + (2 * d + t + 1) * CH]
                                    m = mm(bank[2 * u + 1][hh, P:2 * P], at, v_new[hh, u, :], start=True, stop=True)
                                m.then_inc(sem("av_ready"), 1)
                        for u in range(4):
                            if g < 7:
                                if q:
                                    pe.wait_ge(sem("o_added"), grp * 32 + ((g - 4) * 8 + u + 1))
                                    pe.wait_ge(sem("av_ready"), grp * 16 + ((g - 4) * 4 + u + 1))
                                pe.wait_ge(sem("vtail_done"), grp * 28 + (g * 4 + u + 1))
                                for d in range(2):
                                    hh = HF[hf[d]]
                                    k_tok = recs[hh, 4 * r + u, 768 + T * P:768 + (T + 1) * P]
                                    m = mm(bank[2 * u + d][:, (2 + d) * P:(3 + d) * P], k_tok, v_tail[hh, u, :], start=True, stop=True)
                                m.then_inc(sem("upd_ready"), 1)
                    for u in range(4):
                        pe.wait_ge(sem("o_normed"), grp * 8 + (2 * u + 2))
                        for t in range(2):
                            m = nc.tensor.transpose(bank[2 * u + 1][:, (2 + t) * P:(3 + t) * P], o_acc[:, 2 * u + t, :], const("ident"))
                        m.then_inc(sem("o_turned"), 1)
            pe.sem_inc(sem("br_proj"), 4)
            pe.wait_ge(sem("o_merged"), 5 + 16)
            with pe.Fori(0, 8) as i:
                for s in range(4):
                    weights_in(s, i + 24)
                    pe.wait_ge(sem("br_used"), 1 + i * 4 + s)
                    wide(s, s, (zsT, yhT)[s % 2]).then_inc(sem("br_proj"), 1)
            pe.sem_inc(sem("wo_used"), 2)
            pe.wait_ge(sem("merged"), 16)
            with pe.Fori(0, 4) as i:
                for s in range(2):
                    pe.wait_ge(sem(f"wo_in{s}"), i * 16 + 16)
                    if s == 0:
                        pe.wait_ge(sem("mix_added"), 1 + 2 * i)
                    for t in range(2):
                        for k in range(8):
                            m = mm(bank[4 + t][:, :], gT[:, s * 8 + k, t * P:(t + 1) * P], wo_ring[:, s, k, :],
                                   start=(s == 0 and k == 0), stop=(s == 1 and k == 7))
                    m.then_inc(sem("wo_used"), 1)
            pe.sem_inc(sem("q_proj"), 4)
            for t in range(2):
                pe.wait_ge(sem("h2_done"), t + 1)
                for kq in range(4):
                    b = 4 * t + kq
                    for j in range(4):
                        k = 4 * kq + j
                        m = nc.tensor.transpose(bank[b][:, j * P:(j + 1) * P], h2[:, t, k * P:(k + 1) * P], const("ident"))
                    m.then_inc(sem("h2_turned"), 1)
            pe.wait_ge(sem("h2T_done"), 8)
            pe.wait_ge(sem("subk_in"), 16)
            with pe.Fori(0, 4) as i:
                for s in range(4):
                    weights_in(s, i + 32)
                    wide(s, s, h2T).then_inc(sem("q_proj"), 1)
                for s in range(4):
                    pe.wait_ge(sem("q_copied"), i * 4 + s + 1)
                    pe.wait_ge(sem("sc_copied"), 1 + i * 4)
                    for t in range(2):
                        m = mm(bank[4 + s][:, t * P:(t + 1) * P], q_sb[:, s, t * P:(t + 1) * P], subk[:, bass.ds(i * 4 + s, 1), :].rearrange("p o n -> p (o n)"), start=True, stop=True)
                    m.then_inc(sem("sc_ready"), 1)

        @block.scalar
        def _(act):
            af = nc.scalar.activation
            for name in ("rooted", "k_copied", "sc_copied"):
                act.sem_inc(sem(name), 1)
            act.wait_ge(sem("cond_in"), 16)
            af(cond, cond, ACT.Silu).then_inc(sem("cond_done"), 1)
            act.wait_ge(sem("gating_step"), 1)
            for d in range(2):
                v = ab.rearrange("p t (d k h) -> p t d k h", d=2, k=2)
                m = af(beta[:, :, d * H:(d + 1) * H], v[:, :, d, 1, :], ACT.Sigmoid)
            m.then_inc(sem("beta_done"), 1)
            act.wait_ge(sem("gating_step"), 3)
            af(sp_e, xs, ACT.Abs).then_inc(sem("sp_act"), 1)
            act.wait_ge(sem("sp_act"), 1)
            af(sp_e, sp_e, ACT.Exp, scale=-1.0).then_inc(sem("sp_act"), 1)
            act.wait_ge(sem("sp_act"), 2)
            af(sp_e, sp_e, ACT.Ln, bias=1.0).then_inc(sem("sp_act"), 1)
            act.wait_ge(sem("gate_in"), 32)
            af(gate_row[:, 0, :], gate_row[:, 0, :], ACT.Exp).then_inc(sem("alog_done"), 1)
            act.wait_ge(sem("gating_step"), 10)
            af(etail, etail, ACT.Exp)
            af(eg, gcum, ACT.Exp)
            af(etot, etot, ACT.Exp).then_inc(sem("eg_done"), 1)
            for t in range(4):
                lat = t < 2
                act.wait_ge(sem("xmask_done"), t + 1)
                af(n_e1f[:, t], xm[:, 0:H, :], ACT.Exp, scale=-1.0)
                if lat:
                    af(a_e2f[:, t], xm2, ACT.Exp)
                    af(a_eb[:, t], xm[:, H:HD, :], ACT.Exp)
                af(n_eb[:, t], xm[:, H:HD, :], ACT.Exp).then_inc(sem("exp_done"), 1)

            def evac(h, t):
                act.wait_ge(sem("proj"), 3 + 3 * h + t + 1)
                act.wait_ge(sem("tap"), 25 * h)
                m = af(c_lat[t][:, :, 2:2 + CH], bank[t][:, 0:SEQ].rearrange("p (r w) -> p r w", r=NCH), ACT.Copy)
                if t:
                    m = af(c_ctx[t][:, 2:2 + SEQ], bank[t][:, SEQ:TOK], ACT.Copy)
                m.then_inc(sem("proj_copied"), 1)

            def silu(h, t):
                act.wait_ge(sem("tap"), 25 * h + (5, 15, 25)[t])
                ns = 1 if t == 0 else 2
                src = acc[:, t, 0:ns * SEQ].rearrange("p (s c n) -> p s c n", s=ns, c=NCH)
                dst = raw[:, t, 0:ns * SEQ].rearrange("p (s c n) -> p s c n", s=ns, c=NCH)
                af(dst[:, :, 0:2, :], src[:, :, 0::3, :], ACT.Silu)
                af(dst[:, :, 2:4, :], src[:, :, 1:3, :], ACT.Silu).then_inc(sem("silued"), 1)
                if t < 2:
                    act.wait_ge(sem("silued"), 3 * h + t + 1)
                    af(sq[:, t, 0:ns * SEQ], raw[:, t, 0:ns * SEQ], ACT.Square).then_inc(sem("squared"), 1)

            def roots(h):
                for j, n in ((0, SEQ), (1, TOK)):
                    act.wait_ge(sem("ssq"), 2 * h + j + 1)
                    act.wait_ge(sem("normed"), 1 + 2 * h)
                    af(nrm[:, j, 0:n], (bank[3] if j == 0 else bank[7])[:, 0:n], ACT.Sqrt, bias=eps6[:, 0:1]
                       ).then_inc(sem("rooted"), 1)

            def copy_k(h):
                act.wait_ge(sem("k_turned"), h + 1)
                act.wait_ge(sem("stored"), h + 1)
                af(r_k, bank[4][:, :], ACT.Copy).then_inc(sem("k_copied"), 1)

            act.sem_inc(sem("proj_copied"), 2)
            act.wait_ge(sem("decay_done"), 1)
            for t in range(3):
                evac(0, t)
                silu(0, t)
            with act.Fori(1, H) as h:
                evac(h, 0)
                roots(h - 1)
                act.wait_ge(sem("normed"), 1 + 2 * h)
                silu(h, 0)
                evac(h, 1)
                silu(h, 1)
                evac(h, 2)
                copy_k(h - 1)
                act.wait_ge(sem("v_turned"), h)
                silu(h, 2)
            roots(H - 1)
            copy_k(H - 1)
            act.sem_inc(sem("zg_evac"), 4)
            act.wait_ge(sem("gram_used"), 1 + 4 * H)

            def zg(i, s, func, dst):
                act.wait_ge(sem("zg_proj"), 4 + i * 4 + s + 1)
                af(dst, bank[s][:, 0:SEQ].unsqueeze(1), func).then_inc(sem("zg_evac"), 1)

            with act.Fori(0, 4) as i:
                for s in range(4):
                    zg(i, s, ACT.Silu, zsT[:, bass.ds(i * 4 + s, 1), :])
            with act.Fori(4, 12) as i:
                for s in range(4):
                    zg(i, s, ACT.Sigmoid, gT[:, bass.ds(i * 4 + (s - 16), 1), :])
            act.sem_inc(sem("hy_evac"), 4)
            act.sem_inc(sem("hy_tcopied"), 4)
            act.wait_ge(sem("hpads"), 1)
            act.wait_ge(sem("inv_out"), 32)

            def hy_evac(i, s):
                act.wait_ge(sem("hy_proj"), 4 + i * 4 + s + 1)
                act.wait_ge(sem("hy_tap"), 1 + 3 * (i * 4 + s))
                af(hbuf[:, s, :, 1:1 + CH], bank[s][:, 0:SEQ].rearrange("p (r w) -> p r w", r=NCH), ACT.Copy
                   ).then_inc(sem("hy_evac"), 1)

            def hy_tcopy(i, s):
                act.wait_ge(sem("hy_turned"), 4 + i * 4 + s + 1)
                af(uv[:, :, bass.ds((i * 4 + s) * P, P)], bank[4 + s][:, 0:2 * P].rearrange("p (t n) -> p t n", t=2), ACT.Copy
                   ).then_inc(sem("hy_tcopied"), 1)

            with act.Fori(0, 8) as i:
                hy_evac(i, 0)
                hy_evac(i, 1)
                hy_tcopy(i, 0)
                hy_evac(i, 2)
                hy_tcopy(i, 1)
                hy_evac(i, 3)
                hy_tcopy(i, 2)
                hy_tcopy(i, 3)
            with act.Fori(8, 12) as i:
                for s in range(4):
                    hy_evac(i, s)
            for n, hid in enumerate((hid1, hid2)):
                act.wait_ge(sem("ang_done"), 6 * n + 6)
                af(hid[0:CH, :], ang[0:CH, :], ACT.Sin).then_inc(sem("hid_done"), 1)
            with act.Fori(0, 4) as n:
                for o in range(2):
                    for f in range(2):
                        act.wait_ge(sem("spec_ready"), n * 4 + (2 * o + f + 1))
                        act.wait_ge(sem("prod_done"), n * 24 + (1 + 12 * o))
                        af(Fr[:, f, :], bank[4 + f][:, :], ACT.Copy).then_inc(sem("spec_copied"), 1)
                        af(Fi[:, f, :], bank[6 + f][:, :], ACT.Copy).then_inc(sem("spec_copied"), 1)
            with act.Fori(0, 2) as i:
                for r in range(2):
                    grp = i * 2 + r
                    for g in range(8):
                        q, s = g // 4, g % 4
                        T = 2 * (1 - q) + (0, 1, 1, 0)[s]
                        for u in range(4):
                            h = i * 8 + (4 * r + u)
                            B = bank[2 * u + 1][:, 0:P]
                            act.wait_ge(sem("vn_ready"), grp * 32 + (g * 4 + u + 1))
                            if g < 7:
                                af(v_tail[:, u, :], B, ACT.Copy, scale=mixed[:, 4 + s // 2, T, bass.ds(h, 1)]
                                   ).then_inc(sem("vtail_done"), 1)
                            if q:
                                af(v_new[:, u, :], B, ACT.Copy).then_inc(sem("vn_done"), 1)
                    for u in range(4):
                        act.wait_ge(sem("o_added"), grp * 32 + (24 + 4 + u + 1))
                        for t in range(2):
                            af(o_sq, o_acc[:, 2 * u + t, :], ACT.Square, accum_out=o_ss[:, 2 * u + t:2 * u + t + 1]
                               ).then_inc(sem("o_ss"), 1)
                            act.wait_ge(sem("o_ss"), grp * 9 + (2 * u + t + 1))
                    af(o_ss, o_ss, ACT.Sqrt, bias=eps6[:, 0:1], scale=1.0 / DK).then_inc(sem("o_ss"), 1)
            for t in range(2):
                act.wait_ge(sem("var_done"), t + 1)
                af(rstd[:, t:t + 1], aggr[:, t, 1:2], ACT.Sqrt, bias=eps5[:, 0:1]).then_inc(sem("std_done"), 1)
            for t in range(2):
                for kq in range(4):
                    act.wait_ge(sem("h2_turned"), 4 * t + kq + 1)
                    if t + kq == 0:
                        act.wait_ge(sem("wo_used"), 2 + 8)
                    af(h2T[:, 4 * kq:4 * kq + 4, t * P:(t + 1) * P], bank[4 * t + kq][:, :].rearrange("p (k n) -> p k n", k=4), ACT.Copy
                       ).then_inc(sem("h2T_done"), 1)
            with act.Fori(0, 4) as i:
                for s in range(4):
                    act.wait_ge(sem("q_proj"), 4 + i * 4 + s + 1)
                    af(q_sb[:, s, :], bank[s][:, 0:SEQ], ACT.Copy).then_inc(sem("q_copied"), 1)
                for s in range(4):
                    act.wait_ge(sem("sc_ready"), i * 4 + s + 1)
                    af(sc[:, :, bass.ds(i * 4 + s, 1), :], bank[4 + s][:, 0:2 * P].rearrange("p (t o n) -> p t o n", t=2, o=1), ACT.Copy
                       ).then_inc(sem("sc_copied"), 1)
            act.wait_ge(sem("bdiff"), 2)
            af(gate.rearrange("p t n -> p (t n)"), gate.rearrange("p t n -> p (t n)"), ACT.Exp).then_inc(sem("bexp"), 1)
            def gelus(t, b, n):
                act.wait_ge(sem("ring_used"), n + (7 + t * 256))
                act.wait_ge(sem("coef_done"), b + t * PH)
                af(gelu, dots, ACT.Gelu).then_inc(sem("gelu_done"), 1)

            for t in range(2):
                gelus(t, 0, 16 if t == 0 else 0)
                with act.Fori(1, PH) as b:
                    gelus(t, b, b * 32)
            for t in range(2):
                act.wait_ge(sem("var_done"), t + 3)
                af(rstd[:, t:t + 1], aggr[:, t, 1:2], ACT.Sqrt, bias=eps5[:, 0:1]).then_inc(sem("std_done"), 1)

        @block.vector
        def _(dve):
            v = nc.vector
            tt, stt, ts = v.tensor_tensor, v.scalar_tensor_tensor, v.tensor_scalar
            for name in ("v_copied", "gram_used", "fil_used", "normed", "inv_used", "prod_done", "mix_added", "row_done"):
                dve.sem_inc(sem(name), 1)
            v.memset(eps6, 1e-6)
            v.memset(eps5, 1e-5).then_inc(sem("row_done"), 1)
            dve.wait_ge(sem("bada_in"), 16)
            with dve.Fori(0, 4) as i:
                for j in range(2):
                    dve.wait_ge(sem("ada_used"), 4 + i * 4 + 2 * j + 2)
                    r = ada_row[0:2, bass.ds((i * 2 + j) * N1, N1)]
                    tt(r, bank[j][0:2, :], r, ALU.add).then_inc(sem("row_done"), 1)
            dve.wait_ge(sem("cols_ready"), 1)
            cv = bank[2][:, 0:64].rearrange("p (t s) -> p t s", s=2)
            v.tensor_copy(cols[:, 0:KT, :], cv[:, 0:KT, :])
            ts(cols[:, KT:2 * KT, :], cv[:, KT:2 * KT, :], 1.0, None, ALU.add).then_inc(sem("cols_done"), 1)
            dve.wait_ge(sem("cols_done"), 1)
            dve.wait_ge(sem("x_in"), 16)
            for k in range(KT):
                for s in range(2):
                    x = hT[:, k, s * SEQ:(s + 1) * SEQ]
                    ts(x, x, cols[:, KT + k, s:s + 1], cols[:, k, s:s + 1], ALU.mult, ALU.add
                       ).then_inc(sem("h_done"), 1)
            dve.wait_ge(sem("gating_mm"), 1)
            v.tensor_copy(ab, bank[0][:, 0:256].rearrange("p (t n) -> p t n", t=4)).then_inc(sem("gating_step"), 1)
            dve.wait_ge(sem("gating_step"), 1)
            dve.wait_ge(sem("gate_in"), 32)
            abv = ab.rearrange("p t (d k h) -> p t d k h", d=2, k=2)
            for d in range(2):
                tt(xs[:, :, d * H:(d + 1) * H], abv[:, :, d, 0, :],
                   gate_row[:, 1, d * H:(d + 1) * H].unsqueeze(1).broadcast_to([P, 4, H]), ALU.add
                   ).then_inc(sem("gating_step"), 1)
            dve.wait_ge(sem("gating_step"), 3)
            ts(sp_m, xs, 0.0, None, ALU.max).then_inc(sem("gating_step"), 1)
            dve.wait_ge(sem("gating_step"), 4)
            dve.wait_ge(sem("sp_act"), 3)
            tt(sp_m, sp_m, sp_e, ALU.add).then_inc(sem("gating_step"), 1)
            dve.wait_ge(sem("gating_step"), 5)
            dve.wait_ge(sem("alog_done"), 1)
            stt(g_tok, sp_m, -1.0, gate_row[:, 0, :].unsqueeze(1).broadcast_to([P, 4, HD]), ALU.mult, ALU.mult
                ).then_inc(sem("gating_step"), 1)
            dve.wait_ge(sem("gating_mm"), 2)
            v.tensor_copy(xm.rearrange("p h i -> p (h i)")[0:HD, 0:512], bank[4][0:HD, :]).then_inc(sem("gating_step"), 1)
            dve.wait_ge(sem("gating_mm"), 3)
            v.tensor_copy(gcum, bank[1][:, 0:128].rearrange("p (t h) -> p t h", t=4)).then_inc(sem("gating_step"), 1)
            dve.wait_ge(sem("gating_mm"), 4)
            dve.wait_ge(sem("gating_step"), 8)
            tt(etail, bank[2][:, 0:128].rearrange("p (t h) -> p t h", t=4), gcum, ALU.subtract).then_inc(sem("gating_step"), 1)
            v.tensor_copy(etot, bank[2][:, 128:384].rearrange("p (u n) -> p u n", u=2)).then_inc(sem("gating_step"), 1)
            dve.wait_ge(sem("eg_done"), 1)
            ts(neg_eg, eg, -1.0, None, ALU.mult)
            dve.wait_ge(sem("gating_step"), 6)
            dve.wait_ge(sem("beta_out"), 32)
            for t in range(4):
                if t:
                    dve.wait_ge(sem("gb_ready"), t)
                for d, tri in ((0, "tri_f"), (1, "tri_b")):
                    m = tt(gx[:, d * H:(d + 1) * H, :],
                           g_tok[:, t, d * H:(d + 1) * H].unsqueeze(2).broadcast_to([P, H, CH]),
                           const(tri).unsqueeze(1).broadcast_to([P, H, CH]), ALU.mult)
                m.then_inc(sem("gx_done"), 1)
                dve.wait_ge(sem("gb_ready"), t + 1)
                if t:
                    dve.wait_ge(sem("exp_done"), t)
                for b in range(4):
                    m = tt(xm[:, 8 * b:8 * b + 8, :], bank[4 + b][:, :].rearrange("p (h i) -> p h i", h=8),
                           gcum[:, t, 8 * b:8 * b + 8].unsqueeze(2).broadcast_to([P, 8, CH]), ALU.subtract)
                    m.then_inc(sem("xm_done"), 1)
                dve.wait_ge(sem("xm_done"), 4 * t + 4)
                up = const("mask_above").unsqueeze(1).broadcast_to([P, H, CH])
                dn = const("mask_below").unsqueeze(1).broadcast_to([P, H, CH])
                if t < 2:
                    tt(xm2, xm[:, 0:H, :], dn, ALU.subtract).then_inc(sem("xm2_done"), 1)
                    dve.wait_ge(sem("xm2_done"), t + 1)
                tt(xm[:, 0:H, :], xm[:, 0:H, :], up, ALU.add)
                tt(xm[:, H:HD, :], xm[:, H:HD, :], up, ALU.subtract).then_inc(sem("xmask_done"), 1)
                dve.wait_ge(sem("exp_done"), t + 1)
                for d, e in ((0, n_e1f), (1, n_eb)):
                    m = stt(e[:, t], e[:, t], -1.0,
                            beta[:, t, d * H:(d + 1) * H].unsqueeze(2).broadcast_to([P, H, CH]), ALU.mult, ALU.mult)
                m.then_inc(sem("nbeta_done"), 1)
            dve.wait_ge(sem("nbeta_done"), 4)
            v.memset(cbuf, 0.0).then_inc(sem("decay_done"), 1)

            def conv(h, t):
                base = 25 * h + (0, 5, 15)[t]
                w = lambda j: dnc[:, bass.ds(3 * h + t, 1), j]
                a_lat = acc[:, t, 0:SEQ].rearrange("p (r w) -> p r w", r=NCH)
                a_ctx = acc[:, t, SEQ:TOK]
                dve.wait_ge(sem("proj_copied"), 2 + 3 * h + t + 1)
                dve.wait_ge(sem("silued"), 3 * h)
                per = 1 if t == 0 else 2
                for j in range(TAPS):
                    if j:
                        dve.wait_ge(sem("tap"), base + per * (j - 1) + 1)
                    x = c_lat[t][:, :, j:j + CH]
                    if j == 0:
                        ts(a_lat, x, w(j), None, ALU.mult).then_inc(sem("tap"), 1)
                    else:
                        stt(a_lat, x, w(j), a_lat, ALU.mult, ALU.add).then_inc(sem("tap"), 1)
                    if t:
                        if j:
                            dve.wait_ge(sem("tap"), base + per * j)
                        x = c_ctx[t][:, j:j + SEQ]
                        if j == 0:
                            ts(a_ctx, x, w(j), None, ALU.mult).then_inc(sem("tap"), 1)
                        else:
                            stt(a_ctx, x, w(j), a_ctx, ALU.mult, ALU.add).then_inc(sem("tap"), 1)

            def normalize(h):
                for j, n in ((0, SEQ), (1, TOK)):
                    dve.wait_ge(sem("rooted"), 1 + 2 * h + j + 1)
                    v.reciprocal(nrm[:, j, 0:n], nrm[:, j, 0:n]).then_inc(sem("recip"), 1)
                dve.wait_ge(sem("stored"), h + 1)
                dve.wait_ge(sem("recip"), 2 * h + 1)
                stt(r_qT, raw[:, 0, 0:SEQ], DK ** -0.5, nrm[:, 0, 0:SEQ], ALU.mult, ALU.mult).then_inc(sem("normed"), 1)
                dve.wait_ge(sem("recip"), 2 * h + 2)
                tt(r_kT, raw[:, 1, :], nrm[:, 1, :], ALU.mult).then_inc(sem("normed"), 1)

            def finish(h):
                dve.wait_ge(sem("v_turned"), h + 1)
                v.tensor_copy(r_v, bank[5][:, :]).then_inc(sem("v_copied"), 1)
                dve.wait_ge(sem("gram"), h + 1)
                dve.wait_ge(sem("stored"), h + 1)
                g = bank[6][:, 0:256].rearrange("p (t o i) -> p t o i", t=4, o=1)
                q = bank[6][:, 256:384].rearrange("p (t o i) -> p t o i", t=2, o=1)
                for d, e in ((0, n_e1f), (1, n_eb)):
                    tt(mt[:, d].unsqueeze(2), g, e[:, :, bass.ds(h, 1), :], ALU.mult).then_inc(sem("gram_used"), 1)
                for d, e in ((0, a_e2f), (1, a_eb)):
                    tt(r_at[:, d].unsqueeze(2), q, e[:, :, bass.ds(h, 1), :], ALU.mult).then_inc(sem("gram_used"), 1)

            dve.wait_ge(sem("dnc_in"), 16)
            for t in range(3):
                conv(0, t)
            with dve.Fori(1, H) as h:
                conv(h, 0)
                normalize(h - 1)
                conv(h, 1)
                conv(h, 2)
                finish(h - 1)
            normalize(H - 1)
            finish(H - 1)
            for m_, x in enumerate((neg_eg, eg, etail)):
                for w_ in range(2):
                    for half in range(2):
                        d = half ^ w_
                        k_ = v.tensor_copy(mixed[HF[half], 2 * m_ + w_], x[HF[half], :, d * H:(d + 1) * H])
            k_.then_inc(sem("mixed_done"), 1)
            with dve.Fori(0, 2) as n:
                dve.wait_ge(sem("mix_in"), 32 * n + 32)
                for j in range(1, CH - 1):
                    rows = CH - 1 - j
                    tmp = sol_t[:, 0:rows * j].rearrange("p (i c) -> p i c", c=j)
                    if j > 1:
                        dve.wait_ge(sem("solve_step"), n * 124 + 2 * (j - 1))
                    tt(tmp, sol[:, j + 1:CH, j:j + 1].broadcast_to([P, rows, j]), sol[:, j:j + 1, 0:j].broadcast_to([P, rows, j]),
                       ALU.mult).then_inc(sem("solve_step"), 1)
                    dve.wait_ge(sem("solve_step"), n * 124 + 2 * (j - 1) + 1)
                    tt(sol[:, j + 1:CH, 0:j], sol[:, j + 1:CH, 0:j], tmp, ALU.add).then_inc(sem("solve_step"), 1)
                dve.wait_ge(sem("solve_step"), n * 124 + 124)
                v.memset(sol.rearrange("p a b -> p (a b)")[:, 0:CH * CH:CH + 1], 1.0).then_inc(sem("sol_diag"), 1)
                dve.wait_ge(sem("sol_diag"), n + 1)
                dve.wait_ge(sem("inv_stored"), n + 1)
                lo, hi = HF
                tt(sol_o[lo], sol[lo].rearrange("p r c -> p c r"), sol_b[lo].unsqueeze(2).broadcast_to([CH, CH, CH]), ALU.mult)
                tt(sol_o[hi], sol[hi], sol_b[hi].unsqueeze(1).broadcast_to([CH, CH, CH]), ALU.mult).then_inc(sem("solved"), 1)
            v.memset(hbuf, 0.0).then_inc(sem("hpads"), 1)
            dve.sem_inc(sem("hy_tap"), 10)
            dve.wait_ge(sem("hyc_in"), 32)

            def hconv(i, s, turned):
                m = i * 4 + s
                w = lambda j: hyc[:, bass.ds(m, 1), j]
                dve.wait_ge(sem("hy_evac"), 4 + m + 1)
                if turned:
                    dve.wait_ge(sem("hy_turned"), 1 + m)
                    o_ = hacc[:, s, :].rearrange("p (r w) -> p r w", r=NCH)
                else:
                    o_ = yhT[:, bass.ds(m - 32, 1), :].rearrange("p o (r w) -> p (o r) w", r=NCH)
                for j in range(HTAPS):
                    if j:
                        dve.wait_ge(sem("hy_tap"), 10 + 3 * m + j)
                    x = hbuf[:, s, :, j:j + CH]
                    if j == 0:
                        ts(o_, x, w(j), None, ALU.mult).then_inc(sem("hy_tap"), 1)
                    else:
                        stt(o_, x, w(j), o_, ALU.mult, ALU.add).then_inc(sem("hy_tap"), 1)

            with dve.Fori(0, 8) as i:
                for s in range(4):
                    hconv(i, s, True)
            with dve.Fori(8, 12) as i:
                for s in range(4):
                    hconv(i, s, False)
            MAGIC, TWO_PI = 12582912.0, 6.283185307179586
            T_HI = float(np.float32(6.28125))
            T_MID = float(np.float32(TWO_PI - T_HI))
            T_LO = TWO_PI - T_HI - T_MID
            dve.wait_ge(sem("hyf_in"), 64)
            for n, b in enumerate((0, 1)):
                dve.wait_ge(sem("hid_mm"), n + 1)
                A_, W_ = ang[0:CH, :], turns[0:CH, :]
                steps = 0

                def chain(ins):
                    nonlocal steps
                    steps += 1
                    ins.then_inc(sem("ang_done"), 1)
                    dve.wait_ge(sem("ang_done"), 6 * n + steps)

                chain(ts(A_, bank[b][0:CH, 0:SEQ], fcol[0:CH, n:n + 1], fcol[0:CH, 2:3], ALU.add, ALU.mult))
                chain(ts(W_, A_, 1.0 / TWO_PI, MAGIC, ALU.mult, ALU.add))
                chain(ts(W_, W_, -MAGIC, None, ALU.add))
                chain(stt(A_, W_, -T_HI, A_, ALU.mult, ALU.add))
                chain(stt(A_, W_, -T_MID, A_, ALU.mult, ALU.add))
                stt(A_, W_, -T_LO, A_, ALU.mult, ALU.add).then_inc(sem("ang_clip"), 1)
                dve.wait_ge(sem("ang_clip"), n + 1)
                ts(A_, A_, -3.1415925, 3.1415925, ALU.max, ALU.min).then_inc(sem("ang_done"), 1)
            v.memset(hid2[CH:CH + 1, :], 1.0).then_inc(sem("hid_done"), 1)

            def fold(n, o):
                c = n * 2 + o
                dve.wait_ge(sem("fil_ready"), c + 1)
                dve.wait_ge(sem("w3_in"), 48 * n + 48)
                for t in range(2):
                    tt(t1[:, t, :], bank[4 + t][:, :], win[:, t, :], ALU.mult).then_inc(sem("fstep"), 1)
                    if t == 0:
                        stt(t2[:, t, :], bank[6 + t][:, :], const("not_first"), win[:, t, :], ALU.mult, ALU.mult).then_inc(sem("fstep"), 1)
                    else:
                        tt(t2[:, t, :], bank[6 + t][:, :], win[:, t, :], ALU.mult).then_inc(sem("fstep"), 1)
                for t in range(2):
                    dve.wait_ge(sem("fstep"), c * 6 + (2 * t + 2))
                    tt(fa[:, t, :], t1[:, t, :], t2[:, t, :], ALU.add).then_inc(sem("fstep"), 1)
                    if t == 0:
                        dve.wait_ge(sem("fstep"), c * 6 + 5)
                        tt(fa[0:1, 0, :], fa[0:1, 0, :], skipc[0:1, o, :], ALU.add)
                    m = tt(fb[:, t, :], t1[:, t, :], t2[:, t, :], ALU.subtract)
                m.then_inc(sem("fil_used"), 1)

            def products(n, o, last):
                c = n * 2 + o
                for f in range(2):
                    dve.wait_ge(sem("sig_ready"), c * 2 + (f + 1))
                    dve.wait_ge(sem("spec_copied"), c * 4 + (2 * f + 2))
                    dve.wait_ge(sem("fil_used"), c + 2)
                    ur, ui = bank[f][:, :], bank[2 + f][:, :]
                    done = lambda k: c * 12 + (6 * f + 1 + k)
                    tt(t1[:, f, :], ur, Fr[:, f, :], ALU.mult).then_inc(sem("prod_done"), 1)
                    tt(t2[:, f, :], ui, Fi[:, f, :], ALU.mult).then_inc(sem("prod_done"), 1)
                    dve.wait_ge(sem("prod_done"), done(2))
                    tt(Yr[:, f, :], t1[:, f, :], t2[:, f, :], ALU.subtract).then_inc(sem("prod_done"), 1)
                    dve.wait_ge(sem("prod_done"), done(3))
                    tt(t1[:, f, :], ur, Fi[:, f, :], ALU.mult).then_inc(sem("prod_done"), 1)
                    tt(t2[:, f, :], ui, Fr[:, f, :], ALU.mult).then_inc(sem("prod_done"), 1)
                    dve.wait_ge(sem("prod_done"), done(5))
                    tt(Yi[:, f, :], t1[:, f, :], t2[:, f, :], ALU.add).then_inc(sem("prod_done"), 1)
                if not last:
                    dve.wait_ge(sem("prod_done"), c * 12 + 13)
                    fold(n + o, 1 - o)
                if o == 0:
                    for t in range(2):
                        dve.wait_ge(sem("inv_ready"), n * 6 + (t + 1))
                        tt(yb[:, t, :], bank[t][:, :], uv[:, t, bass.ds(n * N1 + D, N1)], ALU.mult).then_inc(sem("inv_used"), 1)
                else:
                    for b in range(4):
                        dve.wait_ge(sem("inv_ready"), n * 6 + (2 + b + 1))
                        x = yhT[:, bass.ds(n * 4 + b, 1), :]
                        tt(x, bank[b][:, 0:SEQ].unsqueeze(1), x, ALU.mult).then_inc(sem("inv_used"), 1)

            fold(0, 0)
            with dve.Fori(0, 3) as n:
                products(n, 0, False)
                products(n, 1, False)
            products(3, 0, False)
            products(3, 1, True)
            v.tensor_copy(condb, cond[:, :, 0:1].broadcast_to([P, KT, P])).then_inc(sem("condb_done"), 1)
            v.memset(o_ss, 0.0).then_inc(sem("hyena_done"), 1)
            dve.sem_inc(sem("mods_done"), 2)
            dve.wait_ge(sem("mods_in"), 16)
            mflat = mods.rearrange("p s n -> p (s n)")
            with dve.Fori(0, 8) as i:
                for j in range(2):
                    dve.wait_ge(sem("ada2_used"), 4 + i * 4 + 2 * j + 2)
                    x = mflat[:, bass.ds((i * 2 + j) * N1, N1)]
                    tt(x, bank[j][:, :], x, ALU.add).then_inc(sem("mods_done"), 1)
            dve.sem_inc(sem("o_merged"), 5)
            dve.wait_ge(sem("mods_done"), 2 + 16)
            dve.wait_ge(sem("mixed_done"), 1)
            with dve.Fori(0, 2) as i:
                for r in range(2):
                    grp = i * 2 + r
                    v.memset(state, 0.0).then_inc(sem("state_zero"), 1)
                    dve.wait_ge(sem(f"rec_in{r}"), 320 * i + 320)
                    for g in range(8):
                        q, s = g // 4, g % 4
                        t = (0, 1, 1, 0)[s]
                        T = 2 * (1 - q) + t
                        hf = ((0, 1), (1, 0))[s // 2]
                        for u in range(4):
                            h = i * 8 + (4 * r + u)
                            A = bank[2 * u]
                            fac = lambda kind: mixed[:, 2 * kind + s // 2, T, bass.ds(h, 1)]
                            v_tok = recs[:, 4 * r + u, 1280 + T * P:1280 + (T + 1) * P]
                            dve.wait_ge(sem("ks_ready"), grp * 32 + (g * 4 + u + 1))
                            stt(r_in[:, u, :], A[:, 0:P], fac(0), v_tok, ALU.mult, ALU.add).then_inc(sem("r_done"), 1)
                            if q:
                                oa = o_acc[:, 2 * u + t, :]
                                if s < 2:
                                    ts(oa, A[:, P:2 * P], fac(1), None, ALU.mult).then_inc(sem("o_added"), 1)
                                else:
                                    dve.wait_ge(sem("o_added"), grp * 32 + ((3 - s) * 8 + 4 + u + 1))
                                    stt(oa, A[:, P:2 * P], fac(1), oa, ALU.mult, ALU.add).then_inc(sem("o_added"), 1)
                        for u in range(4):
                            h = i * 8 + (4 * r + u)
                            if g < 7:
                                dve.wait_ge(sem("upd_ready"), grp * 28 + (g * 4 + u + 1))
                                for d in range(2):
                                    st = state[:, 2 * u + d, :]
                                    tot = etot[:, hf[d], bass.ds(h + (T * HD + d * H), 1)]
                                    stt(st, st, tot, bank[2 * u + d][:, (2 + d) * P:(3 + d) * P], ALU.mult, ALU.add).then_inc(sem("state_done"), 1)
                        if q:
                            for u in range(4):
                                oa = o_acc[:, 2 * u + t, :]
                                dve.wait_ge(sem("av_ready"), grp * 16 + ((g - 4) * 4 + u + 1))
                                if g == 7:
                                    dve.wait_ge(sem("o_added"), grp * 32 + (24 + u + 1))
                                tt(oa, bank[2 * u + 1][:, P:2 * P], oa, ALU.add).then_inc(sem("o_added"), 1)
                    dve.wait_ge(sem("o_ss"), grp * 9 + 9)
                    v.reciprocal(o_ss, o_ss).then_inc(sem("o_rstd"), 1)
                    dve.wait_ge(sem("o_rstd"), grp + 1)
                    for u in range(4):
                        for t in range(2):
                            oa = o_acc[:, 2 * u + t, :]
                            ts(oa, oa, o_ss[:, 2 * u + t:2 * u + t + 1], None, ALU.mult).then_inc(sem("o_normed"), 1)
                    for u in range(4):
                        h = i * 8 + (4 * r + u)
                        dve.wait_ge(sem("o_turned"), 1 + grp * 4 + (u + 1))
                        z_ = zsT[:, bass.ds(h, 1), :].rearrange("p o (c n) -> p (o c) n", c=NCH)
                        for t, zz in ((0, z_[:, 0::3, :]), (1, z_[:, 1:3, :])):
                            m = stt(zz, bank[2 * u + 1][:, (2 + t) * P:(3 + t) * P].rearrange("p (c n) -> p c n", c=2), dn_nw[:, 0:1], zz,
                                    ALU.mult, ALU.mult)
                        m.then_inc(sem("o_merged"), 1)
            dve.sem_inc(sem("br_used"), 4)
            with dve.Fori(0, 8) as i:
                for j in range(2):
                    ct = i * 2 + j
                    g1_, g2_ = gT[:, bass.ds(ct, 1), :], gT[:, bass.ds(ct + 16, 1), :]
                    dve.wait_ge(sem("br_proj"), 4 + i * 4 + 2 * j + 1)
                    tt(g1_, bank[2 * j][:, 0:SEQ].unsqueeze(1), g1_, ALU.mult).then_inc(sem("br_used"), 1)
                    dve.wait_ge(sem("br_proj"), 4 + i * 4 + 2 * j + 2)
                    tmp = tmp_g[:, j:j + 1, :]
                    tt(tmp, bank[2 * j + 1][:, 0:SEQ].unsqueeze(1), g2_, ALU.mult).then_inc(sem("br_used"), 1)
                    dve.wait_ge(sem("br_used"), 4 + i * 4 + 2 * j + 2)
                    tt(g1_, g1_, tmp, ALU.add).then_inc(sem("merged"), 1)
            dve.wait_ge(sem("xres_in"), 16)
            with dve.Fori(0, 4) as i:
                dve.wait_ge(sem("wo_used"), 2 + 2 * i + 2)
                for t in range(2):
                    tt(tmp_m[:, t:t + 1, :], bank[4 + t][:, :].unsqueeze(1), mods[:, 0:1, bass.ds(i * N1, N1)], ALU.mult
                       ).then_inc(sem("mix_scaled"), 1)
                for t in range(2):
                    dve.wait_ge(sem("mix_scaled"), 2 * i + t + 1)
                    x = xn[:, t:t + 1, bass.ds(i * N1, N1)]
                    stt(x, x, ALPHA, tmp_m[:, t:t + 1, :], ALU.mult, ALU.add).then_inc(sem("mix_added"), 1)

            def layer_norm(first, t, x):
                c = [0]
                per = 5
                base = (first * 2 + t) * per

                def chain(ins):
                    c[0] += 1
                    ins.then_inc(sem("ln_step"), 1)
                    dve.wait_ge(sem("ln_step"), base + c[0])

                for k in range(4):
                    m = v.bn_stats(stats[:, t, 6 * k:6 * k + 6], x[:, k * N1:(k + 1) * N1])
                chain(m)
                v.bn_aggr(aggr[:, t, :], stats[:, t, :]).then_inc(sem("var_done"), 1)
                dve.wait_ge(sem("std_done"), 2 * first + t + 1)
                chain(v.reciprocal(rstd[:, t:t + 1], rstd[:, t:t + 1]))
                chain(ts(x, x, aggr[:, t, 0:1], rstd[:, t:t + 1], ALU.subtract, ALU.mult))
                chain(tt(x, x, lnp[:, 0, :], ALU.mult))
                chain(tt(x, x, lnp[:, 1, :], ALU.add))

            dve.wait_ge(sem("ln1_in"), 32)
            dve.wait_ge(sem("mix_added"), 9)
            for t in range(2):
                layer_norm(0, t, xn[:, t, :])
                stt(h2[:, t, :], mods[:, 2, :], 1.0, xn[:, t, :], ALU.add, ALU.mult).then_inc(sem("h2_scaled"), 1)
                dve.wait_ge(sem("h2_scaled"), t + 1)
                tt(h2[:, t, :], h2[:, t, :], mods[:, 1, :], ALU.add).then_inc(sem("h2_done"), 1)
            v.memset(o_ss, 0.0).then_inc(sem("ln1_done"), 1)
            NEG = -3.0e38
            u32 = lambda x: x.bitcast(U32)
            dve.wait_ge(sem("sc_copied"), 17)
            dve.wait_ge(sem("q_proj"), 4 + 16)
            groups = [(t, c) for t in range(2) for c in range(KT)]
            done = 0

            def top16(rows, name, vals, inds, src, rep):
                nonlocal done
                ops = (lambda r: v.max(vals(r)[:, 0:8], src(r)),
                       lambda r: v.max_index(u32(inds(r)[:, 0:8]), vals(r)[:, 0:8], src(r)),
                       lambda r: v.match_replace(rep(r), vals(r)[:, 0:8], src(r), NEG),
                       lambda r: v.max(vals(r)[:, 8:16], rep(r)),
                       lambda r: v.max_index(u32(inds(r)[:, 8:16]), vals(r)[:, 8:16], rep(r)))
                for op in ops:
                    for r in rows:
                        m = op(r)
                    done += 1
                    m.then_inc(sem("topk_step"), 1)
                    dve.wait_ge(sem("topk_step"), done)

            for g in range(0, 32, 8):
                top16(groups[g:g + 8], "keys", lambda r: tv[:, r[0], r[1], :], lambda r: ti[:, r[0], r[1], :],
                      lambda r: sc[:, r[0], r[1], :], lambda r: sc2[:, r[0], r[1], :])

            def step(ins):
                nonlocal done
                done += 1
                ins.then_inc(sem("topk_step"), 1)
                dve.wait_ge(sem("topk_step"), done)

            step(v.tensor_copy(tf, u32(ti)))
            for t in range(2):
                for h in range(PH):
                    m = tt(cand[:, h, :].rearrange("p (a b) -> p a b", a=TOPK),
                           tv[:, t, 2 * h, :].unsqueeze(2).broadcast_to([P, TOPK, TOPK]),
                           tv[:, t, 2 * h + 1, :].unsqueeze(1).broadcast_to([P, TOPK, TOPK]), ALU.add)
                step(m)
                top16(list(range(PH)), "cand", lambda h: bv[:, t, h * TOPK:(h + 1) * TOPK], lambda h: bj[:, t, h * TOPK:(h + 1) * TOPK],
                      lambda h: cand[:, h, :], lambda h: cand2[:, h, :])
                for part, ix in ((0, i0), (1, i1)):
                    if part == 0:
                        step(ts(u32(bhi[:, 0, :]), u32(bj[:, t, :]), 4, None, ALU.logical_shift_right))
                    else:
                        step(ts(u32(bhi[:, 0, :]), u32(bj[:, t, :]), 15, None, ALU.bitwise_and))
                    step(v.tensor_copy(bhi[:, 1, :], u32(bhi[:, 0, :])))
                    step(tt(onehot, bhi[:, 1, :].unsqueeze(2).broadcast_to([P, SLOTS, TOPK]),
                            const("iota16").unsqueeze(1).broadcast_to([P, SLOTS, TOPK]), ALU.is_equal))
                    o4 = onehot.rearrange("p (h k) m -> p h k m", h=PH)
                    lists = tf[:, t, part::2, :]
                    step(tt(o4, o4, lists.unsqueeze(2).broadcast_to([P, PH, TOPK, TOPK]), ALU.mult))
                    step(v.tensor_reduce(ix, onehot, AX.X, ALU.add))
                step(stt(u32(idx[:, t, :]), i0, float(NKEYS), i1, ALU.mult, ALU.add))
                b3 = bv[:, t, :].rearrange("p (h k) -> p h k", h=PH)
                tt(gate[:, t, :].rearrange("p (h k) -> p h k", h=PH), b3, b3[:, :, 0:1].broadcast_to([P, PH, TOPK]), ALU.subtract
                   ).then_inc(sem("bdiff"), 1)
            dve.wait_ge(sem("bexp"), 1)
            for t in range(2):
                g3 = gate[:, t, :].rearrange("p (h k) -> p h k", h=PH)
                step(v.tensor_reduce(esum, g3, AX.X, ALU.add))
                step(v.reciprocal(esum, esum))
                step(tt(g3, g3, esum.unsqueeze(2).broadcast_to([P, PH, TOPK]), ALU.mult))
            v.memset(idx_all[:, 2 * SLOTS:], 0.0)
            step(v.memset(y_acc, 0.0))
            dve.sem_inc(sem("ring_used"), 7)

            def row_wait(t, n, e):
                dve.wait_ge(sem(f"row_in{e % 8}"), n * 2 + (t * 512 + (e // 8 + 1) * 16))

            def set_idx(t, b, dst, name):
                v.tensor_copy(u32(dst), u32(idx_all[:, bass.ds(b * TOPK + t * SLOTS, TOPK)])).then_inc(sem(name), 1)

            def dot_batch(t, b, n):
                dve.wait_ge(sem("gelu_done"), b + t * PH)
                for e in range(TOPK):
                    row_wait(t, n, e)
                    dve.wait_ge(sem("ring_used"), n + (7 + t * 256 + e))
                    v.tensor_tensor_reduce(junk, ring[:, e % 8, :], h2[:, t, :], 1.0, 0.0, ALU.mult, ALU.add, dots[:, e:e + 1]
                                           ).then_inc(sem("ring_used"), 1)

            def add_batch(t, n):
                for e in range(TOPK):
                    row_wait(t, n, e)
                    dve.wait_ge(sem("ring_used"), n + (7 + t * 256 + e))
                    stt(y_acc[:, t, :], ring[:, e % 8, :], coef[:, e:e + 1], y_acc[:, t, :], ALU.mult, ALU.add
                        ).then_inc(sem("ring_used"), 1)

            def make_coef(t, b, n):
                dve.wait_ge(sem("gelu_done"), b + t * PH + 1)
                dve.wait_ge(sem("ring_used"), n + (7 + t * 256))
                tt(coef, gelu, gate[:, t, bass.ds(b * TOPK, TOPK)], ALU.mult).then_inc(sem("coef_done"), 1)
                dve.wait_ge(sem("coef_done"), b + t * PH + 1)

            set_idx(0, 0, idx_u, "idxu_set")
            for t in range(2):
                dot_batch(t, 0, 0 if t == 0 else -16)
                set_idx(t, 1, idx_u, "idxu_set")
                if t:
                    add_batch(0, 256)
                set_idx(t, 0, idx_v, "idxv_set")
                make_coef(t, 0, 16)
                with dve.Fori(1, PH) as b:
                    dot_batch(t, b, b * 32 - 16)
                    set_idx(t, b + 1, idx_u, "idxu_set")
                    add_batch(t, b * 32)
                    set_idx(t, b, idx_v, "idxv_set")
                    make_coef(t, b, b * 32 + 16)
            add_batch(1, 240)
            dve.wait_ge(sem("ring_used"), 7 + 512)
            for t in range(2):
                step(tt(y_acc[:, t, :], y_acc[:, t, :], mods[:, 3, :], ALU.mult))
                step(stt(xn[:, t, :], xn[:, t, :], ALPHA, y_acc[:, t, :], ALU.mult, ALU.add))
            dve.wait_ge(sem("ln2_in"), 32)
            for t in range(2):
                layer_norm(1, t, xn[:, t, :])
                v.memset(o_ss[:, 0:1], 0.0).then_inc(sem("result"), 1)

        @block.gpsimd
        def _(pool):
            pool.wait_ge(sem("gating_step"), 7)
            for s in range(2):
                pool.dma_start(beta_scr[s], xm.rearrange("p h i -> p (h i)")[0:HD, s * SEQ:(s + 1) * SEQ]
                               ).then_inc(sem("beta_out"), 16)
            pool.wait_ge(sem("beta_out"), 32)
            pool.sem_inc(sem("stored"), 1)
            with pool.Fori(0, H) as h:
                pool.wait_ge(sem("gram_used"), 1 + 4 * h + 2)
                for d in range(2):
                    for s in range(2):
                        dst = mix_scr[s].rearrange("(d h c) (a b) -> d h (c a) b", d=2, h=H, b=CH)[d, bass.ds(h, 1)]
                        dst = dst.rearrange("o (t p) b -> p (o t) b", p=P)
                        pool.dma_start(dst, mt[:, d, 2 * s:2 * s + 2, :]).then_inc(sem("mt_out"), 16)
                pool.wait_ge(sem("gram_used"), 1 + 4 * h + 4)
                pool.wait_ge(sem("k_copied"), 1 + h + 1)
                pool.wait_ge(sem("v_copied"), 1 + h + 1)
                pool.dma_start(rec_scr[bass.ds(h, 1)].rearrange("o p n -> p (o n)"), rec).then_inc(sem("rec_out"), 16)
                pool.wait_ge(sem("mt_out"), 64 * h + 64)
                pool.wait_ge(sem("rec_out"), 16 * h + 16)
                pool.sem_inc(sem("stored"), 1)
            pool.sem_inc(sem("inv_stored"), 1)
            for n, s in enumerate((1, 0)):
                if n:
                    pool.wait_ge(sem("solved"), n)
                pool.dma_start(sol.rearrange("p a b -> p (a b)"), mix_scr[s]).then_inc(sem("mix_in"), 16)
                pool.dma_start(sol_b, beta_scr[s].rearrange("h (c i) -> (h c) i", i=CH)).then_inc(sem("mix_in"), 16)
                pool.wait_ge(sem("solved"), n + 1)
                pool.dma_start(inv_scr[s], sol_o.rearrange("p a b -> p (a b)")).then_inc(sem("inv_out"), 16)
                pool.wait_ge(sem("inv_out"), 16 * n + 16)
                pool.sem_inc(sem("inv_stored"), 1)

            def gather(t, n, table, ids):
                for e in range(TOPK):
                    pool.wait_ge(sem("ring_used"), n + (t * 256 + e))
                    pool.sem_inc(sem("pool_passed"), 1)
                    pool.indirect_dma_start(ring[:, e % 8, :], None, a[table],
                                            bass.IndirectOffsetOnAxis(ap=ids[:, e:e + 1].bitcast(U32), axis=0)
                                            ).then_inc(sem(f"row_in{e % 8}"), 16)

            for t in range(2):
                pool.wait_ge(sem("idxu_set"), t * PH + 1)
                gather(t, 0 if t == 0 else -16, "peer_u", idx_u)
                if t:
                    pool.wait_ge(sem("idxv_set"), PH)
                    gather(0, 256, "peer_v", idx_v)
                with pool.Fori(1, PH) as b:
                    pool.wait_ge(sem("idxu_set"), b + (t * PH + 1))
                    gather(t, b * 32 - 16, "peer_u", idx_u)
                    pool.wait_ge(sem("idxv_set"), b + t * PH)
                    gather(t, b * 32, "peer_v", idx_v)
            pool.wait_ge(sem("idxv_set"), 2 * PH)
            gather(1, 240, "peer_v", idx_v)



def host_layout(i):
    f = lambda v: np.ascontiguousarray(v)
    x, ctx_, c, cc = i["x"][0], i["ctx"][0], i["c"][0], i["c_ctx"]
    w_in = i["w_in"][0]
    o = {}
    o["consts"] = constant_table()
    o["cond"] = f(np.stack([c.reshape(KT, P).T, cc.reshape(KT, P).T], -1))
    o["xcT"] = f(np.concatenate([x.T, ctx_.T], 1).reshape(KT, P, TOK).transpose(1, 0, 2))
    o["x"] = f(x)
    o["b_ada"] = f(i["b_ada"][0])
    o["w_ada"] = f(i["w_ada"][0].reshape(2, 8, P, 24, N1).transpose(3, 0, 2, 1, 4).reshape(48, P, 8, N1))
    tiles = lambda w: w.reshape(KT, P, -1, P).transpose(2, 1, 0, 3)
    q, k, v, z = (tiles(w_in[:, n * D:(n + 1) * D]) for n in range(4))
    hy = tiles(w_in[:, 4 * D + 64:4 * D + 64 + 3 * D])
    gates = tiles(w_in[:, 7 * D + 64:])
    heads = np.stack([q, k, v], 1).reshape(3 * H, P, KT, P)
    o["w_in"] = f(np.concatenate([heads, z, gates, hy]))
    o["w_ab"] = f(w_in[:, 4 * D:4 * D + 64].reshape(KT, P, 64).transpose(1, 0, 2))
    o["dn_a_log"] = f(i["dn_a_log"][0].reshape(-1))
    o["dn_dt_bias"] = f(i["dn_dt_bias"][0].reshape(-1))
    o["dn_conv"] = f(i["dn_conv_w"][0].reshape(TAPS, 3, H, P).transpose(3, 2, 1, 0).reshape(P, 48, TAPS))
    o["hy_conv"] = f(i["hy_conv_w"][0].reshape(HTAPS, 48, P).transpose(2, 1, 0))
    o["dn_norm_w"] = f(i["dn_norm_w"][0].reshape(P, 1))
    n = SEQ
    t = np.linspace(0.0, 1.0, n, dtype=np.float32)
    bands = np.linspace(1e-4, 15, 16, dtype=np.float32)
    angle = np.float32(2.0 * np.pi / n) * np.arange(n, dtype=np.float32)[:, None] * bands[None, :]
    o["hy_z"] = f(np.concatenate([t[:, None], np.cos(angle), -np.sin(angle)], 1).T.astype(np.float32))
    delta = np.abs(np.linspace(np.log(1e-2) / 1.5, np.log(1e-2) / 0.3, D, dtype=np.float32))
    window = np.exp(-t[:, None] * delta[None, :]).astype(np.float32)
    o["hy_win"] = f(window.reshape(2, P, 4, N1).transpose(2, 1, 0, 3))
    o["hy_w1"] = f(i["hy_w1"][0])
    o["hy_w2"] = f(i["hy_w2"][0])
    o["hy_cols"] = f(np.stack([i["hy_b1"][0], i["hy_b2"][0], i["hy_freq"][0]], 1))
    w3 = np.concatenate([i["hy_w3"][0], i["hy_b3"][0][None, :]], 0)
    o["hy_w3"] = f(w3.reshape(65, 4, 4, N1).transpose(2, 0, 1, 3))
    o["hy_skip"] = f(i["hy_skip"][0].reshape(2, 4, N1).transpose(1, 0, 2))
    o["w_branch"] = f(np.stack([tiles(i["w_branch_dn"][0]), tiles(i["w_branch_hy"][0])], 1).reshape(32, P, KT, P))
    o["w_out"] = f(i["w_out"][0].reshape(2, 8, P, 4, N1).transpose(3, 0, 2, 1, 4).reshape(8, P, 8, N1))
    o["w_q"] = f(tiles(i["peer_wq"][0]))
    o["subkeys"] = f(i["peer_subkeys"][0].reshape(KT, NKEYS, P).transpose(2, 0, 1))
    for name in ("ln1_g", "ln1_b", "ln2_g", "ln2_b", "peer_u", "peer_v"):
        o[name] = f(i[name][0])
    return o


def kernel(**inputs):
    import concourse.bacc as bacc
    from concourse.bass_utils import run_bass_kernel_spmd

    arrays = host_layout({n: np.asarray(v) for n, v in inputs.items()})
    nc = bacc.Bacc("TRN2", target_bir_lowering=False, num_devices=1)
    a = {n: nc.dram_tensor(n + "_in", v.shape, F32, kind="ExternalInput").ap() for n, v in arrays.items()}
    out = nc.dram_tensor("out_0_dram", (1, SEQ, D), F32, kind="ExternalOutput").ap()
    build(nc, a, out.rearrange("b n d -> (b n) d"))
    r = run_bass_kernel_spmd(nc, [{n + "_in": v for n, v in arrays.items()}], core_ids=[0])
    return r.results[0]["out_0_dram"]
```

```python
from contextlib import ExitStack

import concourse.bass as bass
from concourse import mybir
import numpy as np

F32 = mybir.dt.float32
U32 = mybir.dt.uint32
ALU = mybir.AluOpType
ACT = mybir.ActivationFunctionType
AX = mybir.AxisListType

P = 128
D = 2048
KT = D // P
SEQ = 256
TOK = 2 * SEQ
CH = 64
NCH = SEQ // CH
H = 16
DK = 128
HD = 2 * H
TAPS = 5
HTAPS = 3
PH = 8
TOPK = 16
NKEYS = 128
SLOTS = PH * TOPK
ALPHA = 2.0 ** 0.25
BIG = 1.0e30
N1 = 512

CONST_COLS = {}
_at = 0
for _n, _w in (("ident", 128), ("ones", 128), ("blockones", 128), ("low_half", 128), ("high_half", 128),
               ("cum_f", 128), ("cum_b", 128), ("tri_f", 64), ("tri_b", 64), ("mask_above", 64),
               ("mask_below", 64), ("cos", 512), ("sin", 512), ("icos", 512), ("isin", 512),
               ("iota16", 16), ("not_first", 1)):
    CONST_COLS[_n] = (_at, _at + _w)
    _at += _w
CONST_W = _at


def constant_table():
    t = np.zeros((P, CONST_W), np.float32)
    p = np.arange(P)[:, None]
    c = np.arange(P)[None, :]
    i = np.arange(CH)[None, :]
    same = (p // CH) == (c // CH)

    def put(name, a):
        lo, hi = CONST_COLS[name]
        t[:, lo:hi] = a

    put("ident", p == c)
    put("ones", 1.0)
    put("blockones", same)
    put("low_half", (p < CH) & (c >= 0))
    put("high_half", (p >= CH) & (c >= 0))
    put("cum_f", same & (p <= c))
    put("cum_b", same & (p >= c))
    put("tri_f", (p % CH) <= i)
    put("tri_b", (p % CH) >= i)
    put("mask_above", BIG * (i > p % CH))
    put("mask_below", BIG * (i < p % CH))
    n = np.arange(SEQ, dtype=np.float64)
    ang = 2 * np.pi * (n[:, None] * (n[None, :] + 0.5)) / (2 * SEQ)
    two = lambda a: a.reshape(2, P, SEQ).transpose(1, 0, 2).reshape(P, 2 * SEQ)
    put("cos", two(np.cos(ang)))
    put("sin", two(np.sin(ang)))
    put("icos", two(np.cos(ang.T) / SEQ))
    put("isin", two(np.sin(ang.T) / SEQ))
    put("iota16", np.arange(16)[None, :])
    put("not_first", p > 0)
    return t


def build(nc, a, out):
    with ExitStack() as ctx:
        made = {}

        def sem(name):
            if name not in made:
                made[name] = ctx.enter_context(nc.semaphore(name))
            return made[name]

        ARENA = 52840
        arena = ctx.enter_context(nc.sbuf_tensor("arena", [P, ARENA], F32))
        bank = [ctx.enter_context(nc.psum_tensor(f"bank{i}", [P, N1], F32)) for i in range(8)]

        def area(at, *shape):
            size = int(np.prod(shape))
            assert at + size <= ARENA, (at, shape)
            v = arena[:, at:at + size]
            if len(shape) == 2:
                v = v.rearrange("p (a b) -> p a b", a=shape[0])
            if len(shape) == 3:
                v = v.rearrange("p (a b c) -> p a b c", a=shape[0], b=shape[1])
            return v

        def dram(name, *shape):
            return nc.dram_tensor(name, shape, F32, kind="Internal").ap()

        mix_scr = dram("mix_scr", 2, P, CH * CH)
        inv_scr = dram("inv_scr", 2, P, CH * CH)
        beta_scr = dram("beta_scr", 2, HD, SEQ)
        rec_scr = dram("rec_scr", H, P, 2048)

        cst = area(0, CONST_W)

        def const(name):
            lo, hi = CONST_COLS[name]
            return cst[:, lo:hi]

        HT0 = 3600
        WR0 = HT0 + KT * TOK
        R0 = WR0 + 4 * KT * P
        assert CONST_W <= HT0
        hT = area(HT0, KT, TOK)
        wring = area(WR0, 4, KT * P).rearrange("p s (k n) -> p s k n", k=KT)
        ada_ring = area(R0, 4, 8 * N1).rearrange("p s (k n) -> p s k n", k=8)
        ada_row = area(R0 + 24576, 4, 2 * N1).rearrange("p g (w n) -> p g w n", w=2)
        cond = area(52600, KT, 2)
        adac = area(52640, 64)
        badac = area(52704, 64)
        cond_row = area(R0 + 22240, D)
        ada_junk = area(R0 + 28672, D)
        ada_dot = area(52768, 4)
        cols = area(R0 + 20540, KT, 4).rearrange("p k (w s) -> p k w s", w=2)
        G0 = R0 + 12288
        w_ab = area(R0 + 19500, KT, CH)
        abT = area(G0 + 512, TOK)
        ab = area(G0 + 1024, 4, 64)
        xs = area(G0 + 1280, 4, HD)
        sp_m = area(G0 + 1408, 4, HD)
        sp_e = area(G0 + 1536, 4, HD)
        gate_row = area(R0 + 20620, 2, HD)
        gx = area(G0 + 2048, HD, CH)
        xm = area(G0 + 4096, HD, CH)
        xm2 = area(G0 + 6144, H, CH)
        K0 = 50900
        g_tok = area(K0, 4, HD)
        beta = area(K0 + 128, 4, HD)
        gcum = area(K0 + 256, 4, HD)
        eg = area(K0 + 384, 4, HD)
        neg_eg = area(K0 + 512, 4, HD)
        etail = area(K0 + 640, 4, HD)
        etot = area(K0 + 768, 2, 4 * HD)
        dn_nw = area(K0 + 1024, 1)
        eps6 = area(K0 + 1025, 1)
        eps5 = area(K0 + 1026, 1)
        hyc = area(K0 + 1032, 48, HTAPS)
        n_e1f = area(R0, 4, H * CH).rearrange("p t (h i) -> p t h i", h=H)
        n_eb = area(R0 + 4096, 4, H * CH).rearrange("p t (h i) -> p t h i", h=H)
        a_e2f = area(R0 + 8192, 2, H * CH).rearrange("p t (h i) -> p t h i", h=H)
        a_eb = area(R0 + 10240, 2, H * CH).rearrange("p t (h i) -> p t h i", h=H)
        X0 = R0 + 12288
        PADL, PADC = CH + TAPS - 1, SEQ + TAPS - 1
        cw = NCH * PADL + PADC
        cbuf = area(X0, 3, cw)
        acc = area(X0 + 1600, 3, TOK)
        raw = area(X0 + 3200, 3, TOK)
        sq = area(X0 + 4800, 2, TOK)
        nrm = area(X0 + 5900, 2, TOK)
        rec = area(X0 + 7000, 2048)
        mt = area(X0 + 9100, 2, 4 * CH).rearrange("p d (t i) -> p d t i", t=4)
        dnc = area(X0 + 9700, 48, TAPS)
        r_kT = rec[:, 0:512]
        r_qT = rec[:, 512:768]
        r_k = rec[:, 768:1280]
        r_v = rec[:, 1280:1792]
        r_at = rec[:, 1792:2048].rearrange("p (d t i) -> p d t i", d=2, t=2)

        c_lat = [cbuf[:, t, 0:NCH * PADL].rearrange("p (r w) -> p r w", r=NCH) for t in range(3)]
        c_ctx = [cbuf[:, t, NCH * PADL:cw] for t in range(3)]

        zsT = area(R0 + 24576, KT, SEQ)
        gT = area(R0 + 4096, 2 * KT, SEQ)
        yhT = area(R0 + 12288, KT, SEQ)
        uv = area(R0 + 16384, 2, 2 * D)
        sol = area(R0 + 16384, CH, CH)
        sol_o = area(R0, CH, CH)
        sol_t = area(R0 + 12288, CH * CH // 4)
        sol_b = area(R0 + 13400, CH)
        hbuf = area(R0 + 28672, 4, NCH * (CH + 2)).rearrange("p s (r w) -> p s r w", r=NCH)
        hacc = area(R0 + 28672 + 1056, 4, SEQ)
        mixed = area(K0 + 1200, 6, 4 * H).rearrange("p m (t h) -> p m t h", t=4)
        w3c = area(HT0, 4, N1)
        win = area(HT0 + 2048, 2, N1)
        skipc = area(HT0 + 3072, 2, N1)
        fa = area(HT0 + 4096, 2, N1)
        fb = area(HT0 + 5120, 2, N1)
        Fr = area(HT0 + 6144, 2, N1)
        Fi = area(HT0 + 7168, 2, N1)
        t1 = area(HT0 + 8192, 2, N1)
        t2 = area(HT0 + 9216, 2, N1)
        Yr = area(HT0 + 10240, 2, N1)
        Yi = area(HT0 + 11264, 2, N1)
        yb = area(HT0 + 12288, 2, N1)
        zT = area(HT0 + 13312, SEQ)
        hid1 = area(HT0 + 13568, SEQ)
        hid2 = area(HT0 + 13824, SEQ)
        ang = area(HT0 + 14080, SEQ)
        turns = area(HT0 + 14336, SEQ)
        fw1 = area(HT0 + 14592, CH)
        fw2 = area(HT0 + 14656, CH)
        fcol = area(HT0 + 14720, 3)
        mods = area(R0 + 16384, 4, D)
        SC0 = R0 + 16384
        recs = area(HT0, 8, 2048)
        invs = area(R0, 8, 512).rearrange("p s (q d t i) -> p s q d t i", q=2, d=2, t=2)
        state = area(SC0, 8, P)
        r_in = area(SC0 + 1024, 4, P)
        v_new = area(SC0 + 1536, 4, P)
        v_tail = area(SC0 + 2048, 4, P)
        o_acc = area(SC0 + 2560, 8, P)
        o_sq = area(SC0 + 3584, P)
        o_ss = area(SC0 + 3712, 8)
        tmp_g = area(R0 + 28672, 2, SEQ)
        wo_ring = area(HT0, 2, 8 * N1).rearrange("p s (k n) -> p s k n", k=8)
        tmp_m = area(R0 + 29184, 2, N1)
        xn = area(R0 + 12288, 2, D)
        lnp = area(R0, 2, D)
        h2 = area(R0 + 8192, 2, D)
        stats = area(K0 + 1200, 2, 24)
        aggr = area(K0 + 1250, 2, 2)
        rstd = area(K0 + 1256, 2)
        h2T = area(HT0, KT, SEQ)
        subk = area(R0 + 24576, KT, NKEYS)
        q_sb = area(R0 + 26624, 4, SEQ)
        sc = area(HT0 + 4096, 2, KT * NKEYS).rearrange("p t (c n) -> p t c n", c=KT)
        tv = area(R0 + 28672, 2, KT * TOPK).rearrange("p t (c n) -> p t c n", c=KT)
        ti = area(R0 + 29184, 2, KT * TOPK).rearrange("p t (c n) -> p t c n", c=KT)
        sc2 = area(R0 + 16384, 2, KT * NKEYS).rearrange("p t (c n) -> p t c n", c=KT)
        cand = area(R0 + 16384, PH, TOPK * TOPK)
        cand2 = area(R0 + 18432, PH, TOPK * TOPK)
        onehot = area(R0 + 20480, SLOTS, TOPK)
        bv = area(R0 + 29696, 2, SLOTS)
        bj = area(R0 + 29952, 2, SLOTS)
        bhi = area(R0 + 30208, 2, SLOTS)
        tf = area(R0 + 26624, 2, KT * TOPK).rearrange("p t (c n) -> p t c n", c=KT)
        i0 = area(R0 + 27136, SLOTS)
        i1 = area(R0 + 27264, SLOTS)
        idx = area(R0 + 30464, 2, SLOTS)  
        idx_all = area(R0 + 30464, 2 * SLOTS + TOPK)
        gate = area(K0, 2, SLOTS)
        esum = area(K0 + 256, PH)
        ring = area(HT0, 8, D)
        y_acc = area(R0 + 4096, 2, D)
        junk = area(R0 + 24576, D)
        idx_u = area(K0 + 300, TOPK)
        idx_v = area(K0 + 320, TOPK)
        dots = area(K0 + 340, TOPK)
        gelu = area(K0 + 360, TOPK)
        coef = area(K0 + 380, TOPK)
        assert K0 >= R0 + 30720

        block = ctx.enter_context(nc.Block())

        HF = (slice(0, CH), slice(CH, P))

        @block.sync
        def _(sp):
            sp.dma_start(cst, a["consts"]).then_inc(sem("consts_in"), 16)
            sp.dma_start(cond, a["cond"]).then_inc(sem("cond_in"), 16)
            sp.dma_start(ada_row[0:2].rearrange("p g w n -> p (g w n)"), a["b_ada1"].partition_broadcast(2)).then_inc(sem("bada_in"), 16)
            for s in range(4):
                sp.dma_start(ada_ring[:, s], a["w_ada1"][s]).then_inc(sem(f"slot_in{4 + s}"), 16)
            sp.dma_start(hT, a["xcT"]).then_inc(sem("x_in"), 16)
            with sp.Fori(1, 4) as i:
                for s in range(4):
                    sp.wait_ge(sem("ada_used"), i * 4 + (s - 3))
                    sp.dma_start(ada_ring[:, s], a["w_ada1"][bass.ds(i * 4 + s, 1)].rearrange("o p k n -> p (o k) n")
                                 ).then_inc(sem(f"slot_in{4 + s}"), 16)
            sp.dma_start(badac, a["b_ada2"]).then_inc(sem("badac_in"), 16)
            sp.dma_start(cond_row, a["c_row"].partition_broadcast(P)).then_inc(sem("badac_in"), 16)
            sp.dma_start(w_ab, a["w_ab"]).then_inc(sem("wab_in"), 16)
            sp.dma_start(gate_row[:, 0, :], a["dn_a_log"].partition_broadcast(P)).then_inc(sem("gate_in"), 16)
            sp.dma_start(gate_row[:, 1, :], a["dn_dt_bias"].partition_broadcast(P)).then_inc(sem("gate_in"), 16)
            sp.dma_start(hyc, a["hy_conv"]).then_inc(sem("hyc_in"), 16)
            sp.dma_start(dn_nw, a["dn_norm_w"]).then_inc(sem("hyc_in"), 16)
            sp.dma_start(dnc, a["dn_conv"]).then_inc(sem("dnc_in"), 16)
            with sp.Fori(0, 4) as i:
                for s in range(4):
                    sp.wait_ge(sem("zg_proj"), 1 + i * 4 + s)
                    sp.dma_start(wring[:, s], a["w_in"][bass.ds(i * 4 + (48 + s), 1)].rearrange("o p k n -> p (o k) n")
                                 ).then_inc(sem(f"slot_in{s}"), 16)
            for t in range(3):
                sp.wait_ge(sem("zg_proj"), 4 + 12 + t + 1)
                sp.dma_start(wring[:, t], a["w_in"][t]).then_inc(sem(f"slot_in{t}"), 16)
            with sp.Fori(1, H) as h:
                for t in range(3):
                    sp.wait_ge(sem("proj"), 1 + 3 * h + t)
                    sp.dma_start(wring[:, t], a["w_in"][bass.ds(3 * h + t, 1)].rearrange("o p k n -> p (o k) n")
                                 ).then_inc(sem(f"slot_in{t}"), 16)
            sp.wait_ge(sem("proj"), 3 + 3 * H)
            sp.wait_ge(sem("ada2_used"), 1 + 4 * H)
            with sp.Fori(4, 12) as i:
                for s in range(4):
                    sp.wait_ge(sem("zg_proj"), 1 + i * 4 + s)
                    sp.dma_start(wring[:, s], a["w_in"][bass.ds(i * 4 + (48 + s), 1)].rearrange("o p k n -> p (o k) n")
                                 ).then_inc(sem(f"slot_in{s}"), 16)
            sp.wait_ge(sem("zg_proj"), 4 + 48)
            with sp.Fori(0, 12) as i:
                for s in range(4):
                    sp.wait_ge(sem("hy_proj"), 1 + i * 4 + s)
                    sp.dma_start(wring[:, s], a["w_in"][bass.ds(i * 4 + (96 + s), 1)].rearrange("o p k n -> p (o k) n")
                                 ).then_inc(sem(f"slot_in{s}"), 16)
            sp.wait_ge(sem("hy_proj"), 4 + 48)
            sp.dma_start(zT[0:33, :], a["hy_z"]).then_inc(sem("hyf_in"), 16)
            sp.dma_start(fw1[0:33, :], a["hy_w1"]).then_inc(sem("hyf_in"), 16)
            sp.dma_start(fw2[0:CH, :], a["hy_w2"]).then_inc(sem("hyf_in"), 16)
            sp.dma_start(fcol[0:CH, :], a["hy_cols"]).then_inc(sem("hyf_in"), 16)
            with sp.Fori(0, 4) as n:
                sp.wait_ge(sem("fil_used"), 1 + 2 * n)
                sp.dma_start(w3c[0:65], a["hy_w3"][bass.ds(n, 1)].rearrange("o p k n -> p (o k) n")).then_inc(sem("w3_in"), 16)
                sp.dma_start(win, a["hy_win"][bass.ds(n, 1)].rearrange("o p k n -> p (o k) n")).then_inc(sem("w3_in"), 16)
                sp.dma_start(skipc[0:1], a["hy_skip"][bass.ds(n, 1)].rearrange("o (p k) n -> (o p) k n", p=1)).then_inc(sem("w3_in"), 16)
            sp.wait_ge(sem("inv_out"), 32)
            sp.wait_ge(sem("rec_out"), 16 * H)
            with sp.Fori(0, 2) as i:
                for r in range(2):
                    sp.wait_ge(sem("o_merged"), 1 + i * 8 + 4 * r)
                    for u in range(4):
                        h = i * 8 + (4 * r + u)
                        for q in range(2):
                            for d in range(2):
                                src = inv_scr[q].rearrange("(d h c) (a b) -> d h (c a) b", d=2, h=H, b=CH)[d, bass.ds(h, 1)]
                                src = src.rearrange("o (t p) b -> p (o t) b", p=P)
                                sp.dma_start(invs[:, 4 * r + u, q, d], src).then_inc(sem(f"rec_in{r}"), 16)
                    sp.wait_ge(sem("inv_used"), 25)
                    for u in range(4):
                        h = i * 8 + (4 * r + u)
                        sp.dma_start(recs[:, 4 * r + u], rec_scr[bass.ds(h, 1)].rearrange("o p n -> p (o n)")).then_inc(sem(f"rec_in{r}"), 16)
            with sp.Fori(0, 8) as i:
                for s in range(4):
                    sp.wait_ge(sem("br_proj"), 1 + i * 4 + s)
                    sp.dma_start(wring[:, s], a["w_branch"][bass.ds(i * 4 + s, 1)].rearrange("o p k n -> p (o k) n")
                                 ).then_inc(sem(f"slot_in{s}"), 16)
            for s in range(2):
                sp.dma_start(wo_ring[:, s], a["w_out"][s]).then_inc(sem(f"wo_in{s}"), 16)
            sp.wait_ge(sem("br_proj"), 4 + 32)
            sp.dma_start(xn, a["x"].rearrange("(t p) n -> p t n", p=P)).then_inc(sem("xres_in"), 16)
            sp.dma_start(lnp[:, 0, :], a["ln1_g"].partition_broadcast(P)).then_inc(sem("ln1_in"), 16)
            sp.dma_start(lnp[:, 1, :], a["ln1_b"].partition_broadcast(P)).then_inc(sem("ln1_in"), 16)
            with sp.Fori(1, 4) as i:
                for s in range(2):
                    sp.wait_ge(sem("wo_used"), 1 + i * 2 + s)
                    sp.dma_start(wo_ring[:, s], a["w_out"][bass.ds(i * 2 + s, 1)].rearrange("o p k n -> p (o k) n")
                                 ).then_inc(sem(f"wo_in{s}"), 16)
            sp.wait_ge(sem("o_merged"), 5 + 16)
            sp.wait_ge(sem("mix_added"), 9)
            sp.dma_start(subk, a["subkeys"]).then_inc(sem("subk_in"), 16)
            with sp.Fori(0, 4) as i:
                for s in range(4):
                    sp.wait_ge(sem("q_proj"), 1 + i * 4 + s)
                    sp.dma_start(wring[:, s], a["w_q"][bass.ds(i * 4 + s, 1)].rearrange("o p k n -> p (o k) n")
                                 ).then_inc(sem(f"slot_in{s}"), 16)
            sp.wait_ge(sem("h2_done"), 2)
            sp.dma_start(lnp[:, 0, :], a["ln2_g"].partition_broadcast(P)).then_inc(sem("ln2_in"), 16)
            sp.dma_start(lnp[:, 1, :], a["ln2_b"].partition_broadcast(P)).then_inc(sem("ln2_in"), 16)
            for t in range(2):
                sp.wait_ge(sem("result"), t + 1)
                sp.dma_start(out[t * P:(t + 1) * P, :], xn[:, t, :]).then_inc(sem("out_done"), 16)
            sp.wait_ge(sem("out_done"), 32)

        @block.tensor
        def _(pe):
            mm = nc.tensor.matmul
            pe.sem_inc(sem("o_turned"), 1)
            pe.wait_ge(sem("consts_in"), 16)
            pe.sem_inc(sem("zg_proj"), 4)
            pe.wait_ge(sem("cond_done"), 1)

            def ada_rows(i):
                for w in range(2):
                    pe.wait_ge(sem("row_done"), i * 2 + (w + 1))
                    for half in range(2):
                        s = 2 * w + half
                        pe.wait_ge(sem(f"slot_in{4 + s}"), i * 16 + 16)
                        for k in range(8):
                            m = mm(bank[w][0:2, :], cond[:, half * 8 + k, :], ada_ring[:, s, k, :],
                                   start=(half == 0 and k == 0), stop=(half == 1 and k == 7))
                        m.then_inc(sem("ada_used"), 1)

            def ada_turn(i):
                pe.wait_ge(sem("row_done"), i * 2 + (2 + 2))
                pe.wait_ge(sem("cols_done"), i + 1)
                for w in range(2):
                    for e in range(4):
                        m = mm(bank[2][:, 4 * e + 2 * w:4 * e + 2 * w + 2], ada_row[0:2, i, w, e * P:(e + 1) * P],
                               const("ident")[0:2, 0:2], start=True, stop=True)
                m.then_inc(sem("cols_ready"), 1)

            ada_rows(0)
            for i in range(1, 4):
                ada_rows(i)
                ada_turn(i - 1)
            ada_turn(3)

            def wide(slot, b, src):
                for k in range(KT):
                    m = mm(bank[b][:, 0:SEQ], wring[:, slot, k, :], src[:, k, 0:SEQ], start=(k == 0), stop=(k == KT - 1))
                return m

            def z_project(i):
                for s in range(4):
                    pe.wait_ge(sem(f"slot_in{s}"), i * 16 + 16)
                    if i * 4 + s >= 2:
                        pe.wait_ge(sem("zg_evac"), 4 + i * 4 + s - 1)
                    wide(s, 0 if s % 2 else 3, hT).then_inc(sem("zg_proj"), 1)

            pe.wait_ge(sem("wab_in"), 16)
            pe.wait_ge(sem("h_done"), 32)
            for k in range(KT):
                m = mm(bank[0][0:CH, :], w_ab[:, k, :], hT[:, k, :], start=(k == 0), stop=(k == KT - 1))
            m.then_inc(sem("abT_ready"), 1)
            pe.wait_ge(sem("abT_copied"), 1)
            for t in range(4):
                for half in range(2):
                    c0 = SEQ * (t // 2) + CH * ((0, 3), (1, 2))[t % 2][half]
                    m = mm(bank[1][HF[half], t * 64:t * 64 + 64], abT[0:CH, c0:c0 + CH], const("ident")[0:CH, 0:CH],
                           start=True, stop=True)
            m.then_inc(sem("gating_mm"), 1)
            pe.wait_ge(sem("gating_step"), 1)
            z_project(0)
            pe.wait_ge(sem("beta_done"), 1)
            for t in range(4):
                m = mm(bank[4][0:HD, t * P:(t + 1) * P], beta[:, t, :], const("ident"), start=True, stop=True)
            m.then_inc(sem("gating_mm"), 1)
            pe.wait_ge(sem("gating_step"), 6)
            gd = lambda d: g_tok[:, :, d * H:(d + 1) * H]
            cum = bank[1][:, 0:128].rearrange("p (t h) -> p t h", t=4)
            mm(cum[:, :, 0:H], const("cum_f"), gd(0), start=True, stop=True)
            m = mm(cum[:, :, H:HD], const("cum_b"), gd(1), start=True, stop=True)
            m.then_inc(sem("gating_mm"), 1)
            gall = g_tok.rearrange("p t h -> p (t h)")
            mm(bank[2][:, 0:128], const("blockones"), gall, start=True, stop=True)
            mm(bank[2][:, 128:256], const("low_half"), gall, start=True, stop=True)
            m = mm(bank[2][:, 256:384], const("high_half"), gall, start=True, stop=True)
            m.then_inc(sem("gating_mm"), 1)
            for t in range(4):
                pe.wait_ge(sem("gx_done"), t + 1)
                if t == 0:
                    pe.wait_ge(sem("gating_step"), 7)
                else:
                    pe.wait_ge(sem("xm_done"), 4 * t)
                for b in range(4):
                    m = mm(bank[4 + b][:, :], const("blockones"), gx.rearrange("p h i -> p (h i)")[:, b * N1:(b + 1) * N1],
                           start=True, stop=True)
                m.then_inc(sem("gb_ready"), 1)
                if t != 2:
                    z_project((1, 2, None, 3)[t])

            def project(h, t):
                n = SEQ if t == 0 else TOK
                pe.wait_ge(sem(f"slot_in{t}"), 16 * h + (64 + 16))
                pe.wait_ge(sem("proj_copied"), 3 * h + t)
                for k in range(KT):
                    m = mm(bank[t][:, 0:n], wring[:, t, k, :], hT[:, k, 0:n], start=(k == 0), stop=(k == KT - 1))
                m.then_inc(sem("proj"), 1)

            def norms(h):
                for j, n in ((0, SEQ), (1, TOK)):
                    pe.wait_ge(sem("squared"), 2 * h + j + 1)
                    pe.wait_ge(sem("rooted"), 1 + 2 * h)
                    mm((bank[3] if j == 0 else bank[7])[:, 0:n], const("ones"), sq[:, j, 0:n], start=True, stop=True
                       ).then_inc(sem("ssq"), 1)

            def turn(h):
                pe.wait_ge(sem("silued"), 3 * h + 3)
                pe.wait_ge(sem("v_copied"), 1 + h)
                for t in range(4):
                    m = nc.tensor.transpose(bank[5][:, t * P:(t + 1) * P], raw[:, 2, t * P:(t + 1) * P], const("ident"))
                m.then_inc(sem("v_turned"), 1)
                pe.wait_ge(sem("normed"), 1 + 2 * h + 2)
                pe.wait_ge(sem("k_copied"), 1 + h)
                for t in range(4):
                    m = nc.tensor.transpose(bank[4][:, t * P:(t + 1) * P], r_kT[:, t * P:(t + 1) * P], const("ident"))
                m.then_inc(sem("k_turned"), 1)
                pe.wait_ge(sem("gram_used"), 1 + 4 * h)
                for t in range(4):
                    for half in range(2):
                        cs = slice(t * P + half * CH, t * P + half * CH + CH)
                        mm(bank[6][HF[half], t * CH:(t + 1) * CH], r_kT[:, cs], r_kT[:, cs], start=True, stop=True)
                for t in range(2):
                    for half in range(2):
                        cs = slice(t * P + half * CH, t * P + half * CH + CH)
                        m = mm(bank[6][HF[half], 256 + t * CH:256 + (t + 1) * CH], r_kT[:, cs], r_qT[:, cs],
                               start=True, stop=True)
                m.then_inc(sem("gram"), 1)

            pe.wait_ge(sem("decay_done"), 1)
            pe.wait_ge(sem("zg_evac"), 4 + 16)
            pe.sem_inc(sem("proj"), 3)
            for t in range(3):
                project(0, t)
            with pe.Fori(1, H) as h:
                project(h, 0)
                norms(h - 1)
                project(h, 1)
                project(h, 2)
                turn(h - 1)
            norms(H - 1)
            turn(H - 1)

            def weights_in(slot, use):
                pe.wait_ge(sem(f"slot_in{slot}"), use * 16 + (16 * H * (slot < 3) + 16))

            with pe.Fori(4, 12) as i:
                for s in range(4):
                    weights_in(s, i)
                    pe.wait_ge(sem("zg_evac"), 1 + i * 4 + s)
                    wide(s, 7 if s == 3 else s, hT).then_inc(sem("zg_proj"), 1)
            pe.sem_inc(sem("hy_proj"), 4)
            pe.sem_inc(sem("hy_turned"), 4)
            pe.wait_ge(sem("zg_evac"), 4 + 48)

            def hy_project(i, s):
                weights_in(s, i + 12)
                pe.wait_ge(sem("hy_evac"), 1 + i * 4 + s)
                wide(s, s, hT).then_inc(sem("hy_proj"), 1)

            def hy_turn(i, s):
                pe.wait_ge(sem("hy_tap"), 10 + 3 * (i * 4 + s) + 3)
                pe.wait_ge(sem("hy_tcopied"), 1 + i * 4 + s)
                for t in range(2):
                    m = nc.tensor.transpose(bank[4 + s][:, t * P:(t + 1) * P], hacc[:, s, t * P:(t + 1) * P], const("ident"))
                m.then_inc(sem("hy_turned"), 1)

            with pe.Fori(0, 8) as i:
                hy_project(i, 0)
                hy_project(i, 1)
                hy_turn(i, 0)
                hy_project(i, 2)
                hy_turn(i, 1)
                hy_project(i, 3)
                hy_turn(i, 2)
                hy_turn(i, 3)
            with pe.Fori(8, 12) as i:
                for s in range(4):
                    hy_project(i, s)
            pe.wait_ge(sem("hyf_in"), 64)
            pe.wait_ge(sem("hy_evac"), 4 + 48)
            mm(bank[0][0:CH, 0:SEQ], fw1[0:33, :], zT[0:33, :], start=True, stop=True).then_inc(sem("hid_mm"), 1)
            pe.wait_ge(sem("hid_done"), 1)
            mm(bank[1][0:CH, 0:SEQ], fw2[0:CH, :], hid1[0:CH, :], start=True, stop=True).then_inc(sem("hid_mm"), 1)
            pe.wait_ge(sem("hid_done"), 3)
            pe.wait_ge(sem("hy_tcopied"), 4 + 32)

            def filters(n, o):
                pe.wait_ge(sem("w3_in"), 48 * n + 48)
                for t in range(2):
                    for d in range(2):
                        m = mm(bank[4 + 2 * d + t][:, :], hid2[0:65, t * P:(t + 1) * P], w3c[0:65, 2 * d + o, :], start=True, stop=True)
                m.then_inc(sem("fil_ready"), 1)

            def convolve(n, o, last):
                c = n * 2 + o
                pe.wait_ge(sem("fil_used"), c + 2)
                for f in range(2):
                    for src, w, b in ((fa, "cos", 4), (fb, "sin", 6)):
                        for t in range(2):
                            m = mm(bank[b + f][:, :], const(w)[:, t * SEQ + f * P:t * SEQ + (f + 1) * P], src[:, t, :],
                                   start=(t == 0), stop=(t == 1))
                    m.then_inc(sem("spec_ready"), 1)
                pe.wait_ge(sem("inv_used"), n * 6 + (1 + 2 * o))
                for f in range(2):
                    for w, b in (("cos", 0), ("sin", 2)):
                        for t in range(2):
                            rhs = yb[:, t, :] if o else uv[:, t, bass.ds(n * N1, N1)]
                            m = mm(bank[b + f][:, :], const(w)[:, t * SEQ + f * P:t * SEQ + (f + 1) * P], rhs,
                                   start=(t == 0), stop=(t == 1))
                    m.then_inc(sem("sig_ready"), 1)
                if not last:
                    pe.wait_ge(sem("spec_copied"), c * 4 + 4)
                    filters(n + o, 1 - o)
                pe.wait_ge(sem("prod_done"), c * 12 + 13)
                if o == 0:
                    for t in range(2):
                        for e, (y, w) in enumerate(((Yr, "icos"), (Yi, "isin"))):
                            for f in range(2):
                                m = mm(bank[t][:, :], const(w)[:, f * SEQ + t * P:f * SEQ + (t + 1) * P], y[:, f, :],
                                       start=(e == 0 and f == 0), stop=(e == 1 and f == 1))
                        m.then_inc(sem("inv_ready"), 1)
                else:
                    for b in range(4):
                        for e, (y, w) in enumerate(((Yr, "icos"), (Yi, "isin"))):
                            for f in range(2):
                                m = mm(bank[b][:, 0:SEQ], y[:, f, b * P:(b + 1) * P], const(w)[:, f * SEQ:(f + 1) * SEQ],
                                       start=(e == 0 and f == 0), stop=(e == 1 and f == 1))
                        m.then_inc(sem("inv_ready"), 1)

            filters(0, 0)
            with pe.Fori(0, 3) as n:
                convolve(n, 0, False)
                convolve(n, 1, False)
            convolve(3, 0, False)
            convolve(3, 1, True)
            pe.wait_ge(sem("inv_used"), 25)
            with pe.Fori(0, 2) as i:
                for r in range(2):
                    grp = i * 2 + r
                    pe.wait_ge(sem(f"rec_in{r}"), 320 * i + 320)
                    kT = lambda u, c: recs[:, 4 * r + u, c:c + CH]
                    qT = lambda u, c: recs[:, 4 * r + u, 512 + c:512 + c + CH]
                    for g in range(8):
                        q, s = g // 4, g % 4
                        t = (0, 1, 1, 0)[s]
                        T = 2 * (1 - q) + t
                        hf = ((0, 1), (1, 0))[s // 2]
                        for u in range(4):
                            A = bank[2 * u]
                            if g == 0:
                                pe.wait_ge(sem("state_zero"), grp + 1)
                            else:
                                pe.wait_ge(sem("state_done"), grp * 56 + ((g - 1) * 8 + 2 * u + 2))
                            for d in range(2):
                                m = mm(A[HF[hf[d]], 0:P], kT(u, T * P + hf[d] * CH), state[:, 2 * u + d, :], start=True, stop=True)
                            if q:
                                for d in range(2):
                                    m = mm(A[HF[hf[d]], P:2 * P], qT(u, t * P + hf[d] * CH), state[:, 2 * u + d, :], start=True, stop=True)
                            m.then_inc(sem("ks_ready"), 1)
                        for u in range(4):
                            pe.wait_ge(sem("r_done"), grp * 32 + (g * 4 + u + 1))
                            pe.sem_inc(sem("pe_passed"), 1)
                            for d in range(2):
                                hh = HF[hf[d]]
                                m = mm(bank[2 * u + 1][hh, 0:P], invs[hh, 4 * r + u, 1 - q, d, t, :], r_in[hh, u, :],
                                       start=True, stop=True)
                            m.then_inc(sem("vn_ready"), 1)
                        for u in range(4):
                            if q:
                                pe.wait_ge(sem("vn_done"), grp * 16 + ((g - 4) * 4 + u + 1))
                                pe.sem_inc(sem("pe_passed"), 1)
                                for d in range(2):
                                    hh = HF[hf[d]]
                                    at = recs[hh, 4 * r + u, 1792 + (2 * d + t) * CH:1792 + (2 * d + t + 1) * CH]
                                    m = mm(bank[2 * u + 1][hh, P:2 * P], at, v_new[hh, u, :], start=True, stop=True)
                                m.then_inc(sem("av_ready"), 1)
                        for u in range(4):
                            if g < 7:
                                if q:
                                    pe.wait_ge(sem("o_added"), grp * 32 + ((g - 4) * 8 + u + 1))
                                    pe.wait_ge(sem("av_ready"), grp * 16 + ((g - 4) * 4 + u + 1))
                                pe.wait_ge(sem("vtail_done"), grp * 28 + (g * 4 + u + 1))
                                for d in range(2):
                                    hh = HF[hf[d]]
                                    k_tok = recs[hh, 4 * r + u, 768 + T * P:768 + (T + 1) * P]
                                    m = mm(bank[2 * u + d][:, (2 + d) * P:(3 + d) * P], k_tok, v_tail[hh, u, :], start=True, stop=True)
                                m.then_inc(sem("upd_ready"), 1)
                    for u in range(4):
                        pe.wait_ge(sem("o_normed"), grp * 8 + (2 * u + 2))
                        for t in range(2):
                            m = nc.tensor.transpose(bank[2 * u + 1][:, (2 + t) * P:(3 + t) * P], o_acc[:, 2 * u + t, :], const("ident"))
                        m.then_inc(sem("o_turned"), 1)
            pe.wait_ge(sem("mods_diag"), 16)
            pe.wait_ge(sem("o_merged"), 5 + 16)
            with pe.Fori(0, 4) as i:
                for j in range(4):
                    pe.wait_ge(sem("mods_done"), 1 + i * 4 + j)
                    mm(bank[4 + j][:, :], const("ones"), mods.rearrange("p s n -> p (s n)")[:, bass.ds(i * D + j * N1, N1)],
                       start=True, stop=True).then_inc(sem("mods_mm"), 1)
            pe.wait_ge(sem("mods_done"), 4 + 16)
            pe.sem_inc(sem("br_proj"), 4)
            pe.wait_ge(sem("o_merged"), 5 + 16)
            with pe.Fori(0, 8) as i:
                for s in range(4):
                    weights_in(s, i + 24)
                    pe.wait_ge(sem("br_used"), 1 + i * 4 + s)
                    wide(s, s, (zsT, yhT)[s % 2]).then_inc(sem("br_proj"), 1)
            pe.sem_inc(sem("wo_used"), 2)
            pe.wait_ge(sem("merged"), 16)
            with pe.Fori(0, 4) as i:
                for s in range(2):
                    pe.wait_ge(sem(f"wo_in{s}"), i * 16 + 16)
                    if s == 0:
                        pe.wait_ge(sem("mix_added"), 1 + 2 * i)
                    for t in range(2):
                        for k in range(8):
                            m = mm(bank[4 + t][:, :], gT[:, s * 8 + k, t * P:(t + 1) * P], wo_ring[:, s, k, :],
                                   start=(s == 0 and k == 0), stop=(s == 1 and k == 7))
                    m.then_inc(sem("wo_used"), 1)
            pe.sem_inc(sem("q_proj"), 4)
            for t in range(2):
                pe.wait_ge(sem("h2_done"), t + 1)
                for kq in range(4):
                    b = 4 * t + kq
                    for j in range(4):
                        k = 4 * kq + j
                        m = nc.tensor.transpose(bank[b][:, j * P:(j + 1) * P], h2[:, t, k * P:(k + 1) * P], const("ident"))
                    m.then_inc(sem("h2_turned"), 1)
            pe.wait_ge(sem("h2T_done"), 8)
            pe.wait_ge(sem("subk_in"), 16)
            with pe.Fori(0, 4) as i:
                for s in range(4):
                    weights_in(s, i + 32)
                    wide(s, s, h2T).then_inc(sem("q_proj"), 1)
                for s in range(4):
                    pe.wait_ge(sem("q_copied"), i * 4 + s + 1)
                    pe.wait_ge(sem("sc_copied"), 1 + i * 4)
                    for t in range(2):
                        m = mm(bank[4 + s][:, t * P:(t + 1) * P], q_sb[:, s, t * P:(t + 1) * P], subk[:, bass.ds(i * 4 + s, 1), :].rearrange("p o n -> p (o n)"), start=True, stop=True)
                    m.then_inc(sem("sc_ready"), 1)

        @block.scalar
        def _(act):
            af = nc.scalar.activation
            for name in ("rooted", "k_copied", "sc_copied"):
                act.sem_inc(sem(name), 1)
            act.wait_ge(sem("cond_in"), 16)
            af(cond, cond, ACT.Silu).then_inc(sem("cond_done"), 1)
            act.wait_ge(sem("gating_step"), 1)
            for d in range(2):
                v = ab.rearrange("p t (d k h) -> p t d k h", d=2, k=2)
                m = af(beta[:, :, d * H:(d + 1) * H], v[:, :, d, 1, :], ACT.Sigmoid)
            m.then_inc(sem("beta_done"), 1)
            act.wait_ge(sem("gating_step"), 3)
            af(sp_e, xs, ACT.Abs).then_inc(sem("sp_act"), 1)
            act.wait_ge(sem("sp_act"), 1)
            af(sp_e, sp_e, ACT.Exp, scale=-1.0).then_inc(sem("sp_act"), 1)
            act.wait_ge(sem("sp_act"), 2)
            af(sp_e, sp_e, ACT.Ln, bias=1.0).then_inc(sem("sp_act"), 1)
            act.wait_ge(sem("gate_in"), 32)
            af(gate_row[:, 0, :], gate_row[:, 0, :], ACT.Exp).then_inc(sem("alog_done"), 1)
            def z_evac(i):
                for s in range(4):
                    act.wait_ge(sem("zg_proj"), 4 + i * 4 + s + 1)
                    af(zsT[:, i * 4 + s, :], bank[0 if s % 2 else 3][:, 0:SEQ], ACT.Silu).then_inc(sem("zg_evac"), 1)

            act.wait_ge(sem("badac_in"), 32)
            af(cond_row, cond_row, ACT.Silu).then_inc(sem("condrow_done"), 1)
            act.sem_inc(sem("zg_evac"), 4)
            z_evac(0)
            act.wait_ge(sem("gating_step"), 10)
            af(etail, etail, ACT.Exp)
            af(eg, gcum, ACT.Exp)
            af(etot, etot, ACT.Exp).then_inc(sem("eg_done"), 1)
            for t in range(4):
                lat = t < 2
                act.wait_ge(sem("xmask_done"), t + 1)
                af(n_e1f[:, t], xm[:, 0:H, :], ACT.Exp, scale=-1.0)
                if lat:
                    af(a_e2f[:, t], xm2, ACT.Exp)
                    af(a_eb[:, t], xm[:, H:HD, :], ACT.Exp)
                af(n_eb[:, t], xm[:, H:HD, :], ACT.Exp).then_inc(sem("exp_done"), 1)
                if t != 2:
                    z_evac((1, 2, None, 3)[t])

            def evac(h, t):
                act.wait_ge(sem("proj"), 3 + 3 * h + t + 1)
                act.wait_ge(sem("tap"), 25 * h)
                m = af(c_lat[t][:, :, 2:2 + CH], bank[t][:, 0:SEQ].rearrange("p (r w) -> p r w", r=NCH), ACT.Copy)
                if t:
                    m = af(c_ctx[t][:, 2:2 + SEQ], bank[t][:, SEQ:TOK], ACT.Copy)
                m.then_inc(sem("proj_copied"), 1)

            def silu(h, t):
                act.wait_ge(sem("tap"), 25 * h + (5, 15, 25)[t])
                ns = 1 if t == 0 else 2
                src = acc[:, t, 0:ns * SEQ].rearrange("p (s c n) -> p s c n", s=ns, c=NCH)
                dst = raw[:, t, 0:ns * SEQ].rearrange("p (s c n) -> p s c n", s=ns, c=NCH)
                af(dst[:, :, 0:2, :], src[:, :, 0::3, :], ACT.Silu)
                af(dst[:, :, 2:4, :], src[:, :, 1:3, :], ACT.Silu).then_inc(sem("silued"), 1)
                if t < 2:
                    act.wait_ge(sem("silued"), 3 * h + t + 1)
                    af(sq[:, t, 0:ns * SEQ], raw[:, t, 0:ns * SEQ], ACT.Square).then_inc(sem("squared"), 1)

            def roots(h):
                for j, n in ((0, SEQ), (1, TOK)):
                    act.wait_ge(sem("ssq"), 2 * h + j + 1)
                    act.wait_ge(sem("normed"), 1 + 2 * h)
                    af(nrm[:, j, 0:n], (bank[3] if j == 0 else bank[7])[:, 0:n], ACT.Sqrt, bias=eps6[:, 0:1]
                       ).then_inc(sem("rooted"), 1)

            def copy_k(h):
                act.wait_ge(sem("k_turned"), h + 1)
                act.wait_ge(sem("stored"), h + 1)
                af(r_k, bank[4][:, :], ACT.Copy).then_inc(sem("k_copied"), 1)

            act.sem_inc(sem("proj_copied"), 2)
            act.wait_ge(sem("decay_done"), 1)
            for t in range(3):
                evac(0, t)
                silu(0, t)
            with act.Fori(1, H) as h:
                evac(h, 0)
                roots(h - 1)
                act.wait_ge(sem("normed"), 1 + 2 * h)
                silu(h, 0)
                evac(h, 1)
                silu(h, 1)
                evac(h, 2)
                copy_k(h - 1)
                act.wait_ge(sem("v_turned"), h)
                silu(h, 2)
            roots(H - 1)
            copy_k(H - 1)
            act.wait_ge(sem("gram_used"), 1 + 4 * H)

            def zg(i, s, func, dst):
                act.wait_ge(sem("zg_proj"), 4 + i * 4 + s + 1)
                af(dst, bank[7 if s == 3 else s][:, 0:SEQ].unsqueeze(1), func).then_inc(sem("zg_evac"), 1)

            with act.Fori(4, 12) as i:
                for s in range(4):
                    zg(i, s, ACT.Sigmoid, gT[:, bass.ds(i * 4 + (s - 16), 1), :])
            act.sem_inc(sem("hy_evac"), 4)
            act.sem_inc(sem("hy_tcopied"), 4)
            act.wait_ge(sem("hpads"), 1)
            act.wait_ge(sem("inv_out"), 32)

            def hy_evac(i, s):
                act.wait_ge(sem("hy_proj"), 4 + i * 4 + s + 1)
                act.wait_ge(sem("hy_tap"), 1 + 3 * (i * 4 + s))
                af(hbuf[:, s, :, 1:1 + CH], bank[s][:, 0:SEQ].rearrange("p (r w) -> p r w", r=NCH), ACT.Copy
                   ).then_inc(sem("hy_evac"), 1)

            def hy_tcopy(i, s):
                act.wait_ge(sem("hy_turned"), 4 + i * 4 + s + 1)
                af(uv[:, :, bass.ds((i * 4 + s) * P, P)], bank[4 + s][:, 0:2 * P].rearrange("p (t n) -> p t n", t=2), ACT.Copy
                   ).then_inc(sem("hy_tcopied"), 1)

            with act.Fori(0, 8) as i:
                hy_evac(i, 0)
                hy_evac(i, 1)
                hy_tcopy(i, 0)
                hy_evac(i, 2)
                hy_tcopy(i, 1)
                hy_evac(i, 3)
                hy_tcopy(i, 2)
                hy_tcopy(i, 3)
            with act.Fori(8, 12) as i:
                for s in range(4):
                    hy_evac(i, s)
            for n, hid in enumerate((hid1, hid2)):
                act.wait_ge(sem("ang_done"), 6 * n + 6)
                af(hid[0:CH, :], ang[0:CH, :], ACT.Sin).then_inc(sem("hid_done"), 1)
            with act.Fori(0, 4) as n:
                for o in range(2):
                    for f in range(2):
                        act.wait_ge(sem("spec_ready"), n * 4 + (2 * o + f + 1))
                        act.wait_ge(sem("prod_done"), n * 24 + (1 + 12 * o))
                        af(Fr[:, f, :], bank[4 + f][:, :], ACT.Copy).then_inc(sem("spec_copied"), 1)
                        af(Fi[:, f, :], bank[6 + f][:, :], ACT.Copy).then_inc(sem("spec_copied"), 1)
            with act.Fori(0, 2) as i:
                for r in range(2):
                    grp = i * 2 + r
                    for g in range(8):
                        q, s = g // 4, g % 4
                        T = 2 * (1 - q) + (0, 1, 1, 0)[s]
                        for u in range(4):
                            h = i * 8 + (4 * r + u)
                            B = bank[2 * u + 1][:, 0:P]
                            act.wait_ge(sem("vn_ready"), grp * 32 + (g * 4 + u + 1))
                            if g < 7:
                                af(v_tail[:, u, :], B, ACT.Copy, scale=mixed[:, 4 + s // 2, T, bass.ds(h, 1)]
                                   ).then_inc(sem("vtail_done"), 1)
                            if q:
                                af(v_new[:, u, :], B, ACT.Copy).then_inc(sem("vn_done"), 1)
                    for u in range(4):
                        act.wait_ge(sem("o_added"), grp * 32 + (24 + 4 + u + 1))
                        for t in range(2):
                            af(o_sq, o_acc[:, 2 * u + t, :], ACT.Square, accum_out=o_ss[:, 2 * u + t:2 * u + t + 1]
                               ).then_inc(sem("o_ss"), 1)
                            act.wait_ge(sem("o_ss"), grp * 9 + (2 * u + t + 1))
                    af(o_ss, o_ss, ACT.Sqrt, bias=eps6[:, 0:1], scale=1.0 / DK).then_inc(sem("o_ss"), 1)
            act.sem_inc(sem("mods_done"), 4)
            with act.Fori(0, 4) as i:
                for j in range(4):
                    act.wait_ge(sem("mods_mm"), i * 4 + (j + 1))
                    af(mods.rearrange("p s n -> p (s n)")[:, bass.ds(i * D + j * N1, N1)], bank[4 + j][:, :], ACT.Copy
                       ).then_inc(sem("mods_done"), 1)
            for t in range(2):
                act.wait_ge(sem("var_done"), t + 1)
                af(rstd[:, t:t + 1], aggr[:, t, 1:2], ACT.Sqrt, bias=eps5[:, 0:1]).then_inc(sem("std_done"), 1)
            for t in range(2):
                for kq in range(4):
                    act.wait_ge(sem("h2_turned"), 4 * t + kq + 1)
                    if t + kq == 0:
                        act.wait_ge(sem("wo_used"), 2 + 8)
                    af(h2T[:, 4 * kq:4 * kq + 4, t * P:(t + 1) * P], bank[4 * t + kq][:, :].rearrange("p (k n) -> p k n", k=4), ACT.Copy
                       ).then_inc(sem("h2T_done"), 1)
            with act.Fori(0, 4) as i:
                for s in range(4):
                    act.wait_ge(sem("q_proj"), 4 + i * 4 + s + 1)
                    af(q_sb[:, s, :], bank[s][:, 0:SEQ], ACT.Copy).then_inc(sem("q_copied"), 1)
                for s in range(4):
                    act.wait_ge(sem("sc_ready"), i * 4 + s + 1)
                    af(sc[:, :, bass.ds(i * 4 + s, 1), :], bank[4 + s][:, 0:2 * P].rearrange("p (t o n) -> p t o n", t=2, o=1), ACT.Copy
                       ).then_inc(sem("sc_copied"), 1)

            def exps(t):
                act.wait_ge(sem("bdiff"), t + 1)
                af(gate[:, t, :], gate[:, t, :], ACT.Exp).then_inc(sem("bexp"), 1)

            def gelus(t, b, n):
                act.wait_ge(sem("ring_used"), n + (7 + t * 256))
                act.wait_ge(sem("coef_done"), b + t * PH)
                af(gelu, dots, ACT.Gelu).then_inc(sem("gelu_done"), 1)

            exps(0)
            gelus(0, 0, 16)
            gelus(0, 1, 32)
            exps(1)
            with act.Fori(2, PH) as b:
                gelus(0, b, b * 32)
            gelus(1, 0, 0)
            with act.Fori(1, PH) as b:
                gelus(1, b, b * 32)
            for t in range(2):
                act.wait_ge(sem("var_done"), t + 3)
                af(rstd[:, t:t + 1], aggr[:, t, 1:2], ACT.Sqrt, bias=eps5[:, 0:1]).then_inc(sem("std_done"), 1)

        @block.vector
        def _(dve):
            v = nc.vector
            tt, stt, ts = v.tensor_tensor, v.scalar_tensor_tensor, v.tensor_scalar
            for name in ("v_copied", "gram_used", "fil_used", "normed", "inv_used", "prod_done", "mix_added"):
                dve.sem_inc(sem(name), 1)
            v.memset(eps6, 1e-6)
            v.memset(eps5, 1e-5)
            dve.sem_inc(sem("cols_done"), 1)
            dve.sem_inc(sem("row_done"), 2)
            dve.wait_ge(sem("bada_in"), 16)
            dve.wait_ge(sem("x_in"), 16)

            def ada_bias(i):
                for w in range(2):
                    dve.wait_ge(sem("ada_used"), i * 4 + 2 * w + 2)
                    r = ada_row[0:2, i, w, :]
                    tt(r, bank[w][0:2, :], r, ALU.add).then_inc(sem("row_done"), 1)

            def modulate(i):
                dve.wait_ge(sem("cols_ready"), i + 1)
                c4 = cols[:, 4 * i:4 * i + 4]
                v4 = bank[2][:, 0:16].rearrange("p (k w s) -> p k w s", k=4, w=2)
                v.tensor_copy(c4[:, :, 0, :], v4[:, :, 0, :])
                ts(c4[:, :, 1, :], v4[:, :, 1, :], 1.0, None, ALU.add).then_inc(sem("cols_done"), 1)
                dve.wait_ge(sem("cols_done"), 1 + i + 1)
                for k in range(4 * i, 4 * i + 4):
                    for s in range(2):
                        x = hT[:, k, s * SEQ:(s + 1) * SEQ]
                        ts(x, x, cols[:, k, 1, s:s + 1], cols[:, k, 0, s:s + 1], ALU.mult, ALU.add
                           ).then_inc(sem("h_done"), 1)

            ada_bias(0)
            for i in range(1, 4):
                ada_bias(i)
                modulate(i - 1)
            modulate(3)
            dve.wait_ge(sem("abT_ready"), 1)
            v.tensor_copy(abT[0:CH, :], bank[0][0:CH, :]).then_inc(sem("abT_copied"), 1)
            dve.wait_ge(sem("gating_mm"), 1)
            v.tensor_copy(ab, bank[1][:, 0:256].rearrange("p (t n) -> p t n", t=4)).then_inc(sem("gating_step"), 1)
            dve.wait_ge(sem("gating_step"), 1)
            dve.wait_ge(sem("gate_in"), 32)
            abv = ab.rearrange("p t (d k h) -> p t d k h", d=2, k=2)
            for d in range(2):
                tt(xs[:, :, d * H:(d + 1) * H], abv[:, :, d, 0, :],
                   gate_row[:, 1, d * H:(d + 1) * H].unsqueeze(1).broadcast_to([P, 4, H]), ALU.add
                   ).then_inc(sem("gating_step"), 1)
            dve.wait_ge(sem("gating_step"), 3)
            ts(sp_m, xs, 0.0, None, ALU.max).then_inc(sem("gating_step"), 1)
            dve.wait_ge(sem("gating_step"), 4)
            dve.wait_ge(sem("sp_act"), 3)
            tt(sp_m, sp_m, sp_e, ALU.add).then_inc(sem("gating_step"), 1)
            dve.wait_ge(sem("gating_step"), 5)
            dve.wait_ge(sem("alog_done"), 1)
            stt(g_tok, sp_m, -1.0, gate_row[:, 0, :].unsqueeze(1).broadcast_to([P, 4, HD]), ALU.mult, ALU.mult
                ).then_inc(sem("gating_step"), 1)
            dve.wait_ge(sem("gating_mm"), 2)
            v.tensor_copy(xm.rearrange("p h i -> p (h i)")[0:HD, 0:512], bank[4][0:HD, :]).then_inc(sem("gating_step"), 1)
            dve.wait_ge(sem("gating_mm"), 3)
            v.tensor_copy(gcum, bank[1][:, 0:128].rearrange("p (t h) -> p t h", t=4)).then_inc(sem("gating_step"), 1)
            dve.wait_ge(sem("gating_mm"), 4)
            dve.wait_ge(sem("gating_step"), 8)
            tt(etail, bank[2][:, 0:128].rearrange("p (t h) -> p t h", t=4), gcum, ALU.subtract).then_inc(sem("gating_step"), 1)
            v.tensor_copy(etot, bank[2][:, 128:384].rearrange("p (u n) -> p u n", u=2)).then_inc(sem("gating_step"), 1)
            dve.wait_ge(sem("eg_done"), 1)
            ts(neg_eg, eg, -1.0, None, ALU.mult)
            dve.wait_ge(sem("gating_step"), 6)
            dve.wait_ge(sem("beta_out"), 32)
            for t in range(4):
                if t:
                    dve.wait_ge(sem("gb_ready"), t)
                for d, tri in ((0, "tri_f"), (1, "tri_b")):
                    m = tt(gx[:, d * H:(d + 1) * H, :],
                           g_tok[:, t, d * H:(d + 1) * H].unsqueeze(2).broadcast_to([P, H, CH]),
                           const(tri).unsqueeze(1).broadcast_to([P, H, CH]), ALU.mult)
                m.then_inc(sem("gx_done"), 1)
                dve.wait_ge(sem("gb_ready"), t + 1)
                if t:
                    dve.wait_ge(sem("exp_done"), t)
                for b in range(4):
                    m = tt(xm[:, 8 * b:8 * b + 8, :], bank[4 + b][:, :].rearrange("p (h i) -> p h i", h=8),
                           gcum[:, t, 8 * b:8 * b + 8].unsqueeze(2).broadcast_to([P, 8, CH]), ALU.subtract)
                    m.then_inc(sem("xm_done"), 1)
                dve.wait_ge(sem("xm_done"), 4 * t + 4)
                up = const("mask_above").unsqueeze(1).broadcast_to([P, H, CH])
                dn = const("mask_below").unsqueeze(1).broadcast_to([P, H, CH])
                if t < 2:
                    tt(xm2, xm[:, 0:H, :], dn, ALU.subtract).then_inc(sem("xm2_done"), 1)
                    dve.wait_ge(sem("xm2_done"), t + 1)
                tt(xm[:, 0:H, :], xm[:, 0:H, :], up, ALU.add)
                tt(xm[:, H:HD, :], xm[:, H:HD, :], up, ALU.subtract).then_inc(sem("xmask_done"), 1)
                dve.wait_ge(sem("exp_done"), t + 1)
                for d, e in ((0, n_e1f), (1, n_eb)):
                    m = stt(e[:, t], e[:, t], -1.0,
                            beta[:, t, d * H:(d + 1) * H].unsqueeze(2).broadcast_to([P, H, CH]), ALU.mult, ALU.mult)
                m.then_inc(sem("nbeta_done"), 1)
            dve.wait_ge(sem("nbeta_done"), 4)
            v.memset(cbuf, 0.0).then_inc(sem("decay_done"), 1)

            def conv(h, t):
                base = 25 * h + (0, 5, 15)[t]
                w = lambda j: dnc[:, bass.ds(3 * h + t, 1), j]
                a_lat = acc[:, t, 0:SEQ].rearrange("p (r w) -> p r w", r=NCH)
                a_ctx = acc[:, t, SEQ:TOK]
                dve.wait_ge(sem("proj_copied"), 2 + 3 * h + t + 1)
                dve.wait_ge(sem("silued"), 3 * h)
                per = 1 if t == 0 else 2
                for j in range(TAPS):
                    if j:
                        dve.wait_ge(sem("tap"), base + per * (j - 1) + 1)
                    x = c_lat[t][:, :, j:j + CH]
                    if j == 0:
                        ts(a_lat, x, w(j), None, ALU.mult).then_inc(sem("tap"), 1)
                    else:
                        stt(a_lat, x, w(j), a_lat, ALU.mult, ALU.add).then_inc(sem("tap"), 1)
                    if t:
                        if j:
                            dve.wait_ge(sem("tap"), base + per * j)
                        x = c_ctx[t][:, j:j + SEQ]
                        if j == 0:
                            ts(a_ctx, x, w(j), None, ALU.mult).then_inc(sem("tap"), 1)
                        else:
                            stt(a_ctx, x, w(j), a_ctx, ALU.mult, ALU.add).then_inc(sem("tap"), 1)

            def ada_tile(h, e):
                dve.wait_ge(sem("ada_tile_in"), h * 64 + (16 * e + 16))
                dve.wait_ge(sem("ada2_used"), h * 4 + (e + 1))
                v.tensor_tensor_reduce(ada_junk, wring[:, 3].rearrange("p k n -> p (k n)"), cond_row, 1.0, 0.0, ALU.mult, ALU.add,
                                       ada_dot[:, e:e + 1]).then_inc(sem("ada2_used"), 1)

            def ada_bias2(h):
                dve.wait_ge(sem("ada2_used"), h * 4 + (1 + 4))
                x = badac[:, bass.ds(h * 4, 4)]
                tt(adac[:, bass.ds(h * 4, 4)], ada_dot, x, ALU.add).then_inc(sem("adac_done"), 1)
                dve.wait_ge(sem("adac_done"), h + 1)

            def normalize(h):
                for j, n in ((0, SEQ), (1, TOK)):
                    dve.wait_ge(sem("rooted"), 1 + 2 * h + j + 1)
                    v.reciprocal(nrm[:, j, 0:n], nrm[:, j, 0:n]).then_inc(sem("recip"), 1)
                dve.wait_ge(sem("stored"), h + 1)
                dve.wait_ge(sem("recip"), 2 * h + 1)
                stt(r_qT, raw[:, 0, 0:SEQ], DK ** -0.5, nrm[:, 0, 0:SEQ], ALU.mult, ALU.mult).then_inc(sem("normed"), 1)
                dve.wait_ge(sem("recip"), 2 * h + 2)
                tt(r_kT, raw[:, 1, :], nrm[:, 1, :], ALU.mult).then_inc(sem("normed"), 1)

            def finish(h):
                dve.wait_ge(sem("v_turned"), h + 1)
                v.tensor_copy(r_v, bank[5][:, :]).then_inc(sem("v_copied"), 1)
                dve.wait_ge(sem("gram"), h + 1)
                dve.wait_ge(sem("stored"), h + 1)
                g = bank[6][:, 0:256].rearrange("p (t o i) -> p t o i", t=4, o=1)
                q = bank[6][:, 256:384].rearrange("p (t o i) -> p t o i", t=2, o=1)
                for d, e in ((0, n_e1f), (1, n_eb)):
                    tt(mt[:, d].unsqueeze(2), g, e[:, :, bass.ds(h, 1), :], ALU.mult).then_inc(sem("gram_used"), 1)
                for d, e in ((0, a_e2f), (1, a_eb)):
                    tt(r_at[:, d].unsqueeze(2), q, e[:, :, bass.ds(h, 1), :], ALU.mult).then_inc(sem("gram_used"), 1)

            dve.wait_ge(sem("dnc_in"), 16)
            dve.wait_ge(sem("condrow_done"), 1)
            dve.sem_inc(sem("ada2_used"), 1)
            for t in range(3):
                conv(0, t)
                ada_tile(0, t)
            ada_tile(0, 3)
            ada_bias2(0)
            with dve.Fori(1, H) as h:
                conv(h, 0)
                normalize(h - 1)
                ada_tile(h, 0)
                conv(h, 1)
                ada_tile(h, 1)
                conv(h, 2)
                ada_tile(h, 2)
                finish(h - 1)
                ada_tile(h, 3)
                ada_bias2(h)
            normalize(H - 1)
            finish(H - 1)
            for m_, x in enumerate((neg_eg, eg, etail)):
                for w_ in range(2):
                    for half in range(2):
                        d = half ^ w_
                        k_ = v.tensor_copy(mixed[HF[half], 2 * m_ + w_], x[HF[half], :, d * H:(d + 1) * H])
            k_.then_inc(sem("mixed_done"), 1)
            with dve.Fori(0, 2) as n:
                dve.wait_ge(sem("mix_in"), 32 * n + 32)
                for j in range(1, CH - 1):
                    rows = CH - 1 - j
                    tmp = sol_t[:, 0:rows * j].rearrange("p (i c) -> p i c", c=j)
                    if j > 1:
                        dve.wait_ge(sem("solve_step"), n * 124 + 2 * (j - 1))
                    tt(tmp, sol[:, j + 1:CH, j:j + 1].broadcast_to([P, rows, j]), sol[:, j:j + 1, 0:j].broadcast_to([P, rows, j]),
                       ALU.mult).then_inc(sem("solve_step"), 1)
                    dve.wait_ge(sem("solve_step"), n * 124 + 2 * (j - 1) + 1)
                    tt(sol[:, j + 1:CH, 0:j], sol[:, j + 1:CH, 0:j], tmp, ALU.add).then_inc(sem("solve_step"), 1)
                dve.wait_ge(sem("solve_step"), n * 124 + 124)
                v.memset(sol.rearrange("p a b -> p (a b)")[:, 0:CH * CH:CH + 1], 1.0).then_inc(sem("sol_diag"), 1)
                dve.wait_ge(sem("sol_diag"), n + 1)
                dve.wait_ge(sem("inv_stored"), n + 1)
                lo, hi = HF
                tt(sol_o[lo], sol[lo].rearrange("p r c -> p c r"), sol_b[lo].unsqueeze(2).broadcast_to([CH, CH, CH]), ALU.mult)
                tt(sol_o[hi], sol[hi], sol_b[hi].unsqueeze(1).broadcast_to([CH, CH, CH]), ALU.mult).then_inc(sem("solved"), 1)
            v.memset(hbuf, 0.0).then_inc(sem("hpads"), 1)
            dve.sem_inc(sem("hy_tap"), 10)
            dve.wait_ge(sem("hyc_in"), 32)

            def hconv(i, s, turned):
                m = i * 4 + s
                w = lambda j: hyc[:, bass.ds(m, 1), j]
                dve.wait_ge(sem("hy_evac"), 4 + m + 1)
                if turned:
                    dve.wait_ge(sem("hy_turned"), 1 + m)
                    o_ = hacc[:, s, :].rearrange("p (r w) -> p r w", r=NCH)
                else:
                    o_ = yhT[:, bass.ds(m - 32, 1), :].rearrange("p o (r w) -> p (o r) w", r=NCH)
                for j in range(HTAPS):
                    if j:
                        dve.wait_ge(sem("hy_tap"), 10 + 3 * m + j)
                    x = hbuf[:, s, :, j:j + CH]
                    if j == 0:
                        ts(o_, x, w(j), None, ALU.mult).then_inc(sem("hy_tap"), 1)
                    else:
                        stt(o_, x, w(j), o_, ALU.mult, ALU.add).then_inc(sem("hy_tap"), 1)

            with dve.Fori(0, 8) as i:
                for s in range(4):
                    hconv(i, s, True)
            with dve.Fori(8, 12) as i:
                for s in range(4):
                    hconv(i, s, False)
            MAGIC, TWO_PI = 12582912.0, 6.283185307179586
            T_HI = float(np.float32(6.28125))
            T_MID = float(np.float32(TWO_PI - T_HI))
            T_LO = TWO_PI - T_HI - T_MID
            dve.wait_ge(sem("hyf_in"), 64)
            for n, b in enumerate((0, 1)):
                dve.wait_ge(sem("hid_mm"), n + 1)
                A_, W_ = ang[0:CH, :], turns[0:CH, :]
                steps = 0

                def chain(ins):
                    nonlocal steps
                    steps += 1
                    ins.then_inc(sem("ang_done"), 1)
                    dve.wait_ge(sem("ang_done"), 6 * n + steps)

                chain(ts(A_, bank[b][0:CH, 0:SEQ], fcol[0:CH, n:n + 1], fcol[0:CH, 2:3], ALU.add, ALU.mult))
                chain(ts(W_, A_, 1.0 / TWO_PI, MAGIC, ALU.mult, ALU.add))
                chain(ts(W_, W_, -MAGIC, None, ALU.add))
                chain(stt(A_, W_, -T_HI, A_, ALU.mult, ALU.add))
                chain(stt(A_, W_, -T_MID, A_, ALU.mult, ALU.add))
                stt(A_, W_, -T_LO, A_, ALU.mult, ALU.add).then_inc(sem("ang_clip"), 1)
                dve.wait_ge(sem("ang_clip"), n + 1)
                ts(A_, A_, -3.1415925, 3.1415925, ALU.max, ALU.min).then_inc(sem("ang_done"), 1)
            v.memset(hid2[CH:CH + 1, :], 1.0).then_inc(sem("hid_done"), 1)

            def fold(n, o):
                c = n * 2 + o
                dve.wait_ge(sem("fil_ready"), c + 1)
                dve.wait_ge(sem("w3_in"), 48 * n + 48)
                for t in range(2):
                    tt(t1[:, t, :], bank[4 + t][:, :], win[:, t, :], ALU.mult).then_inc(sem("fstep"), 1)
                    if t == 0:
                        stt(t2[:, t, :], bank[6 + t][:, :], const("not_first"), win[:, t, :], ALU.mult, ALU.mult).then_inc(sem("fstep"), 1)
                    else:
                        tt(t2[:, t, :], bank[6 + t][:, :], win[:, t, :], ALU.mult).then_inc(sem("fstep"), 1)
                for t in range(2):
                    dve.wait_ge(sem("fstep"), c * 6 + (2 * t + 2))
                    tt(fa[:, t, :], t1[:, t, :], t2[:, t, :], ALU.add).then_inc(sem("fstep"), 1)
                    if t == 0:
                        dve.wait_ge(sem("fstep"), c * 6 + 5)
                        tt(fa[0:1, 0, :], fa[0:1, 0, :], skipc[0:1, o, :], ALU.add)
                    m = tt(fb[:, t, :], t1[:, t, :], t2[:, t, :], ALU.subtract)
                m.then_inc(sem("fil_used"), 1)

            def products(n, o, last):
                c = n * 2 + o
                for f in range(2):
                    dve.wait_ge(sem("sig_ready"), c * 2 + (f + 1))
                    dve.wait_ge(sem("spec_copied"), c * 4 + (2 * f + 2))
                    dve.wait_ge(sem("fil_used"), c + 2)
                    ur, ui = bank[f][:, :], bank[2 + f][:, :]
                    done = lambda k: c * 12 + (6 * f + 1 + k)
                    tt(t1[:, f, :], ur, Fr[:, f, :], ALU.mult).then_inc(sem("prod_done"), 1)
                    tt(t2[:, f, :], ui, Fi[:, f, :], ALU.mult).then_inc(sem("prod_done"), 1)
                    dve.wait_ge(sem("prod_done"), done(2))
                    tt(Yr[:, f, :], t1[:, f, :], t2[:, f, :], ALU.subtract).then_inc(sem("prod_done"), 1)
                    dve.wait_ge(sem("prod_done"), done(3))
                    tt(t1[:, f, :], ur, Fi[:, f, :], ALU.mult).then_inc(sem("prod_done"), 1)
                    tt(t2[:, f, :], ui, Fr[:, f, :], ALU.mult).then_inc(sem("prod_done"), 1)
                    dve.wait_ge(sem("prod_done"), done(5))
                    tt(Yi[:, f, :], t1[:, f, :], t2[:, f, :], ALU.add).then_inc(sem("prod_done"), 1)
                if not last:
                    dve.wait_ge(sem("prod_done"), c * 12 + 13)
                    fold(n + o, 1 - o)
                if o == 0:
                    for t in range(2):
                        dve.wait_ge(sem("inv_ready"), n * 6 + (t + 1))
                        tt(yb[:, t, :], bank[t][:, :], uv[:, t, bass.ds(n * N1 + D, N1)], ALU.mult).then_inc(sem("inv_used"), 1)
                else:
                    for b in range(4):
                        dve.wait_ge(sem("inv_ready"), n * 6 + (2 + b + 1))
                        x = yhT[:, bass.ds(n * 4 + b, 1), :]
                        tt(x, bank[b][:, 0:SEQ].unsqueeze(1), x, ALU.mult).then_inc(sem("inv_used"), 1)

            fold(0, 0)
            with dve.Fori(0, 3) as n:
                products(n, 0, False)
                products(n, 1, False)
            products(3, 0, False)
            products(3, 1, True)
            dve.sem_inc(sem("o_merged"), 5)
            dve.wait_ge(sem("mixed_done"), 1)
            with dve.Fori(0, 2) as i:
                for r in range(2):
                    grp = i * 2 + r
                    v.memset(state, 0.0).then_inc(sem("state_zero"), 1)
                    dve.wait_ge(sem(f"rec_in{r}"), 320 * i + 320)
                    for g in range(8):
                        q, s = g // 4, g % 4
                        t = (0, 1, 1, 0)[s]
                        T = 2 * (1 - q) + t
                        hf = ((0, 1), (1, 0))[s // 2]
                        for u in range(4):
                            h = i * 8 + (4 * r + u)
                            A = bank[2 * u]
                            fac = lambda kind: mixed[:, 2 * kind + s // 2, T, bass.ds(h, 1)]
                            v_tok = recs[:, 4 * r + u, 1280 + T * P:1280 + (T + 1) * P]
                            dve.wait_ge(sem("ks_ready"), grp * 32 + (g * 4 + u + 1))
                            stt(r_in[:, u, :], A[:, 0:P], fac(0), v_tok, ALU.mult, ALU.add).then_inc(sem("r_done"), 1)
                            if q:
                                oa = o_acc[:, 2 * u + t, :]
                                if s < 2:
                                    ts(oa, A[:, P:2 * P], fac(1), None, ALU.mult).then_inc(sem("o_added"), 1)
                                else:
                                    dve.wait_ge(sem("o_added"), grp * 32 + ((3 - s) * 8 + 4 + u + 1))
                                    stt(oa, A[:, P:2 * P], fac(1), oa, ALU.mult, ALU.add).then_inc(sem("o_added"), 1)
                        for u in range(4):
                            h = i * 8 + (4 * r + u)
                            if g < 7:
                                dve.wait_ge(sem("upd_ready"), grp * 28 + (g * 4 + u + 1))
                                for d in range(2):
                                    st = state[:, 2 * u + d, :]
                                    tot = etot[:, hf[d], bass.ds(h + (T * HD + d * H), 1)]
                                    stt(st, st, tot, bank[2 * u + d][:, (2 + d) * P:(3 + d) * P], ALU.mult, ALU.add).then_inc(sem("state_done"), 1)
                        if q:
                            for u in range(4):
                                oa = o_acc[:, 2 * u + t, :]
                                dve.wait_ge(sem("av_ready"), grp * 16 + ((g - 4) * 4 + u + 1))
                                if g == 7:
                                    dve.wait_ge(sem("o_added"), grp * 32 + (24 + u + 1))
                                tt(oa, bank[2 * u + 1][:, P:2 * P], oa, ALU.add).then_inc(sem("o_added"), 1)
                    dve.wait_ge(sem("o_ss"), grp * 9 + 9)
                    v.reciprocal(o_ss, o_ss).then_inc(sem("o_rstd"), 1)
                    dve.wait_ge(sem("o_rstd"), grp + 1)
                    for u in range(4):
                        for t in range(2):
                            oa = o_acc[:, 2 * u + t, :]
                            ts(oa, oa, o_ss[:, 2 * u + t:2 * u + t + 1], None, ALU.mult).then_inc(sem("o_normed"), 1)
                    for u in range(4):
                        h = i * 8 + (4 * r + u)
                        dve.wait_ge(sem("o_turned"), 1 + grp * 4 + (u + 1))
                        z_ = zsT[:, bass.ds(h, 1), :].rearrange("p o (c n) -> p (o c) n", c=NCH)
                        for t, zz in ((0, z_[:, 0::3, :]), (1, z_[:, 1:3, :])):
                            m = stt(zz, bank[2 * u + 1][:, (2 + t) * P:(3 + t) * P].rearrange("p (c n) -> p c n", c=2), dn_nw[:, 0:1], zz,
                                    ALU.mult, ALU.mult)
                        m.then_inc(sem("o_merged"), 1)
            with dve.Fori(0, 4) as i:
                for j in range(4):
                    x = mods.rearrange("p s n -> p (s n)")[:, bass.ds(i * D + j * N1, N1)].rearrange("p (k n) -> p k n", k=4)
                    tt(x, const("ident").unsqueeze(1).broadcast_to([P, 4, P]),
                       adac[:, bass.ds(i * 16 + 4 * j, 4)].unsqueeze(2).broadcast_to([P, 4, P]), ALU.mult
                       ).then_inc(sem("mods_diag"), 1)
            dve.sem_inc(sem("br_used"), 4)
            with dve.Fori(0, 8) as i:
                for j in range(2):
                    ct = i * 2 + j
                    g1_, g2_ = gT[:, bass.ds(ct, 1), :], gT[:, bass.ds(ct + 16, 1), :]
                    dve.wait_ge(sem("br_proj"), 4 + i * 4 + 2 * j + 1)
                    tt(g1_, bank[2 * j][:, 0:SEQ].unsqueeze(1), g1_, ALU.mult).then_inc(sem("br_used"), 1)
                    dve.wait_ge(sem("br_proj"), 4 + i * 4 + 2 * j + 2)
                    tmp = tmp_g[:, j:j + 1, :]
                    tt(tmp, bank[2 * j + 1][:, 0:SEQ].unsqueeze(1), g2_, ALU.mult).then_inc(sem("br_used"), 1)
                    dve.wait_ge(sem("br_used"), 4 + i * 4 + 2 * j + 2)
                    tt(g1_, g1_, tmp, ALU.add).then_inc(sem("merged"), 1)
            dve.wait_ge(sem("xres_in"), 16)
            dve.wait_ge(sem("mods_done"), 4 + 16)
            with dve.Fori(0, 4) as i:
                dve.wait_ge(sem("wo_used"), 2 + 2 * i + 2)
                for t in range(2):
                    tt(tmp_m[:, t:t + 1, :], bank[4 + t][:, :].unsqueeze(1), mods[:, 0:1, bass.ds(i * N1, N1)], ALU.mult
                       ).then_inc(sem("mix_scaled"), 1)
                for t in range(2):
                    dve.wait_ge(sem("mix_scaled"), 2 * i + t + 1)
                    x = xn[:, t:t + 1, bass.ds(i * N1, N1)]
                    stt(x, x, ALPHA, tmp_m[:, t:t + 1, :], ALU.mult, ALU.add).then_inc(sem("mix_added"), 1)

            def layer_norm(first, t, x):
                c = [0]
                per = 5
                base = (first * 2 + t) * per

                def chain(ins):
                    c[0] += 1
                    ins.then_inc(sem("ln_step"), 1)
                    dve.wait_ge(sem("ln_step"), base + c[0])

                for k in range(4):
                    m = v.bn_stats(stats[:, t, 6 * k:6 * k + 6], x[:, k * N1:(k + 1) * N1])
                chain(m)
                v.bn_aggr(aggr[:, t, :], stats[:, t, :]).then_inc(sem("var_done"), 1)
                dve.wait_ge(sem("std_done"), 2 * first + t + 1)
                chain(v.reciprocal(rstd[:, t:t + 1], rstd[:, t:t + 1]))
                chain(ts(x, x, aggr[:, t, 0:1], rstd[:, t:t + 1], ALU.subtract, ALU.mult))
                chain(tt(x, x, lnp[:, 0, :], ALU.mult))
                chain(tt(x, x, lnp[:, 1, :], ALU.add))

            dve.wait_ge(sem("ln1_in"), 32)
            dve.wait_ge(sem("mix_added"), 9)
            for t in range(2):
                layer_norm(0, t, xn[:, t, :])
                stt(h2[:, t, :], mods[:, 2, :], 1.0, xn[:, t, :], ALU.add, ALU.mult).then_inc(sem("h2_scaled"), 1)
                dve.wait_ge(sem("h2_scaled"), t + 1)
                tt(h2[:, t, :], h2[:, t, :], mods[:, 1, :], ALU.add).then_inc(sem("h2_done"), 1)
            NEG = -3.0e38
            u32 = lambda x: x.bitcast(U32)
            done = 0

            def top16(rows, vals, inds, src, rep):
                nonlocal done
                ops = (lambda r: v.max(vals(r)[:, 0:8], src(r)),
                       lambda r: v.max_index(u32(inds(r)[:, 0:8]), vals(r)[:, 0:8], src(r)),
                       lambda r: v.match_replace(rep(r), vals(r)[:, 0:8], src(r), NEG),
                       lambda r: v.max(vals(r)[:, 8:16], rep(r)),
                       lambda r: v.max_index(u32(inds(r)[:, 8:16]), vals(r)[:, 8:16], rep(r)))
                for op in ops:
                    for r in rows:
                        m = op(r)
                    done += 1
                    m.then_inc(sem("topk_step"), 1)
                    dve.wait_ge(sem("topk_step"), done)

            for g in range(0, KT, 4):
                dve.wait_ge(sem("sc_copied"), 1 + g + 4)
                top16([(t, c) for c in range(g, g + 4) for t in range(2)], lambda r: tv[:, r[0], r[1], :], lambda r: ti[:, r[0], r[1], :],
                      lambda r: sc[:, r[0], r[1], :], lambda r: sc2[:, r[0], r[1], :])

            def step(ins):
                nonlocal done
                done += 1
                ins.then_inc(sem("topk_step"), 1)
                dve.wait_ge(sem("topk_step"), done)

            step(v.tensor_copy(tf, u32(ti)))

            def candidates(t):
                for h in range(PH):
                    m = tt(cand[:, h, :].rearrange("p (a b) -> p a b", a=TOPK),
                           tv[:, t, 2 * h, :].unsqueeze(2).broadcast_to([P, TOPK, TOPK]),
                           tv[:, t, 2 * h + 1, :].unsqueeze(1).broadcast_to([P, TOPK, TOPK]), ALU.add)
                step(m)
                top16(list(range(PH)), lambda h: bv[:, t, h * TOPK:(h + 1) * TOPK], lambda h: bj[:, t, h * TOPK:(h + 1) * TOPK],
                      lambda h: cand[:, h, :], lambda h: cand2[:, h, :])

            def choose(t):
                for part, ix in ((0, i0), (1, i1)):
                    if part == 0:
                        step(ts(u32(bhi[:, 0, :]), u32(bj[:, t, :]), 4, None, ALU.logical_shift_right))
                    else:
                        step(ts(u32(bhi[:, 0, :]), u32(bj[:, t, :]), 15, None, ALU.bitwise_and))
                    step(v.tensor_copy(bhi[:, 1, :], u32(bhi[:, 0, :])))
                    step(tt(onehot, bhi[:, 1, :].unsqueeze(2).broadcast_to([P, SLOTS, TOPK]),
                            const("iota16").unsqueeze(1).broadcast_to([P, SLOTS, TOPK]), ALU.is_equal))
                    o4 = onehot.rearrange("p (h k) m -> p h k m", h=PH)
                    lists = tf[:, t, part::2, :]
                    step(tt(o4, o4, lists.unsqueeze(2).broadcast_to([P, PH, TOPK, TOPK]), ALU.mult))
                    step(v.tensor_reduce(ix, onehot, AX.X, ALU.add))
                step(stt(u32(idx[:, t, :]), i0, float(NKEYS), i1, ALU.mult, ALU.add))

            def softmax(t, meanwhile=None):
                b3 = bv[:, t, :].rearrange("p (h k) -> p h k", h=PH)
                g3 = gate[:, t, :].rearrange("p (h k) -> p h k", h=PH)
                tt(g3, b3, b3[:, :, 0:1].broadcast_to([P, PH, TOPK]), ALU.subtract).then_inc(sem("bdiff"), 1)
                if meanwhile:
                    meanwhile()
                dve.wait_ge(sem("bexp"), t + 1)
                step(v.tensor_reduce(esum, g3, AX.X, ALU.add))
                step(v.reciprocal(esum, esum))
                step(tt(g3, g3, esum.unsqueeze(2).broadcast_to([P, PH, TOPK]), ALU.mult))

            candidates(0)
            choose(0)
            dve.sem_inc(sem("ring_used"), 7)

            def row_wait(t, n, e):
                dve.wait_ge(sem(f"row_in{e % 8}"), n * 2 + (t * 512 + (e // 8 + 1) * 16))

            def set_idx(t, b, dst, name):
                v.tensor_copy(u32(dst), u32(idx_all[:, bass.ds(b * TOPK + t * SLOTS, TOPK)])).then_inc(sem(name), 1)

            def dot_batch(t, b, n):
                dve.wait_ge(sem("gelu_done"), b + t * PH)
                for e in range(TOPK):
                    row_wait(t, n, e)
                    dve.wait_ge(sem("ring_used"), n + (7 + t * 256 + e))
                    v.tensor_tensor_reduce(junk, ring[:, e % 8, :], h2[:, t, :], 1.0, 0.0, ALU.mult, ALU.add, dots[:, e:e + 1]
                                           ).then_inc(sem("ring_used"), 1)

            def add_batch(t, n):
                for e in range(TOPK):
                    row_wait(t, n, e)
                    dve.wait_ge(sem("ring_used"), n + (7 + t * 256 + e))
                    stt(y_acc[:, t, :], ring[:, e % 8, :], coef[:, e:e + 1], y_acc[:, t, :], ALU.mult, ALU.add
                        ).then_inc(sem("ring_used"), 1)

            def make_coef(t, b, n):
                dve.wait_ge(sem("gelu_done"), b + t * PH + 1)
                dve.wait_ge(sem("ring_used"), n + (7 + t * 256))
                tt(coef, gelu, gate[:, t, bass.ds(b * TOPK, TOPK)], ALU.mult).then_inc(sem("coef_done"), 1)
                dve.wait_ge(sem("coef_done"), b + t * PH + 1)

            set_idx(0, 0, idx_u, "idxu_set")
            v.memset(idx_all[:, 2 * SLOTS:], 0.0)
            v.memset(y_acc, 0.0)
            softmax(0, lambda: candidates(1))

            def both(t, b):
                dot_batch(t, b, b * 32 - 16)
                set_idx(t, b + 1, idx_u, "idxu_set")
                add_batch(t, b * 32)
                set_idx(t, b, idx_v, "idxv_set")
                make_coef(t, b, b * 32 + 16)

            for t in range(2):
                dot_batch(t, 0, 0 if t == 0 else -16)
                set_idx(t, 1, idx_u, "idxu_set")
                if t:
                    add_batch(0, 256)
                set_idx(t, 0, idx_v, "idxv_set")
                make_coef(t, 0, 16)
                if t == 0:
                    both(0, 1)
                    choose(1)
                    softmax(1)
                with dve.Fori(2 - t, PH) as b:
                    both(t, b)
            add_batch(1, 240)
            dve.wait_ge(sem("ring_used"), 7 + 512)
            for t in range(2):
                step(tt(y_acc[:, t, :], y_acc[:, t, :], mods[:, 3, :], ALU.mult))
                step(stt(xn[:, t, :], xn[:, t, :], ALPHA, y_acc[:, t, :], ALU.mult, ALU.add))
            dve.wait_ge(sem("ln2_in"), 32)
            for t in range(2):
                layer_norm(1, t, xn[:, t, :])
                dve.sem_inc(sem("result"), 1)

        @block.gpsimd
        def _(pool):
            pool.wait_ge(sem("gating_step"), 7)
            for s in range(2):
                pool.dma_start(beta_scr[s], xm.rearrange("p h i -> p (h i)")[0:HD, s * SEQ:(s + 1) * SEQ]
                               ).then_inc(sem("beta_out"), 16)
            pool.wait_ge(sem("beta_out"), 32)
            pool.sem_inc(sem("stored"), 1)

            def ada_load(h):
                for e in range(4):
                    pool.wait_ge(sem("ada2_used"), h * 4 + (e + 1))
                    pool.dma_start(wring[:, 3].rearrange("p k n -> p (k n)"), a["w_ada2"][bass.ds(h * 4 + e, 1)].rearrange("o p n -> p (o n)")
                                   ).then_inc(sem("ada_tile_in"), 16)

            def store(h):
                pool.wait_ge(sem("gram_used"), 1 + 4 * h + 2)
                for d in range(2):
                    for s in range(2):
                        dst = mix_scr[s].rearrange("(d h c) (a b) -> d h (c a) b", d=2, h=H, b=CH)[d, bass.ds(h, 1)]
                        dst = dst.rearrange("o (t p) b -> p (o t) b", p=P)
                        pool.dma_start(dst, mt[:, d, 2 * s:2 * s + 2, :]).then_inc(sem("mt_out"), 16)
                pool.wait_ge(sem("gram_used"), 1 + 4 * h + 4)
                pool.wait_ge(sem("k_copied"), 1 + h + 1)
                pool.wait_ge(sem("v_copied"), 1 + h + 1)
                pool.dma_start(rec_scr[bass.ds(h, 1)].rearrange("o p n -> p (o n)"), rec).then_inc(sem("rec_out"), 16)
                pool.wait_ge(sem("mt_out"), 64 * h + 64)
                pool.wait_ge(sem("rec_out"), 16 * h + 16)
                pool.sem_inc(sem("stored"), 1)

            pool.wait_ge(sem("zg_proj"), 4 + 16)
            ada_load(0)
            with pool.Fori(1, H) as h:
                ada_load(h)
                store(h - 1)
            store(H - 1)
            pool.sem_inc(sem("inv_stored"), 1)
            for n, s in enumerate((1, 0)):
                if n:
                    pool.wait_ge(sem("solved"), n)
                pool.dma_start(sol.rearrange("p a b -> p (a b)"), mix_scr[s]).then_inc(sem("mix_in"), 16)
                pool.dma_start(sol_b, beta_scr[s].rearrange("h (c i) -> (h c) i", i=CH)).then_inc(sem("mix_in"), 16)
                pool.wait_ge(sem("solved"), n + 1)
                pool.dma_start(inv_scr[s], sol_o.rearrange("p a b -> p (a b)")).then_inc(sem("inv_out"), 16)
                pool.wait_ge(sem("inv_out"), 16 * n + 16)
                pool.sem_inc(sem("inv_stored"), 1)

            def gather(t, n, table, ids):
                for e in range(TOPK):
                    pool.wait_ge(sem("ring_used"), n + (t * 256 + e))
                    pool.sem_inc(sem("pool_passed"), 1)
                    pool.indirect_dma_start(ring[:, e % 8, :], None, a[table],
                                            bass.IndirectOffsetOnAxis(ap=ids[:, e:e + 1].bitcast(U32), axis=0)
                                            ).then_inc(sem(f"row_in{e % 8}"), 16)

            for t in range(2):
                pool.wait_ge(sem("idxu_set"), t * PH + 1)
                gather(t, 0 if t == 0 else -16, "peer_u", idx_u)
                if t:
                    pool.wait_ge(sem("idxv_set"), PH)
                    gather(0, 256, "peer_v", idx_v)
                with pool.Fori(1, PH) as b:
                    pool.wait_ge(sem("idxu_set"), b + (t * PH + 1))
                    gather(t, b * 32 - 16, "peer_u", idx_u)
                    pool.wait_ge(sem("idxv_set"), b + t * PH)
                    gather(t, b * 32, "peer_v", idx_v)
            pool.wait_ge(sem("idxv_set"), 2 * PH)
            gather(1, 240, "peer_v", idx_v)



def host_layout(i):
    f = lambda v: np.ascontiguousarray(v)
    x, ctx_, c, cc = i["x"][0], i["ctx"][0], i["c"][0], i["c_ctx"]
    w_in = i["w_in"][0]
    o = {}
    o["consts"] = constant_table()
    o["cond"] = f(np.stack([c.reshape(KT, P).T, cc.reshape(KT, P).T], -1))
    o["xcT"] = f(np.concatenate([x.T, ctx_.T], 1).reshape(KT, P, TOK).transpose(1, 0, 2))
    o["x"] = f(x)
    tiles = lambda w: w.reshape(KT, P, -1, P).transpose(2, 1, 0, 3)
    q, k, v, z = (tiles(w_in[:, n * D:(n + 1) * D]) for n in range(4))
    hy = tiles(w_in[:, 4 * D + 64:4 * D + 64 + 3 * D])
    gates = tiles(w_in[:, 7 * D + 64:])
    heads = np.stack([q, k, v], 1).reshape(3 * H, P, KT, P)
    o["w_in"] = f(np.concatenate([heads, z, gates, hy]))
    o["w_ab"] = f(w_in[:, 4 * D:4 * D + 64].reshape(KT, P, 64).transpose(1, 0, 2))
    o["dn_a_log"] = f(i["dn_a_log"][0].reshape(-1))
    o["dn_dt_bias"] = f(i["dn_dt_bias"][0].reshape(-1))
    o["dn_conv"] = f(i["dn_conv_w"][0].reshape(TAPS, 3, H, P).transpose(3, 2, 1, 0).reshape(P, 48, TAPS))
    o["hy_conv"] = f(i["hy_conv_w"][0].reshape(HTAPS, 48, P).transpose(2, 1, 0))
    o["dn_norm_w"] = f(i["dn_norm_w"][0].reshape(P, 1))
    n = SEQ
    t = np.linspace(0.0, 1.0, n, dtype=np.float32)
    bands = np.linspace(1e-4, 15, 16, dtype=np.float32)
    angle = np.float32(2.0 * np.pi / n) * np.arange(n, dtype=np.float32)[:, None] * bands[None, :]
    o["hy_z"] = f(np.concatenate([t[:, None], np.cos(angle), -np.sin(angle)], 1).T.astype(np.float32))
    delta = np.abs(np.linspace(np.log(1e-2) / 1.5, np.log(1e-2) / 0.3, D, dtype=np.float32))
    window = np.exp(-t[:, None] * delta[None, :]).astype(np.float32)
    o["hy_win"] = f(window.reshape(2, P, 4, N1).transpose(2, 1, 0, 3))
    o["hy_w1"] = f(i["hy_w1"][0])
    o["hy_w2"] = f(i["hy_w2"][0])
    o["hy_cols"] = f(np.stack([i["hy_b1"][0], i["hy_b2"][0], i["hy_freq"][0]], 1))
    w3 = np.concatenate([i["hy_w3"][0], i["hy_b3"][0][None, :]], 0)
    o["hy_w3"] = f(w3.reshape(65, 4, 4, N1).transpose(2, 0, 1, 3))
    o["hy_skip"] = f(i["hy_skip"][0].reshape(2, 4, N1).transpose(1, 0, 2))
    o["w_branch"] = f(np.stack([tiles(i["w_branch_dn"][0]), tiles(i["w_branch_hy"][0])], 1).reshape(32, P, KT, P))
    w_ada, b_ada = i["w_ada"][0], i["b_ada"][0]
    o["w_ada1"] = f(w_ada[:, :2 * D].reshape(2, 8, P, 2, 4, N1).transpose(4, 3, 0, 2, 1, 5).reshape(16, P, 8, N1))
    o["b_ada1"] = f(b_ada[:2 * D].reshape(2, 4, N1).transpose(1, 0, 2).reshape(-1))
    o["w_ada2"] = f(w_ada[:, 2 * D:].T.reshape(64, P, D))
    o["b_ada2"] = f(b_ada[2 * D:].reshape(64, P).T)
    o["c_row"] = f(c)
    o["w_out"] = f(i["w_out"][0].reshape(2, 8, P, 4, N1).transpose(3, 0, 2, 1, 4).reshape(8, P, 8, N1))
    o["w_q"] = f(tiles(i["peer_wq"][0]))
    o["subkeys"] = f(i["peer_subkeys"][0].reshape(KT, NKEYS, P).transpose(2, 0, 1))
    for name in ("ln1_g", "ln1_b", "ln2_g", "ln2_b", "peer_u", "peer_v"):
        o[name] = f(i[name][0])
    return o


def kernel(**inputs):
    import concourse.bacc as bacc
    from concourse.bass_utils import run_bass_kernel_spmd

    arrays = host_layout({n: np.asarray(v) for n, v in inputs.items()})
    nc = bacc.Bacc("TRN2", target_bir_lowering=False, num_devices=1)
    a = {n: nc.dram_tensor(n + "_in", v.shape, F32, kind="ExternalInput").ap() for n, v in arrays.items()}
    out = nc.dram_tensor("out_0_dram", (1, SEQ, D), F32, kind="ExternalOutput").ap()
    build(nc, a, out.rearrange("b n d -> (b n) d"))
    r = run_bass_kernel_spmd(nc, [{n + "_in": v for n, v in arrays.items()}], core_ids=[0])
    return r.results[0]["out_0_dram"]
```

```python
from contextlib import ExitStack

import concourse.bass as bass
from concourse import mybir
import numpy as np

F32 = mybir.dt.float32
U32 = mybir.dt.uint32
ALU = mybir.AluOpType
ACT = mybir.ActivationFunctionType
AX = mybir.AxisListType

P = 128
D = 2048
KT = D // P
SEQ = 256
TOK = 2 * SEQ
CH = 64
NCH = SEQ // CH
H = 16
DK = 128
HD = 2 * H
TAPS = 5
HTAPS = 3
PH = 8
TOPK = 16
NKEYS = 128
SLOTS = PH * TOPK
ALPHA = 2.0 ** 0.25
BIG = 1.0e30
N1 = 512

CONST_COLS = {}
_at = 0
for _n, _w in (("ident", 128), ("ones", 128), ("blockones", 128), ("low_half", 128), ("high_half", 128),
               ("cum_f", 128), ("cum_b", 128), ("tri_f", 64), ("tri_b", 64), ("mask_above", 64),
               ("mask_below", 64), ("cos", 512), ("sin", 512), ("icos", 512), ("isin", 512),
               ("iota16", 16), ("not_first", 1)):
    CONST_COLS[_n] = (_at, _at + _w)
    _at += _w
CONST_W = _at


def constant_table():
    t = np.zeros((P, CONST_W), np.float32)
    p = np.arange(P)[:, None]
    c = np.arange(P)[None, :]
    i = np.arange(CH)[None, :]
    same = (p // CH) == (c // CH)

    def put(name, a):
        lo, hi = CONST_COLS[name]
        t[:, lo:hi] = a

    put("ident", p == c)
    put("ones", 1.0)
    put("blockones", same)
    put("low_half", (p < CH) & (c >= 0))
    put("high_half", (p >= CH) & (c >= 0))
    put("cum_f", same & (p <= c))
    put("cum_b", same & (p >= c))
    put("tri_f", (p % CH) <= i)
    put("tri_b", (p % CH) >= i)
    put("mask_above", BIG * (i > p % CH))
    put("mask_below", BIG * (i < p % CH))
    n = np.arange(SEQ, dtype=np.float64)
    ang = 2 * np.pi * (n[:, None] * (n[None, :] + 0.5)) / (2 * SEQ)
    two = lambda a: a.reshape(2, P, SEQ).transpose(1, 0, 2).reshape(P, 2 * SEQ)
    put("cos", two(np.cos(ang)))
    put("sin", two(np.sin(ang)))
    put("icos", two(np.cos(ang.T) / SEQ))
    put("isin", two(np.sin(ang.T) / SEQ))
    put("iota16", np.arange(16)[None, :])
    put("not_first", p > 0)
    return t


def build(nc, a, out):
    with ExitStack() as ctx:
        made = {}

        def sem(name):
            if name not in made:
                made[name] = ctx.enter_context(nc.semaphore(name))
            return made[name]

        ARENA = 52840
        arena = ctx.enter_context(nc.sbuf_tensor("arena", [P, ARENA], F32))
        bank = [ctx.enter_context(nc.psum_tensor(f"bank{i}", [P, N1], F32)) for i in range(8)]

        def area(at, *shape):
            size = int(np.prod(shape))
            assert at + size <= ARENA, (at, shape)
            v = arena[:, at:at + size]
            if len(shape) == 2:
                v = v.rearrange("p (a b) -> p a b", a=shape[0])
            if len(shape) == 3:
                v = v.rearrange("p (a b c) -> p a b c", a=shape[0], b=shape[1])
            return v

        def dram(name, *shape):
            return nc.dram_tensor(name, shape, F32, kind="Internal").ap()

        mix_scr = dram("mix_scr", 2, P, CH * CH)
        inv_scr = dram("inv_scr", 2, P, CH * CH)
        beta_scr = dram("beta_scr", 2, HD, SEQ)
        rec_scr = dram("rec_scr", H, P, 2048)

        cst = area(0, CONST_W)

        def const(name):
            lo, hi = CONST_COLS[name]
            return cst[:, lo:hi]

        HT0 = 3600
        WR0 = HT0 + KT * TOK
        R0 = WR0 + 4 * KT * P
        assert CONST_W <= HT0
        hT = area(HT0, KT, TOK)
        wring = area(WR0, 4, KT * P).rearrange("p s (k n) -> p s k n", k=KT)
        ada_ring = area(R0, 4, 8 * N1).rearrange("p s (k n) -> p s k n", k=8)
        ada_row = area(R0 + 24576, 4, 2 * N1).rearrange("p g (w n) -> p g w n", w=2)
        cond = area(52600, KT, 2)
        adac = area(52640, 64)
        badac = area(52704, 64)
        cond_row = area(R0 + 22240, D)
        ada_junk = area(R0 + 28672, D)
        ada_dot = area(52768, 4)
        cols = area(R0 + 20540, KT, 4).rearrange("p k (w s) -> p k w s", w=2)
        G0 = R0 + 12288
        w_ab = area(R0 + 19500, KT, CH)
        abT = area(G0 + 512, TOK)
        ab = area(G0 + 1024, 4, 64)
        xs = area(G0 + 1280, 4, HD)
        sp_m = area(G0 + 1408, 4, HD)
        sp_e = area(G0 + 1536, 4, HD)
        gate_row = area(R0 + 20620, 2, HD)
        gx = area(G0 + 2048, HD, CH)
        xm = area(G0 + 4096, HD, CH)
        xm2 = area(G0 + 6144, H, CH)
        K0 = 50900
        g_tok = area(K0, 4, HD)
        beta = area(K0 + 128, 4, HD)
        gcum = area(K0 + 256, 4, HD)
        eg = area(K0 + 384, 4, HD)
        neg_eg = area(K0 + 512, 4, HD)
        etail = area(K0 + 640, 4, HD)
        etot = area(K0 + 768, 2, 4 * HD)
        dn_nw = area(K0 + 1024, 1)
        eps6 = area(K0 + 1025, 1)
        eps5 = area(K0 + 1026, 1)
        hyc = area(K0 + 1032, 48, HTAPS)
        n_e1f = area(R0, 4, H * CH).rearrange("p t (h i) -> p t h i", h=H)
        n_eb = area(R0 + 4096, 4, H * CH).rearrange("p t (h i) -> p t h i", h=H)
        a_e2f = area(R0 + 8192, 2, H * CH).rearrange("p t (h i) -> p t h i", h=H)
        a_eb = area(R0 + 10240, 2, H * CH).rearrange("p t (h i) -> p t h i", h=H)
        X0 = R0 + 12288
        PADL, PADC = CH + TAPS - 1, SEQ + TAPS - 1
        cw = NCH * PADL + PADC
        cbuf = area(X0, 3, cw)
        acc = area(X0 + 1600, 3, TOK)
        raw = area(X0 + 3200, 3, TOK)
        sq = area(X0 + 4800, 2, TOK)
        nrm = area(X0 + 5900, 2, TOK)
        rec = area(X0 + 7000, 2048)
        mt = area(X0 + 9100, 2, 4 * CH).rearrange("p d (t i) -> p d t i", t=4)
        dnc = area(X0 + 9700, 48, TAPS)
        r_kT = rec[:, 0:512]
        r_qT = rec[:, 512:768]
        r_k = rec[:, 768:1280]
        r_v = rec[:, 1280:1792]
        r_at = rec[:, 1792:2048].rearrange("p (d t i) -> p d t i", d=2, t=2)

        c_lat = [cbuf[:, t, 0:NCH * PADL].rearrange("p (r w) -> p r w", r=NCH) for t in range(3)]
        c_ctx = [cbuf[:, t, NCH * PADL:cw] for t in range(3)]

        zsT = area(R0 + 24576, KT, SEQ)
        gT = area(R0 + 4096, 2 * KT, SEQ)
        yhT = area(R0 + 12288, KT, SEQ)
        uv = area(R0 + 16384, 2, 2 * D)
        sol = area(R0 + 16384, 2 * CH, CH)
        sol_o = area(R0, CH, CH)
        sol_t = area(R0 + 12288, CH * CH // 4)
        sol_b = area(R0 + 13400, 2, CH)
        hbuf = area(R0 + 28672, 8, NCH * (CH + 2)).rearrange("p s (r w) -> p s r w", r=NCH)
        hacc = area(R0 + 14336, 4, SEQ)
        mixed = area(K0 + 1200, 6, 4 * H).rearrange("p m (t h) -> p m t h", t=4)
        w3c = area(HT0, 4, N1)
        win = area(HT0 + 2048, 2, N1)
        skipc = area(HT0 + 3072, 2, N1)
        fa = area(HT0 + 4096, 2, N1)
        fb = area(HT0 + 5120, 2, N1)
        Fr = area(HT0 + 6144, 2, N1)
        Fi = area(HT0 + 7168, 2, N1)
        t1 = area(HT0 + 8192, 2, N1)
        t2 = area(HT0 + 9216, 2, N1)
        Yr = area(HT0 + 10240, 2, N1)
        Yi = area(HT0 + 11264, 2, N1)
        yb = area(HT0 + 12288, 2, N1)
        zT = area(HT0 + 13312, SEQ)
        hid1 = area(HT0 + 13568, SEQ)
        hid2 = area(HT0 + 13824, SEQ)
        ang = area(HT0 + 14080, SEQ)
        turns = area(HT0 + 14336, SEQ)
        fw1 = area(HT0 + 14592, CH)
        fw2 = area(HT0 + 14656, CH)
        fcol = area(HT0 + 14720, 3)
        mods = area(R0 + 16384, 4, D)
        SC0 = R0 + 16384
        recs = area(HT0, 8, 2048)
        invs = [area(at, 4, 1024).rearrange("p u (q t w i) -> p u q t w i", q=2, t=2, w=2) for at in (R0, R0 + 20480)]
        att = area(R0 + 28672, 4, 512).rearrange("p u (t w i) -> p u t w i", t=2, w=2)
        state = area(SC0, 8, P)
        r_in = area(SC0 + 1024, 4, P)
        v_new = area(SC0 + 1536, 4, P)
        v_tail = area(SC0 + 2048, 4, P)
        o_acc = area(SC0 + 2560, 8, P)
        o_sq = area(SC0 + 3584, P)
        o_ss = area(SC0 + 3712, 8)
        tmp_g = area(R0 + 28672, 2, SEQ)
        wo_ring = area(HT0, 2, 8 * N1).rearrange("p s (k n) -> p s k n", k=8)
        tmp_m = area(R0 + 29184, 2, N1)
        xn = area(R0 + 12288, 2, D)
        lnp = area(R0, 2, D)
        h2 = area(R0 + 8192, 2, D)
        stats = area(K0 + 1200, 2, 24)
        aggr = area(K0 + 1250, 2, 2)
        rstd = area(K0 + 1256, 2)
        h2T = area(HT0, KT, SEQ)
        subk = area(R0 + 24576, KT, NKEYS)
        q_sb = area(R0 + 26624, 4, SEQ)
        sc = area(R0 + 4096, 2, KT * NKEYS).rearrange("p t (c n) -> p t c n", c=KT)
        tv = area(R0 + 28672, 2, KT * TOPK).rearrange("p t (c n) -> p t c n", c=KT)
        ti = area(R0 + 29184, 2, KT * TOPK).rearrange("p t (c n) -> p t c n", c=KT)
        sc2 = area(R0 + 16384, 2, KT * NKEYS).rearrange("p t (c n) -> p t c n", c=KT)
        cand = area(R0 + 20480, 2, TOPK * TOPK)
        cand2 = area(R0 + 20992, 2, TOPK * TOPK)
        onehot = area(R0 + 21504, 2 * TOPK, TOPK)
        bv = area(R0 + 29696, 2, SLOTS)
        bj = area(R0 + 29952, 2, SLOTS)
        bhi = area(R0 + 30208, 2, SLOTS)
        tf = area(R0 + 27648, 2, KT * TOPK).rearrange("p t (c n) -> p t c n", c=KT)
        i0 = area(R0 + 28160, SLOTS)
        i1 = area(R0 + 28288, SLOTS)
        idx = area(R0 + 30464, 2, SLOTS)
        idx_all = area(R0 + 30464, 2 * SLOTS + TOPK)
        gate = area(K0, 2, SLOTS)
        esum = area(K0 + 256, PH)
        ring = area(HT0, 8, D)
        y_acc = area(R0 + 4096, 2, D)
        junk = area(R0 + 24576, D)
        idx_u = area(K0 + 300, TOPK)
        idx_v = area(K0 + 320, TOPK)
        dots = area(K0 + 340, TOPK)
        gelu = area(K0 + 360, TOPK)
        coef = area(K0 + 380, TOPK)
        assert K0 >= R0 + 30464 + 2 * SLOTS + TOPK

        block = ctx.enter_context(nc.Block())

        HF = (slice(0, CH), slice(CH, P))

        @block.sync
        def _(sp):
            sp.dma_start(cond, a["cond"]).then_inc(sem("cond_in"), 16)
            sp.dma_start(ada_row[0:2].rearrange("p g w n -> p (g w n)"), a["b_ada1"].partition_broadcast(2)).then_inc(sem("bada_in"), 16)
            for s in range(4):
                sp.dma_start(ada_ring[:, s], a["w_ada1"][s]).then_inc(sem(f"slot_in{4 + s}"), 16)
                if s == 1:
                    sp.dma_start(cst, a["consts"]).then_inc(sem("consts_in"), 16)
            sp.dma_start(hT, a["xcT"]).then_inc(sem("x_in"), 16)
            with sp.Fori(1, 4) as i:
                for s in range(4):
                    sp.wait_ge(sem("ada_used"), i * 4 + (s - 3))
                    sp.dma_start(ada_ring[:, s], a["w_ada1"][bass.ds(i * 4 + s, 1)].rearrange("o p k n -> p (o k) n")
                                 ).then_inc(sem(f"slot_in{4 + s}"), 16)
            sp.dma_start(badac, a["b_ada2"]).then_inc(sem("badac_in"), 16)
            sp.dma_start(cond_row, a["c_row"].partition_broadcast(P)).then_inc(sem("badac_in"), 16)
            sp.dma_start(w_ab, a["w_ab"]).then_inc(sem("wab_in"), 16)
            sp.dma_start(gate_row[:, 0, :], a["dn_a_log"].partition_broadcast(P)).then_inc(sem("gate_in"), 16)
            sp.dma_start(gate_row[:, 1, :], a["dn_dt_bias"].partition_broadcast(P)).then_inc(sem("gate_in"), 16)
            sp.dma_start(hyc, a["hy_conv"]).then_inc(sem("hyc_in"), 16)
            sp.dma_start(dn_nw, a["dn_norm_w"]).then_inc(sem("hyc_in"), 16)
            sp.dma_start(dnc, a["dn_conv"]).then_inc(sem("dnc_in"), 16)
            with sp.Fori(0, 4) as i:
                for s in range(4):
                    sp.wait_ge(sem("zg_proj"), 1 + i * 4 + s)
                    sp.dma_start(wring[:, s], a["w_in"][bass.ds(i * 4 + (48 + s), 1)].rearrange("o p k n -> p (o k) n")
                                 ).then_inc(sem(f"slot_in{s}"), 16)
            for t in range(3):
                sp.wait_ge(sem("zg_proj"), 4 + 12 + t + 1)
                sp.dma_start(wring[:, t], a["w_in"][t]).then_inc(sem(f"slot_in{t}"), 16)
            with sp.Fori(1, H) as h:
                for t in range(3):
                    sp.wait_ge(sem("proj"), 1 + 3 * h + t)
                    sp.dma_start(wring[:, t], a["w_in"][bass.ds(3 * h + t, 1)].rearrange("o p k n -> p (o k) n")
                                 ).then_inc(sem(f"slot_in{t}"), 16)
            for s in range(4):
                if s < 3:
                    sp.wait_ge(sem("proj"), 3 + 3 * (H - 1) + s + 1)
                else:
                    sp.wait_ge(sem("ada2_used"), 1 + 4 * H)
                sp.dma_start(wring[:, s], a["w_in"][64 + s]).then_inc(sem(f"slot_in{s}"), 16)
            with sp.Fori(5, 12) as i:
                for s in range(4):
                    sp.wait_ge(sem("zg_proj"), 1 + i * 4 + s)
                    sp.dma_start(wring[:, s], a["w_in"][bass.ds(i * 4 + (48 + s), 1)].rearrange("o p k n -> p (o k) n")
                                 ).then_inc(sem(f"slot_in{s}"), 16)
            for s in range(4):
                sp.wait_ge(sem("zg_proj"), 4 + 44 + s + 1)
                sp.dma_start(wring[:, s], a["w_in"][96 + s]).then_inc(sem(f"slot_in{s}"), 16)
            with sp.Fori(1, 12) as i:
                for s in range(4):
                    sp.wait_ge(sem("hy_proj"), 1 + i * 4 + s)
                    sp.dma_start(wring[:, s], a["w_in"][bass.ds(i * 4 + (96 + s), 1)].rearrange("o p k n -> p (o k) n")
                                 ).then_inc(sem(f"slot_in{s}"), 16)
            sp.wait_ge(sem("hy_proj"), 4 + 48)
            sp.dma_start(zT[0:33, :], a["hy_z"]).then_inc(sem("hyf_in"), 16)
            sp.dma_start(fw1[0:33, :], a["hy_w1"]).then_inc(sem("hyf_in"), 16)
            sp.dma_start(fw2[0:CH, :], a["hy_w2"]).then_inc(sem("hyf_in"), 16)
            sp.dma_start(fcol[0:CH, :], a["hy_cols"]).then_inc(sem("hyf_in"), 16)
            with sp.Fori(0, 4) as n:
                sp.wait_ge(sem("fil_used"), 1 + 2 * n)
                sp.dma_start(w3c[0:65], a["hy_w3"][bass.ds(n, 1)].rearrange("o p k n -> p (o k) n")).then_inc(sem("w3_in"), 16)
                sp.dma_start(win, a["hy_win"][bass.ds(n, 1)].rearrange("o p k n -> p (o k) n")).then_inc(sem("w3_in"), 16)
                sp.dma_start(skipc[0:1], a["hy_skip"][bass.ds(n, 1)].rearrange("o (p k) n -> (o p) k n", p=1)).then_inc(sem("w3_in"), 16)
            sp.wait_ge(sem("inv_out"), 32)
            sp.wait_ge(sem("rec_out"), 16 * H)
            with sp.Fori(0, 2) as i:
                for r in range(2):
                    sp.wait_ge(sem("o_merged"), 1 + i * 8 + 4 * r)
                    sp.wait_ge(sem("bd_zero"), 1 + 2 * r)
                    for u in range(4):
                        h = i * 8 + (4 * r + u)
                        for q in range(2):
                            for half in range(2):
                                for w in range(2):
                                    src = inv_scr[q].rearrange("(d h c) (a b) -> d h (c a) b", d=2, h=H, b=CH)[half ^ w, bass.ds(h, 1)]
                                    src = src.rearrange("o (t p) b -> p (o t) b", p=P)[HF[half]]
                                    sp.dma_start(invs[r][HF[half], u, q, :, w, half * CH:(half + 1) * CH], src).then_inc(sem(f"rec_in{r}"), 16)
                    sp.wait_ge(sem("inv_used"), 25)
                    for u in range(4):
                        h = i * 8 + (4 * r + u)
                        sp.dma_start(recs[:, 4 * r + u], rec_scr[bass.ds(h, 1)].rearrange("o p n -> p (o n)")).then_inc(sem(f"rec_in{r}"), 16)
                    sp.wait_ge(sem("o_merged"), 5 + i * 8 + 4 * r)
                    sp.wait_ge(sem("bd_zero"), 2)
                    for u in range(4):
                        h = i * 8 + (4 * r + u)
                        for half in range(2):
                            for w in range(2):
                                d = half ^ w
                                src = rec_scr[bass.ds(h, 1), HF[half], 1792 + 2 * d * CH:1792 + 2 * (d + 1) * CH]
                                sp.dma_start(att[HF[half], u, :, w, half * CH:(half + 1) * CH],
                                             src.rearrange("o p (t n) -> p (o t) n", t=2)).then_inc(sem("att_in"), 16)
            with sp.Fori(0, 8) as i:
                for s in range(4):
                    sp.wait_ge(sem("br_proj"), 1 + i * 4 + s)
                    sp.dma_start(wring[:, s], a["w_branch"][bass.ds(i * 4 + s, 1)].rearrange("o p k n -> p (o k) n")
                                 ).then_inc(sem(f"slot_in{s}"), 16)
            for s in range(2):
                sp.dma_start(wo_ring[:, s], a["w_out"][s]).then_inc(sem(f"wo_in{s}"), 16)
            sp.wait_ge(sem("br_proj"), 4 + 32)
            sp.dma_start(xn, a["x"].rearrange("(t p) n -> p t n", p=P)).then_inc(sem("xres_in"), 16)
            sp.dma_start(lnp[:, 0, :], a["ln1_g"].partition_broadcast(P)).then_inc(sem("ln1_in"), 16)
            sp.dma_start(lnp[:, 1, :], a["ln1_b"].partition_broadcast(P)).then_inc(sem("ln1_in"), 16)
            with sp.Fori(1, 4) as i:
                for s in range(2):
                    sp.wait_ge(sem("wo_used"), 1 + i * 2 + s)
                    sp.dma_start(wo_ring[:, s], a["w_out"][bass.ds(i * 2 + s, 1)].rearrange("o p k n -> p (o k) n")
                                 ).then_inc(sem(f"wo_in{s}"), 16)
            sp.wait_ge(sem("o_merged"), 5 + 16)
            sp.wait_ge(sem("mix_added"), 9)
            sp.dma_start(subk, a["subkeys"]).then_inc(sem("subk_in"), 16)
            with sp.Fori(0, 4) as i:
                for s in range(4):
                    sp.wait_ge(sem("q_proj"), 1 + i * 4 + s)
                    sp.dma_start(wring[:, s], a["w_q"][bass.ds(i * 4 + s, 1)].rearrange("o p k n -> p (o k) n")
                                 ).then_inc(sem(f"slot_in{s}"), 16)
            sp.wait_ge(sem("xn_done"), 1)
            sp.dma_start(lnp[:, 0, :], a["ln2_g"].partition_broadcast(P)).then_inc(sem("ln2_in"), 16)
            sp.dma_start(lnp[:, 1, :], a["ln2_b"].partition_broadcast(P)).then_inc(sem("ln2_in"), 16)
            for t in range(2):
                sp.wait_ge(sem("result"), t + 1)
                sp.dma_start(out[t * P:(t + 1) * P, :], xn[:, t, :]).then_inc(sem("out_done"), 16)
            sp.wait_ge(sem("out_done"), 32)

        @block.tensor
        def _(pe):
            mm = nc.tensor.matmul
            pe.sem_inc(sem("o_turned"), 1)
            pe.sem_inc(sem("zg_proj"), 4)
            pe.wait_ge(sem("cond_done"), 1)

            def ada_rows(i):
                for w in range(2):
                    pe.wait_ge(sem("row_done"), i * 2 + (w + 1))
                    for half in range(2):
                        s = 2 * w + half
                        pe.wait_ge(sem(f"slot_in{4 + s}"), i * 16 + 16)
                        for k in range(8):
                            m = mm(bank[w][0:2, :], cond[:, half * 8 + k, :], ada_ring[:, s, k, :],
                                   start=(half == 0 and k == 0), stop=(half == 1 and k == 7))
                        m.then_inc(sem("ada_used"), 1)

            def ada_turn(i):
                pe.wait_ge(sem("row_done"), i * 2 + (2 + 2))
                pe.wait_ge(sem("cols_done"), i + 1)
                for w in range(2):
                    for e in range(4):
                        m = mm(bank[2][:, 4 * e + 2 * w:4 * e + 2 * w + 2], ada_row[0:2, i, w, e * P:(e + 1) * P],
                               const("ident")[0:2, 0:2], start=True, stop=True)
                m.then_inc(sem("cols_ready"), 1)

            ada_rows(0)
            for i in range(1, 4):
                ada_rows(i)
                if i == 1:
                    pe.wait_ge(sem("consts_in"), 16)
                ada_turn(i - 1)
            ada_turn(3)

            def wide(slot, b, src):
                for k in range(KT):
                    m = mm(bank[b][:, 0:SEQ], wring[:, slot, k, :], src[:, k, 0:SEQ], start=(k == 0), stop=(k == KT - 1))
                return m

            def z_project(i):
                for s in range(4):
                    pe.wait_ge(sem(f"slot_in{s}"), i * 16 + 16)
                    if i * 4 + s >= 2:
                        pe.wait_ge(sem("zg_evac"), 4 + i * 4 + s - 1)
                    wide(s, 0 if s % 2 else 3, hT).then_inc(sem("zg_proj"), 1)

            pe.wait_ge(sem("wab_in"), 16)
            pe.wait_ge(sem("h_done"), 32)
            for k in range(KT):
                m = mm(bank[0][0:CH, :], w_ab[:, k, :], hT[:, k, :], start=(k == 0), stop=(k == KT - 1))
            m.then_inc(sem("abT_ready"), 1)
            pe.wait_ge(sem("abT_copied"), 1)
            for t in range(4):
                for half in range(2):
                    c0 = SEQ * (t // 2) + CH * ((0, 3), (1, 2))[t % 2][half]
                    m = mm(bank[1][HF[half], t * 64:t * 64 + 64], abT[0:CH, c0:c0 + CH], const("ident")[0:CH, 0:CH],
                           start=True, stop=True)
            m.then_inc(sem("gating_mm"), 1)
            pe.wait_ge(sem("gating_step"), 1)
            z_project(0)
            pe.wait_ge(sem("beta_done"), 1)
            for t in range(4):
                m = mm(bank[4][0:HD, t * P:(t + 1) * P], beta[:, t, :], const("ident"), start=True, stop=True)
            m.then_inc(sem("gating_mm"), 1)
            pe.wait_ge(sem("gating_step"), 6)
            gd = lambda d: g_tok[:, :, d * H:(d + 1) * H]
            cum = bank[1][:, 0:128].rearrange("p (t h) -> p t h", t=4)
            mm(cum[:, :, 0:H], const("cum_f"), gd(0), start=True, stop=True)
            m = mm(cum[:, :, H:HD], const("cum_b"), gd(1), start=True, stop=True)
            m.then_inc(sem("gating_mm"), 1)
            gall = g_tok.rearrange("p t h -> p (t h)")
            mm(bank[2][:, 0:128], const("blockones"), gall, start=True, stop=True)
            mm(bank[2][:, 128:256], const("low_half"), gall, start=True, stop=True)
            m = mm(bank[2][:, 256:384], const("high_half"), gall, start=True, stop=True)
            m.then_inc(sem("gating_mm"), 1)
            for t in range(4):
                pe.wait_ge(sem("gx_done"), t + 1)
                if t == 0:
                    pe.wait_ge(sem("gating_step"), 7)
                else:
                    pe.wait_ge(sem("xm_done"), 4 * t)
                for b in range(4):
                    m = mm(bank[4 + b][:, :], const("blockones"), gx.rearrange("p h i -> p (h i)")[:, b * N1:(b + 1) * N1],
                           start=True, stop=True)
                m.then_inc(sem("gb_ready"), 1)
                if t < 3:
                    z_project(t + 1)

            def project(h, t):
                n = SEQ if t == 0 else TOK
                pe.wait_ge(sem(f"slot_in{t}"), 16 * h + (64 + 16))
                pe.wait_ge(sem("proj_copied"), 3 * h + t)
                for k in range(KT):
                    m = mm(bank[t][:, 0:n], wring[:, t, k, :], hT[:, k, 0:n], start=(k == 0), stop=(k == KT - 1))
                m.then_inc(sem("proj"), 1)

            def norms(h):
                for j, n in ((0, SEQ), (1, TOK)):
                    pe.wait_ge(sem("squared"), 2 * h + j + 1)
                    pe.wait_ge(sem("rooted"), 1 + 2 * h)
                    mm((bank[3] if j == 0 else bank[7])[:, 0:n], const("ones"), sq[:, j, 0:n], start=True, stop=True
                       ).then_inc(sem("ssq"), 1)

            def turn(h):
                pe.wait_ge(sem("silued"), 3 * h + 3)
                pe.wait_ge(sem("v_copied"), 1 + h)
                for t in range(4):
                    m = nc.tensor.transpose(bank[5][:, t * P:(t + 1) * P], raw[:, 2, t * P:(t + 1) * P], const("ident"))
                m.then_inc(sem("v_turned"), 1)
                pe.wait_ge(sem("normed"), 1 + 2 * h + 2)
                pe.wait_ge(sem("k_copied"), 1 + h)
                for t in range(4):
                    m = nc.tensor.transpose(bank[4][:, t * P:(t + 1) * P], r_kT[:, t * P:(t + 1) * P], const("ident"))
                m.then_inc(sem("k_turned"), 1)
                pe.wait_ge(sem("gram_used"), 1 + 4 * h)
                for t in range(4):
                    for half in range(2):
                        cs = slice(t * P + half * CH, t * P + half * CH + CH)
                        mm(bank[6][HF[half], t * CH:(t + 1) * CH], r_kT[:, cs], r_kT[:, cs], start=True, stop=True)
                for t in range(2):
                    for half in range(2):
                        cs = slice(t * P + half * CH, t * P + half * CH + CH)
                        m = mm(bank[6][HF[half], 256 + t * CH:256 + (t + 1) * CH], r_kT[:, cs], r_qT[:, cs],
                               start=True, stop=True)
                m.then_inc(sem("gram"), 1)

            def weights_in(slot, use):
                pe.wait_ge(sem(f"slot_in{slot}"), use * 16 + (16 * H * (slot < 3) + 16))

            def gates(i, s):
                weights_in(s, i)
                pe.wait_ge(sem("zg_evac"), 1 + i * 4 + s)
                if isinstance(i, int):
                    pe.wait_ge(sem("proj_copied"), 2 + 3 * H)
                wide(s, 7 if s == 3 else s, hT).then_inc(sem("zg_proj"), 1)

            pe.wait_ge(sem("zg_evac"), 4 + 16)
            pe.sem_inc(sem("proj"), 3)
            for t in range(3):
                project(0, t)
            with pe.Fori(1, H) as h:
                project(h, 0)
                norms(h - 1)
                project(h, 1)
                project(h, 2)
                turn(h - 1)
            gates(4, 0)
            norms(H - 1)
            gates(4, 1)
            gates(4, 2)
            turn(H - 1)
            gates(4, 3)

            with pe.Fori(5, 12) as i:
                for s in range(4):
                    gates(i, s)
            pe.sem_inc(sem("hy_proj"), 4)
            pe.sem_inc(sem("hy_turned"), 4)
            pe.wait_ge(sem("zg_evac"), 4 + 48)

            def hy_project(i, s):
                weights_in(s, i + 12)
                pe.wait_ge(sem("hy_evac"), 1 + i * 4 + s)
                wide(s, s, hT).then_inc(sem("hy_proj"), 1)

            def hy_turn(i, s):
                pe.wait_ge(sem("hy_tap"), 22 + 3 * (i * 4 + s) + 3)
                pe.wait_ge(sem("hy_tcopied"), 1 + i * 4 + s)
                for t in range(2):
                    m = nc.tensor.transpose(bank[4 + s][:, t * P:(t + 1) * P], hacc[:, s, t * P:(t + 1) * P], const("ident"))
                m.then_inc(sem("hy_turned"), 1)

            for s in range(8):
                hy_project(s // 4, s % 4)
            with pe.Fori(2, 10) as i:
                for s in range(4):
                    hy_project(i, s)
                    hy_turn(i - 2, s)
            with pe.Fori(10, 12) as i:
                for s in range(4):
                    hy_project(i, s)
            pe.wait_ge(sem("hyf_in"), 64)
            pe.wait_ge(sem("hy_evac"), 4 + 48)
            mm(bank[0][0:CH, 0:SEQ], fw1[0:33, :], zT[0:33, :], start=True, stop=True).then_inc(sem("hid_mm"), 1)
            pe.wait_ge(sem("hid_done"), 1)
            mm(bank[1][0:CH, 0:SEQ], fw2[0:CH, :], hid1[0:CH, :], start=True, stop=True).then_inc(sem("hid_mm"), 1)
            pe.wait_ge(sem("hid_done"), 3)
            pe.wait_ge(sem("hy_tcopied"), 4 + 32)

            def filters(n, o):
                pe.wait_ge(sem("w3_in"), 48 * n + 48)
                for t in range(2):
                    for d in range(2):
                        m = mm(bank[4 + 2 * d + t][:, :], hid2[0:65, t * P:(t + 1) * P], w3c[0:65, 2 * d + o, :], start=True, stop=True)
                m.then_inc(sem("fil_ready"), 1)

            def convolve(n, o, last):
                c = n * 2 + o
                pe.wait_ge(sem("fil_used"), c + 2)
                for f in range(2):
                    for src, w, b in ((fa, "cos", 4), (fb, "sin", 6)):
                        for t in range(2):
                            m = mm(bank[b + f][:, :], const(w)[:, t * SEQ + f * P:t * SEQ + (f + 1) * P], src[:, t, :],
                                   start=(t == 0), stop=(t == 1))
                    m.then_inc(sem("spec_ready"), 1)
                pe.wait_ge(sem("inv_used"), n * 6 + (1 + 2 * o))
                for f in range(2):
                    for w, b in (("cos", 0), ("sin", 2)):
                        for t in range(2):
                            rhs = yb[:, t, :] if o else uv[:, t, bass.ds(n * N1, N1)]
                            m = mm(bank[b + f][:, :], const(w)[:, t * SEQ + f * P:t * SEQ + (f + 1) * P], rhs,
                                   start=(t == 0), stop=(t == 1))
                    m.then_inc(sem("sig_ready"), 1)
                if not last:
                    pe.wait_ge(sem("spec_copied"), c * 4 + 4)
                    filters(n + o, 1 - o)
                pe.wait_ge(sem("prod_done"), c * 12 + 13)
                if o == 0:
                    for t in range(2):
                        for e, (y, w) in enumerate(((Yr, "icos"), (Yi, "isin"))):
                            for f in range(2):
                                m = mm(bank[t][:, :], const(w)[:, f * SEQ + t * P:f * SEQ + (t + 1) * P], y[:, f, :],
                                       start=(e == 0 and f == 0), stop=(e == 1 and f == 1))
                        m.then_inc(sem("inv_ready"), 1)
                else:
                    for b in range(4):
                        for e, (y, w) in enumerate(((Yr, "icos"), (Yi, "isin"))):
                            for f in range(2):
                                m = mm(bank[b][:, 0:SEQ], y[:, f, b * P:(b + 1) * P], const(w)[:, f * SEQ:(f + 1) * SEQ],
                                       start=(e == 0 and f == 0), stop=(e == 1 and f == 1))
                        m.then_inc(sem("inv_ready"), 1)

            filters(0, 0)
            with pe.Fori(0, 3) as n:
                convolve(n, 0, False)
                convolve(n, 1, False)
            convolve(3, 0, False)
            convolve(3, 1, True)
            pe.wait_ge(sem("inv_used"), 25)
            with pe.Fori(0, 2) as i:
                for r in range(2):
                    grp = i * 2 + r
                    pe.wait_ge(sem(f"rec_in{r}"), 576 * i + 576)
                    kT = lambda u, c: recs[:, 4 * r + u, c:c + CH]
                    qT = lambda u, c: recs[:, 4 * r + u, 512 + c:512 + c + CH]
                    for g in range(8):
                        q, s = g // 4, g % 4
                        t = (0, 1, 1, 0)[s]
                        T = 2 * (1 - q) + t
                        hf = ((0, 1), (1, 0))[s // 2]
                        for u in range(4):
                            if g == 0:
                                continue
                            A = bank[2 * u]
                            pe.wait_ge(sem("state_done"), grp * 56 + ((g - 1) * 8 + 2 * u + 2))
                            for d in range(2):
                                m = mm(A[HF[hf[d]], 0:P], kT(u, T * P + hf[d] * CH), state[:, 2 * u + d, :], start=True, stop=True)
                            if q:
                                for d in range(2):
                                    m = mm(A[HF[hf[d]], P:2 * P], qT(u, t * P + hf[d] * CH), state[:, 2 * u + d, :], start=True, stop=True)
                            m.then_inc(sem("ks_ready"), 1)
                        for u in range(4):
                            if g == 0:
                                pe.wait_ge(sem("o_merged"), 5 + grp * 4)
                                rhs = recs[:, 4 * r + u, 1280 + T * P:1280 + (T + 1) * P]
                            else:
                                pe.wait_ge(sem("r_done"), grp * 28 + ((g - 1) * 4 + u + 1))
                                rhs = r_in[:, u, :]
                            mm(bank[2 * u + 1][:, 0:P], invs[r][:, u, 1 - q, t, s // 2, :], rhs,
                               start=True, stop=True).then_inc(sem("vn_ready"), 1)
                        if g == 4:
                            pe.wait_ge(sem("att_in"), grp * 256 + 256)
                        for u in range(4):
                            if q:
                                pe.wait_ge(sem("vn_done"), grp * 16 + ((g - 4) * 4 + u + 1))
                                mm(bank[2 * u + 1][:, P:2 * P], att[:, u, t, s // 2, :], v_new[:, u, :],
                                   start=True, stop=True).then_inc(sem("av_ready"), 1)
                        for u in range(4):
                            if g < 7:
                                if q:
                                    pe.wait_ge(sem("o_added"), grp * 32 + ((g - 4) * 8 + u + 1))
                                    pe.wait_ge(sem("av_ready"), grp * 16 + ((g - 4) * 4 + u + 1))
                                pe.wait_ge(sem("vtail_done"), grp * 28 + (g * 4 + u + 1))
                                for d in range(2):
                                    hh = HF[hf[d]]
                                    k_tok = recs[hh, 4 * r + u, 768 + T * P:768 + (T + 1) * P]
                                    m = mm(bank[2 * u + d][:, (2 + d) * P:(3 + d) * P], k_tok, v_tail[hh, u, :], start=True, stop=True)
                                m.then_inc(sem("upd_ready"), 1)
                    for u in range(4):
                        pe.wait_ge(sem("o_normed"), grp * 8 + (2 * u + 2))
                        for t in range(2):
                            m = nc.tensor.transpose(bank[2 * u + 1][:, (2 + t) * P:(3 + t) * P], o_acc[:, 2 * u + t, :], const("ident"))
                        m.then_inc(sem("o_turned"), 1)
            pe.sem_inc(sem("br_proj"), 4)
            pe.wait_ge(sem("o_merged"), 5 + 16)
            with pe.Fori(0, 8) as i:
                for s in range(4):
                    weights_in(s, i + 24)
                    pe.wait_ge(sem("br_used"), 1 + i * 4 + s)
                    wide(s, s, (zsT, yhT)[s % 2]).then_inc(sem("br_proj"), 1)
            pe.wait_ge(sem("mods_diag"), 16)
            with pe.Fori(0, 4) as i:
                for j in range(4):
                    pe.wait_ge(sem("mods_done"), 1 + i * 4 + j)
                    mm(bank[4 + j][:, :], const("ones"), mods.rearrange("p s n -> p (s n)")[:, bass.ds(i * D + j * N1, N1)],
                       start=True, stop=True).then_inc(sem("mods_mm"), 1)
            pe.wait_ge(sem("mods_done"), 4 + 16)
            pe.sem_inc(sem("wo_used"), 2)
            pe.wait_ge(sem("merged"), 16)
            with pe.Fori(0, 4) as i:
                for s in range(2):
                    pe.wait_ge(sem(f"wo_in{s}"), i * 16 + 16)
                    if s == 0:
                        pe.wait_ge(sem("mix_added"), 1 + 2 * i)
                    for t in range(2):
                        for k in range(8):
                            m = mm(bank[4 + t][:, :], gT[:, s * 8 + k, t * P:(t + 1) * P], wo_ring[:, s, k, :],
                                   start=(s == 0 and k == 0), stop=(s == 1 and k == 7))
                    m.then_inc(sem("wo_used"), 1)
            pe.sem_inc(sem("q_proj"), 4)
            for t in range(2):
                pe.wait_ge(sem("h2_done"), t + 1)
                for kq in range(4):
                    b = 4 * t + kq
                    for j in range(4):
                        k = 4 * kq + j
                        m = nc.tensor.transpose(bank[b][:, j * P:(j + 1) * P], h2[:, t, k * P:(k + 1) * P], const("ident"))
                    m.then_inc(sem("h2_turned"), 1)
            pe.wait_ge(sem("h2T_done"), 8)
            pe.wait_ge(sem("subk_in"), 16)
            with pe.Fori(0, 4) as i:
                for s in range(4):
                    weights_in(s, i + 32)
                    wide(s, s, h2T).then_inc(sem("q_proj"), 1)
                for s in range(4):
                    pe.wait_ge(sem("q_copied"), i * 4 + s + 1)
                    pe.wait_ge(sem("sc_copied"), 1 + i * 4)
                    for t in range(2):
                        keys = subk[:, bass.ds(i * 4 + s, 1), :].rearrange("p o n -> p (o n)")
                        m = mm(bank[4 + s][:, t * P:(t + 1) * P], q_sb[:, s, t * P:(t + 1) * P], keys, start=True, stop=True)
                    m.then_inc(sem("sc_ready"), 1)

        @block.scalar
        def _(act):
            af = nc.scalar.activation
            for name in ("rooted", "k_copied", "sc_copied"):
                act.sem_inc(sem(name), 1)
            act.wait_ge(sem("cond_in"), 16)
            af(cond, cond, ACT.Silu).then_inc(sem("cond_done"), 1)
            act.wait_ge(sem("gating_step"), 1)
            for d in range(2):
                v = ab.rearrange("p t (d k h) -> p t d k h", d=2, k=2)
                m = af(beta[:, :, d * H:(d + 1) * H], v[:, :, d, 1, :], ACT.Sigmoid)
            m.then_inc(sem("beta_done"), 1)
            act.wait_ge(sem("gating_step"), 3)
            af(sp_e, xs, ACT.Abs).then_inc(sem("sp_act"), 1)
            act.wait_ge(sem("sp_act"), 1)
            af(sp_e, sp_e, ACT.Exp, scale=-1.0).then_inc(sem("sp_act"), 1)
            act.wait_ge(sem("sp_act"), 2)
            af(sp_e, sp_e, ACT.Ln, bias=1.0).then_inc(sem("sp_act"), 1)
            act.wait_ge(sem("gate_in"), 32)
            af(gate_row[:, 0, :], gate_row[:, 0, :], ACT.Exp).then_inc(sem("alog_done"), 1)
            def z_evac(i):
                for s in range(4):
                    act.wait_ge(sem("zg_proj"), 4 + i * 4 + s + 1)
                    af(zsT[:, i * 4 + s, :], bank[0 if s % 2 else 3][:, 0:SEQ], ACT.Silu).then_inc(sem("zg_evac"), 1)

            act.wait_ge(sem("badac_in"), 32)
            af(cond_row, cond_row, ACT.Silu).then_inc(sem("condrow_done"), 1)
            act.sem_inc(sem("zg_evac"), 4)
            z_evac(0)
            act.wait_ge(sem("gating_step"), 10)
            af(etail, etail, ACT.Exp)
            af(eg, gcum, ACT.Exp)
            af(etot, etot, ACT.Exp).then_inc(sem("eg_done"), 1)
            for t in range(4):
                lat = t < 2
                act.wait_ge(sem("xmask_done"), t + 1)
                af(n_e1f[:, t], xm[:, 0:H, :], ACT.Exp, scale=-1.0)
                if lat:
                    af(a_e2f[:, t], xm2, ACT.Exp)
                    af(a_eb[:, t], xm[:, H:HD, :], ACT.Exp)
                af(n_eb[:, t], xm[:, H:HD, :], ACT.Exp).then_inc(sem("exp_done"), 1)
                if t < 3:
                    z_evac(t + 1)

            def evac(h, t):
                act.wait_ge(sem("proj"), 3 + 3 * h + t + 1)
                act.wait_ge(sem("tap"), 25 * h)
                m = af(c_lat[t][:, :, 2:2 + CH], bank[t][:, 0:SEQ].rearrange("p (r w) -> p r w", r=NCH), ACT.Copy)
                if t:
                    m = af(c_ctx[t][:, 2:2 + SEQ], bank[t][:, SEQ:TOK], ACT.Copy)
                m.then_inc(sem("proj_copied"), 1)

            def silu(h, t):
                act.wait_ge(sem("tap"), 25 * h + (5, 15, 25)[t])
                ns = 1 if t == 0 else 2
                src = acc[:, t, 0:ns * SEQ].rearrange("p (s c n) -> p s c n", s=ns, c=NCH)
                dst = raw[:, t, 0:ns * SEQ].rearrange("p (s c n) -> p s c n", s=ns, c=NCH)
                af(dst[:, :, 0:2, :], src[:, :, 0::3, :], ACT.Silu)
                af(dst[:, :, 2:4, :], src[:, :, 1:3, :], ACT.Silu).then_inc(sem("silued"), 1)
                if t < 2:
                    act.wait_ge(sem("silued"), 3 * h + t + 1)
                    af(sq[:, t, 0:ns * SEQ], raw[:, t, 0:ns * SEQ], ACT.Square).then_inc(sem("squared"), 1)

            def roots(h):
                for j, n in ((0, SEQ), (1, TOK)):
                    act.wait_ge(sem("ssq"), 2 * h + j + 1)
                    act.wait_ge(sem("normed"), 1 + 2 * h)
                    af(nrm[:, j, 0:n], (bank[3] if j == 0 else bank[7])[:, 0:n], ACT.Sqrt, bias=eps6[:, 0:1]
                       ).then_inc(sem("rooted"), 1)

            def copy_k(h):
                act.wait_ge(sem("k_turned"), h + 1)
                act.wait_ge(sem("stored"), h + 1)
                af(r_k, bank[4][:, :], ACT.Copy).then_inc(sem("k_copied"), 1)

            act.sem_inc(sem("proj_copied"), 2)
            act.wait_ge(sem("decay_done"), 1)
            for t in range(3):
                evac(0, t)
                silu(0, t)
            with act.Fori(1, H) as h:
                evac(h, 0)
                roots(h - 1)
                act.wait_ge(sem("normed"), 1 + 2 * h)
                silu(h, 0)
                evac(h, 1)
                silu(h, 1)
                evac(h, 2)
                copy_k(h - 1)
                act.wait_ge(sem("v_turned"), h)
                silu(h, 2)
            roots(H - 1)
            copy_k(H - 1)
            act.wait_ge(sem("gram_used"), 1 + 4 * H)

            def zg(i, s, func, dst):
                act.wait_ge(sem("zg_proj"), 4 + i * 4 + s + 1)
                af(dst, bank[7 if s == 3 else s][:, 0:SEQ].unsqueeze(1), func).then_inc(sem("zg_evac"), 1)

            with act.Fori(4, 12) as i:
                for s in range(4):
                    zg(i, s, ACT.Sigmoid, gT[:, bass.ds(i * 4 + (s - 16), 1), :])
            act.sem_inc(sem("hy_evac"), 4)
            act.sem_inc(sem("hy_tcopied"), 4)
            act.wait_ge(sem("hpads"), 1)

            def hy_evac(i, s, odd):
                act.wait_ge(sem("hy_proj"), 4 + i * 4 + s + 1)
                act.wait_ge(sem("hy_tap"), 1 + 3 * (i * 4 + s))
                af(hbuf[:, 4 * odd + s, :, 1:1 + CH], bank[s][:, 0:SEQ].rearrange("p (r w) -> p r w", r=NCH), ACT.Copy
                   ).then_inc(sem("hy_evac"), 1)

            def hy_tcopy(i, s):
                act.wait_ge(sem("hy_turned"), 4 + i * 4 + s + 1)
                af(uv[:, :, bass.ds((i * 4 + s) * P, P)], bank[4 + s][:, 0:2 * P].rearrange("p (t n) -> p t n", t=2), ACT.Copy
                   ).then_inc(sem("hy_tcopied"), 1)

            for s in range(8):
                hy_evac(s // 4, s % 4, s // 4)
            act.wait_ge(sem("inv_out"), 32)
            with act.Fori(1, 5) as n:
                for odd in range(2):
                    for s in range(4):
                        hy_evac(n * 2 + odd, s, odd)
                        hy_tcopy(n * 2 + (odd - 2), s)
            for odd in range(2):
                for s in range(4):
                    hy_evac(10 + odd, s, odd)
            for n, hid in enumerate((hid1, hid2)):
                act.wait_ge(sem("ang_done"), 6 * n + 6)
                af(hid[0:CH, :], ang[0:CH, :], ACT.Sin).then_inc(sem("hid_done"), 1)
            with act.Fori(0, 4) as n:
                for o in range(2):
                    for f in range(2):
                        act.wait_ge(sem("spec_ready"), n * 4 + (2 * o + f + 1))
                        act.wait_ge(sem("prod_done"), n * 24 + (1 + 12 * o))
                        af(Fr[:, f, :], bank[4 + f][:, :], ACT.Copy).then_inc(sem("spec_copied"), 1)
                        af(Fi[:, f, :], bank[6 + f][:, :], ACT.Copy).then_inc(sem("spec_copied"), 1)
            with act.Fori(0, 2) as i:
                for r in range(2):
                    grp = i * 2 + r
                    for g in range(8):
                        q, s = g // 4, g % 4
                        T = 2 * (1 - q) + (0, 1, 1, 0)[s]
                        for u in range(4):
                            h = i * 8 + (4 * r + u)
                            B = bank[2 * u + 1][:, 0:P]
                            act.wait_ge(sem("vn_ready"), grp * 32 + (g * 4 + u + 1))
                            if g < 7:
                                af(v_tail[:, u, :], B, ACT.Copy, scale=mixed[:, 4 + s // 2, T, bass.ds(h, 1)]
                                   ).then_inc(sem("vtail_done"), 1)
                            if q:
                                af(v_new[:, u, :], B, ACT.Copy).then_inc(sem("vn_done"), 1)
                    for u in range(4):
                        act.wait_ge(sem("o_added"), grp * 32 + (24 + 4 + u + 1))
                        for t in range(2):
                            af(o_sq, o_acc[:, 2 * u + t, :], ACT.Square, accum_out=o_ss[:, 2 * u + t:2 * u + t + 1]
                               ).then_inc(sem("o_ss"), 1)
                            act.wait_ge(sem("o_ss"), grp * 9 + (2 * u + t + 1))
                    af(o_ss, o_ss, ACT.Sqrt, bias=eps6[:, 0:1], scale=1.0 / DK).then_inc(sem("o_ss"), 1)
            act.sem_inc(sem("mods_done"), 4)
            with act.Fori(0, 4) as i:
                for j in range(4):
                    act.wait_ge(sem("mods_mm"), i * 4 + (j + 1))
                    af(mods.rearrange("p s n -> p (s n)")[:, bass.ds(i * D + j * N1, N1)], bank[4 + j][:, :], ACT.Copy
                       ).then_inc(sem("mods_done"), 1)
            for t in range(2):
                act.wait_ge(sem("var_done"), t + 1)
                af(rstd[:, t:t + 1], aggr[:, t, 1:2], ACT.Sqrt, bias=eps5[:, 0:1]).then_inc(sem("std_done"), 1)
            for t in range(2):
                for kq in range(4):
                    act.wait_ge(sem("h2_turned"), 4 * t + kq + 1)
                    if t + kq == 0:
                        act.wait_ge(sem("wo_used"), 2 + 8)
                    af(h2T[:, 4 * kq:4 * kq + 4, t * P:(t + 1) * P], bank[4 * t + kq][:, :].rearrange("p (k n) -> p k n", k=4), ACT.Copy
                       ).then_inc(sem("h2T_done"), 1)
            with act.Fori(0, 4) as i:
                for s in range(4):
                    act.wait_ge(sem("q_proj"), 4 + i * 4 + s + 1)
                    af(q_sb[:, s, :], bank[s][:, 0:SEQ], ACT.Copy).then_inc(sem("q_copied"), 1)
                for s in range(4):
                    act.wait_ge(sem("sc_ready"), i * 4 + s + 1)
                    af(sc[:, :, bass.ds(i * 4 + s, 1), :], bank[4 + s][:, 0:2 * P].rearrange("p (t o n) -> p t o n", t=2, o=1), ACT.Copy
                       ).then_inc(sem("sc_copied"), 1)

            def exps(t):
                act.wait_ge(sem("bdiff"), t + 1)
                af(gate[:, t, :], gate[:, t, :], ACT.Exp).then_inc(sem("bexp"), 1)

            def deviation(t):
                act.wait_ge(sem("var_done"), t + 3)
                af(rstd[:, t:t + 1], aggr[:, t, 1:2], ACT.Sqrt, bias=eps5[:, 0:1]).then_inc(sem("std_done"), 1)

            def gelus(t, b, n):
                act.wait_ge(sem("ring_used"), n + (7 + t * 256))
                act.wait_ge(sem("coef_done"), b + t * PH)
                af(gelu, dots, ACT.Gelu).then_inc(sem("gelu_done"), 1)

            exps(0)
            exps(1)
            for t in range(2):
                gelus(t, 0, 16 if t == 0 else 0)
                if t:
                    deviation(0)
                with act.Fori(1, PH) as b:
                    gelus(t, b, b * 32)
            deviation(1)

        @block.vector
        def _(dve):
            v = nc.vector
            tt, stt, ts = v.tensor_tensor, v.scalar_tensor_tensor, v.tensor_scalar
            for name in ("v_copied", "gram_used", "fil_used", "normed", "inv_used", "prod_done", "mix_added"):
                dve.sem_inc(sem(name), 1)
            v.memset(eps6, 1e-6)
            v.memset(eps5, 1e-5)
            dve.sem_inc(sem("cols_done"), 1)
            dve.sem_inc(sem("row_done"), 2)
            dve.wait_ge(sem("bada_in"), 16)
            dve.wait_ge(sem("x_in"), 16)

            def ada_bias(i):
                for w in range(2):
                    dve.wait_ge(sem("ada_used"), i * 4 + 2 * w + 2)
                    r = ada_row[0:2, i, w, :]
                    tt(r, bank[w][0:2, :], r, ALU.add).then_inc(sem("row_done"), 1)

            def modulate(i):
                dve.wait_ge(sem("cols_ready"), i + 1)
                c4 = cols[:, 4 * i:4 * i + 4]
                v4 = bank[2][:, 0:16].rearrange("p (k w s) -> p k w s", k=4, w=2)
                v.tensor_copy(c4[:, :, 0, :], v4[:, :, 0, :])
                ts(c4[:, :, 1, :], v4[:, :, 1, :], 1.0, None, ALU.add).then_inc(sem("cols_done"), 1)
                dve.wait_ge(sem("cols_done"), 1 + i + 1)
                for k in range(4 * i, 4 * i + 4):
                    for s in range(2):
                        x = hT[:, k, s * SEQ:(s + 1) * SEQ]
                        ts(x, x, cols[:, k, 1, s:s + 1], cols[:, k, 0, s:s + 1], ALU.mult, ALU.add
                           ).then_inc(sem("h_done"), 1)

            ada_bias(0)
            for i in range(1, 4):
                ada_bias(i)
                modulate(i - 1)
            modulate(3)
            dve.wait_ge(sem("abT_ready"), 1)
            v.tensor_copy(abT[0:CH, :], bank[0][0:CH, :]).then_inc(sem("abT_copied"), 1)
            dve.wait_ge(sem("gating_mm"), 1)
            v.tensor_copy(ab, bank[1][:, 0:256].rearrange("p (t n) -> p t n", t=4)).then_inc(sem("gating_step"), 1)
            dve.wait_ge(sem("gating_step"), 1)
            dve.wait_ge(sem("gate_in"), 32)
            abv = ab.rearrange("p t (d k h) -> p t d k h", d=2, k=2)
            for d in range(2):
                tt(xs[:, :, d * H:(d + 1) * H], abv[:, :, d, 0, :],
                   gate_row[:, 1, d * H:(d + 1) * H].unsqueeze(1).broadcast_to([P, 4, H]), ALU.add
                   ).then_inc(sem("gating_step"), 1)
            dve.wait_ge(sem("gating_step"), 3)
            ts(sp_m, xs, 0.0, None, ALU.max).then_inc(sem("gating_step"), 1)
            dve.wait_ge(sem("gating_step"), 4)
            dve.wait_ge(sem("sp_act"), 3)
            tt(sp_m, sp_m, sp_e, ALU.add).then_inc(sem("gating_step"), 1)
            dve.wait_ge(sem("gating_step"), 5)
            dve.wait_ge(sem("alog_done"), 1)
            stt(g_tok, sp_m, -1.0, gate_row[:, 0, :].unsqueeze(1).broadcast_to([P, 4, HD]), ALU.mult, ALU.mult
                ).then_inc(sem("gating_step"), 1)
            dve.wait_ge(sem("gating_mm"), 2)
            v.tensor_copy(xm.rearrange("p h i -> p (h i)")[0:HD, 0:512], bank[4][0:HD, :]).then_inc(sem("gating_step"), 1)
            dve.wait_ge(sem("gating_mm"), 3)
            v.tensor_copy(gcum, bank[1][:, 0:128].rearrange("p (t h) -> p t h", t=4)).then_inc(sem("gating_step"), 1)
            dve.wait_ge(sem("gating_mm"), 4)
            dve.wait_ge(sem("gating_step"), 8)
            tt(etail, bank[2][:, 0:128].rearrange("p (t h) -> p t h", t=4), gcum, ALU.subtract).then_inc(sem("gating_step"), 1)
            v.tensor_copy(etot, bank[2][:, 128:384].rearrange("p (u n) -> p u n", u=2)).then_inc(sem("gating_step"), 1)
            dve.wait_ge(sem("eg_done"), 1)
            ts(neg_eg, eg, -1.0, None, ALU.mult)
            dve.wait_ge(sem("gating_step"), 6)
            dve.wait_ge(sem("beta_out"), 32)
            for t in range(4):
                if t:
                    dve.wait_ge(sem("gb_ready"), t)
                for d, tri in ((0, "tri_f"), (1, "tri_b")):
                    m = tt(gx[:, d * H:(d + 1) * H, :],
                           g_tok[:, t, d * H:(d + 1) * H].unsqueeze(2).broadcast_to([P, H, CH]),
                           const(tri).unsqueeze(1).broadcast_to([P, H, CH]), ALU.mult)
                m.then_inc(sem("gx_done"), 1)
                dve.wait_ge(sem("gb_ready"), t + 1)
                if t:
                    dve.wait_ge(sem("exp_done"), t)
                for b in range(4):
                    m = tt(xm[:, 8 * b:8 * b + 8, :], bank[4 + b][:, :].rearrange("p (h i) -> p h i", h=8),
                           gcum[:, t, 8 * b:8 * b + 8].unsqueeze(2).broadcast_to([P, 8, CH]), ALU.subtract)
                    m.then_inc(sem("xm_done"), 1)
                dve.wait_ge(sem("xm_done"), 4 * t + 4)
                up = const("mask_above").unsqueeze(1).broadcast_to([P, H, CH])
                dn = const("mask_below").unsqueeze(1).broadcast_to([P, H, CH])
                if t < 2:
                    tt(xm2, xm[:, 0:H, :], dn, ALU.subtract).then_inc(sem("xm2_done"), 1)
                    dve.wait_ge(sem("xm2_done"), t + 1)
                tt(xm[:, 0:H, :], xm[:, 0:H, :], up, ALU.add)
                tt(xm[:, H:HD, :], xm[:, H:HD, :], up, ALU.subtract).then_inc(sem("xmask_done"), 1)
                dve.wait_ge(sem("exp_done"), t + 1)
                for d, e in ((0, n_e1f), (1, n_eb)):
                    m = stt(e[:, t], e[:, t], -1.0,
                            beta[:, t, d * H:(d + 1) * H].unsqueeze(2).broadcast_to([P, H, CH]), ALU.mult, ALU.mult)
                m.then_inc(sem("nbeta_done"), 1)
            dve.wait_ge(sem("nbeta_done"), 4)
            v.memset(cbuf, 0.0).then_inc(sem("decay_done"), 1)

            def conv(h, t):
                base = 25 * h + (0, 5, 15)[t]
                w = lambda j: dnc[:, bass.ds(3 * h + t, 1), j]
                a_lat = acc[:, t, 0:SEQ].rearrange("p (r w) -> p r w", r=NCH)
                a_ctx = acc[:, t, SEQ:TOK]
                dve.wait_ge(sem("proj_copied"), 2 + 3 * h + t + 1)
                dve.wait_ge(sem("silued"), 3 * h)
                per = 1 if t == 0 else 2
                for j in range(TAPS):
                    if j:
                        dve.wait_ge(sem("tap"), base + per * (j - 1) + 1)
                    x = c_lat[t][:, :, j:j + CH]
                    if j == 0:
                        ts(a_lat, x, w(j), None, ALU.mult).then_inc(sem("tap"), 1)
                    else:
                        stt(a_lat, x, w(j), a_lat, ALU.mult, ALU.add).then_inc(sem("tap"), 1)
                    if t:
                        if j:
                            dve.wait_ge(sem("tap"), base + per * j)
                        x = c_ctx[t][:, j:j + SEQ]
                        if j == 0:
                            ts(a_ctx, x, w(j), None, ALU.mult).then_inc(sem("tap"), 1)
                        else:
                            stt(a_ctx, x, w(j), a_ctx, ALU.mult, ALU.add).then_inc(sem("tap"), 1)

            def ada_tile(h, e):
                dve.wait_ge(sem("ada_tile_in"), h * 64 + (16 * e + 16))
                dve.wait_ge(sem("ada2_used"), h * 4 + (e + 1))
                v.tensor_tensor_reduce(ada_junk, wring[:, 3].rearrange("p k n -> p (k n)"), cond_row, 1.0, 0.0, ALU.mult, ALU.add,
                                       ada_dot[:, e:e + 1]).then_inc(sem("ada2_used"), 1)

            def ada_bias2(h):
                dve.wait_ge(sem("ada2_used"), h * 4 + (1 + 4))
                x = badac[:, bass.ds(h * 4, 4)]
                tt(adac[:, bass.ds(h * 4, 4)], ada_dot, x, ALU.add).then_inc(sem("adac_done"), 1)
                dve.wait_ge(sem("adac_done"), h + 1)

            def normalize(h):
                for j, n in ((0, SEQ), (1, TOK)):
                    dve.wait_ge(sem("rooted"), 1 + 2 * h + j + 1)
                    v.reciprocal(nrm[:, j, 0:n], nrm[:, j, 0:n]).then_inc(sem("recip"), 1)
                dve.wait_ge(sem("stored"), h + 1)
                dve.wait_ge(sem("recip"), 2 * h + 1)
                stt(r_qT, raw[:, 0, 0:SEQ], DK ** -0.5, nrm[:, 0, 0:SEQ], ALU.mult, ALU.mult).then_inc(sem("normed"), 1)
                dve.wait_ge(sem("recip"), 2 * h + 2)
                tt(r_kT, raw[:, 1, :], nrm[:, 1, :], ALU.mult).then_inc(sem("normed"), 1)

            def finish(h):
                dve.wait_ge(sem("v_turned"), h + 1)
                v.tensor_copy(r_v, bank[5][:, :]).then_inc(sem("v_copied"), 1)
                dve.wait_ge(sem("gram"), h + 1)
                dve.wait_ge(sem("stored"), h + 1)
                g = bank[6][:, 0:256].rearrange("p (t o i) -> p t o i", t=4, o=1)
                q = bank[6][:, 256:384].rearrange("p (t o i) -> p t o i", t=2, o=1)
                for d, e in ((0, n_e1f), (1, n_eb)):
                    tt(mt[:, d].unsqueeze(2), g, e[:, :, bass.ds(h, 1), :], ALU.mult).then_inc(sem("gram_used"), 1)
                for d, e in ((0, a_e2f), (1, a_eb)):
                    tt(r_at[:, d].unsqueeze(2), q, e[:, :, bass.ds(h, 1), :], ALU.mult).then_inc(sem("gram_used"), 1)

            dve.wait_ge(sem("dnc_in"), 16)
            dve.wait_ge(sem("condrow_done"), 1)
            dve.sem_inc(sem("ada2_used"), 1)
            for t in range(3):
                conv(0, t)
                ada_tile(0, t)
            ada_tile(0, 3)
            ada_bias2(0)
            with dve.Fori(1, H) as h:
                conv(h, 0)
                normalize(h - 1)
                ada_tile(h, 0)
                conv(h, 1)
                ada_tile(h, 1)
                conv(h, 2)
                ada_tile(h, 2)
                finish(h - 1)
                ada_tile(h, 3)
                ada_bias2(h)
            normalize(H - 1)
            finish(H - 1)
            dve.wait_ge(sem("adac_done"), H)
            v.memset(hbuf, 0.0).then_inc(sem("hpads"), 1)
            dve.sem_inc(sem("o_merged"), 5)
            for m_, x in enumerate((neg_eg, eg, etail)):
                for w_ in range(2):
                    for half in range(2):
                        d = half ^ w_
                        k_ = v.tensor_copy(mixed[HF[half], 2 * m_ + w_], x[HF[half], :, d * H:(d + 1) * H])
            k_.then_inc(sem("mixed_done"), 1)
            for n in range(2):
                dve.wait_ge(sem("mix_in"), 32 * n + 32)
                m_ = sol[:, n * CH:(n + 1) * CH, :]
                for j in range(1, CH - 1):
                    rows = CH - 1 - j
                    tmp = sol_t[:, 0:rows * j].rearrange("p (i c) -> p i c", c=j)
                    below = m_[:, j + 1:CH, 0:j]
                    if j > 1:
                        dve.wait_ge(sem("solve_step"), n * 124 + 2 * (j - 1))
                    tt(tmp, m_[:, j + 1:CH, j:j + 1].broadcast_to([P, rows, j]),
                       m_[:, j:j + 1, 0:j].broadcast_to([P, rows, j]), ALU.mult).then_inc(sem("solve_step"), 1)
                    dve.wait_ge(sem("solve_step"), n * 124 + (2 * (j - 1) + 1))
                    tt(below, below, tmp, ALU.add).then_inc(sem("solve_step"), 1)
                dve.wait_ge(sem("solve_step"), n * 124 + 124)
                v.memset(m_.rearrange("p a b -> p (a b)")[:, 0:CH * CH:CH + 1], 1.0).then_inc(sem("sol_diag"), 1)
                dve.wait_ge(sem("sol_diag"), n + 1)
                dve.wait_ge(sem("inv_stored"), n + 1)
                lo, hi = HF
                b_ = sol_b[:, n:n + 1, :]
                tt(sol_o[lo], m_[lo].rearrange("p r c -> p c r"), b_[lo].rearrange("p o c -> p c o").broadcast_to([CH, CH, CH]), ALU.mult)
                tt(sol_o[hi], m_[hi], b_[hi].broadcast_to([CH, CH, CH]), ALU.mult).then_inc(sem("solved"), 1)
            dve.sem_inc(sem("hy_tap"), 22)
            dve.wait_ge(sem("hyc_in"), 32)

            def hconv(i, s, odd, turned):
                m = i * 4 + s
                w = lambda j: hyc[:, bass.ds(m, 1), j]
                dve.wait_ge(sem("hy_evac"), 4 + m + 1)
                if turned:
                    dve.wait_ge(sem("hy_turned"), 1 + m)
                    o_ = hacc[:, s, :].rearrange("p (r w) -> p r w", r=NCH)
                else:
                    o_ = yhT[:, bass.ds(m - 32, 1), :].rearrange("p o (r w) -> p (o r) w", r=NCH)
                for j in range(HTAPS):
                    if j:
                        dve.wait_ge(sem("hy_tap"), 22 + 3 * m + j)
                    x = hbuf[:, 4 * odd + s, :, j:j + CH]
                    if j == 0:
                        ts(o_, x, w(j), None, ALU.mult).then_inc(sem("hy_tap"), 1)
                    else:
                        stt(o_, x, w(j), o_, ALU.mult, ALU.add).then_inc(sem("hy_tap"), 1)

            for first, last, turned in ((0, 4, True), (4, 6, False)):
                with dve.Fori(first, last) as n:
                    for odd in range(2):
                        for s in range(4):
                            hconv(n * 2 + odd, s, odd, turned)
            MAGIC, TWO_PI = 12582912.0, 6.283185307179586
            T_HI = float(np.float32(6.28125))
            T_MID = float(np.float32(TWO_PI - T_HI))
            T_LO = TWO_PI - T_HI - T_MID
            dve.wait_ge(sem("hyf_in"), 64)
            for n, b in enumerate((0, 1)):
                dve.wait_ge(sem("hid_mm"), n + 1)
                A_, W_ = ang[0:CH, :], turns[0:CH, :]
                steps = 0

                def chain(ins):
                    nonlocal steps
                    steps += 1
                    ins.then_inc(sem("ang_done"), 1)
                    dve.wait_ge(sem("ang_done"), 6 * n + steps)

                chain(ts(A_, bank[b][0:CH, 0:SEQ], fcol[0:CH, n:n + 1], fcol[0:CH, 2:3], ALU.add, ALU.mult))
                chain(ts(W_, A_, 1.0 / TWO_PI, MAGIC, ALU.mult, ALU.add))
                chain(ts(W_, W_, -MAGIC, None, ALU.add))
                chain(stt(A_, W_, -T_HI, A_, ALU.mult, ALU.add))
                chain(stt(A_, W_, -T_MID, A_, ALU.mult, ALU.add))
                stt(A_, W_, -T_LO, A_, ALU.mult, ALU.add).then_inc(sem("ang_clip"), 1)
                dve.wait_ge(sem("ang_clip"), n + 1)
                ts(A_, A_, -3.1415925, 3.1415925, ALU.max, ALU.min).then_inc(sem("ang_done"), 1)
            v.memset(hid2[CH:CH + 1, :], 1.0).then_inc(sem("hid_done"), 1)

            def fold(n, o):
                c = n * 2 + o
                dve.wait_ge(sem("fil_ready"), c + 1)
                dve.wait_ge(sem("w3_in"), 48 * n + 48)
                for t in range(2):
                    tt(t1[:, t, :], bank[4 + t][:, :], win[:, t, :], ALU.mult).then_inc(sem("fstep"), 1)
                    if t == 0:
                        stt(t2[:, t, :], bank[6 + t][:, :], const("not_first"), win[:, t, :], ALU.mult, ALU.mult).then_inc(sem("fstep"), 1)
                    else:
                        tt(t2[:, t, :], bank[6 + t][:, :], win[:, t, :], ALU.mult).then_inc(sem("fstep"), 1)
                for t in range(2):
                    dve.wait_ge(sem("fstep"), c * 6 + (2 * t + 2))
                    tt(fa[:, t, :], t1[:, t, :], t2[:, t, :], ALU.add).then_inc(sem("fstep"), 1)
                    if t == 0:
                        dve.wait_ge(sem("fstep"), c * 6 + 5)
                        tt(fa[0:1, 0, :], fa[0:1, 0, :], skipc[0:1, o, :], ALU.add)
                    m = tt(fb[:, t, :], t1[:, t, :], t2[:, t, :], ALU.subtract)
                m.then_inc(sem("fil_used"), 1)

            def products(n, o, last):
                c = n * 2 + o
                for f in range(2):
                    dve.wait_ge(sem("sig_ready"), c * 2 + (f + 1))
                    dve.wait_ge(sem("spec_copied"), c * 4 + (2 * f + 2))
                    dve.wait_ge(sem("fil_used"), c + 2)
                    ur, ui = bank[f][:, :], bank[2 + f][:, :]
                    done = lambda k: c * 12 + (6 * f + 1 + k)
                    tt(t1[:, f, :], ur, Fr[:, f, :], ALU.mult).then_inc(sem("prod_done"), 1)
                    tt(t2[:, f, :], ui, Fi[:, f, :], ALU.mult).then_inc(sem("prod_done"), 1)
                    dve.wait_ge(sem("prod_done"), done(2))
                    tt(Yr[:, f, :], t1[:, f, :], t2[:, f, :], ALU.subtract).then_inc(sem("prod_done"), 1)
                    dve.wait_ge(sem("prod_done"), done(3))
                    tt(t1[:, f, :], ur, Fi[:, f, :], ALU.mult).then_inc(sem("prod_done"), 1)
                    tt(t2[:, f, :], ui, Fr[:, f, :], ALU.mult).then_inc(sem("prod_done"), 1)
                    dve.wait_ge(sem("prod_done"), done(5))
                    tt(Yi[:, f, :], t1[:, f, :], t2[:, f, :], ALU.add).then_inc(sem("prod_done"), 1)
                if not last:
                    dve.wait_ge(sem("prod_done"), c * 12 + 13)
                    fold(n + o, 1 - o)
                if o == 0:
                    for t in range(2):
                        dve.wait_ge(sem("inv_ready"), n * 6 + (t + 1))
                        tt(yb[:, t, :], bank[t][:, :], uv[:, t, bass.ds(n * N1 + D, N1)], ALU.mult).then_inc(sem("inv_used"), 1)
                else:
                    for b in range(4):
                        dve.wait_ge(sem("inv_ready"), n * 6 + (2 + b + 1))
                        x = yhT[:, bass.ds(n * 4 + b, 1), :]
                        tt(x, bank[b][:, 0:SEQ].unsqueeze(1), x, ALU.mult).then_inc(sem("inv_used"), 1)

            fold(0, 0)
            with dve.Fori(0, 3) as n:
                products(n, 0, False)
                products(n, 1, False)
            products(3, 0, False)
            products(3, 1, True)
            dve.wait_ge(sem("mixed_done"), 1)
            with dve.Fori(0, 2) as i:
                for r in range(2):
                    grp = i * 2 + r
                    dve.wait_ge(sem(f"rec_in{r}"), 576 * i + 576)
                    for g in range(8):
                        q, s = g // 4, g % 4
                        t = (0, 1, 1, 0)[s]
                        T = 2 * (1 - q) + t
                        hf = ((0, 1), (1, 0))[s // 2]
                        for u in range(4):
                            h = i * 8 + (4 * r + u)
                            A = bank[2 * u]
                            fac = lambda kind: mixed[:, 2 * kind + s // 2, T, bass.ds(h, 1)]
                            v_tok = recs[:, 4 * r + u, 1280 + T * P:1280 + (T + 1) * P]
                            if g == 0:
                                continue
                            dve.wait_ge(sem("ks_ready"), grp * 28 + ((g - 1) * 4 + u + 1))
                            stt(r_in[:, u, :], A[:, 0:P], fac(0), v_tok, ALU.mult, ALU.add).then_inc(sem("r_done"), 1)
                            if q:
                                oa = o_acc[:, 2 * u + t, :]
                                if s < 2:
                                    ts(oa, A[:, P:2 * P], fac(1), None, ALU.mult).then_inc(sem("o_added"), 1)
                                else:
                                    dve.wait_ge(sem("o_added"), grp * 32 + ((3 - s) * 8 + 4 + u + 1))
                                    stt(oa, A[:, P:2 * P], fac(1), oa, ALU.mult, ALU.add).then_inc(sem("o_added"), 1)
                        for u in range(4):
                            h = i * 8 + (4 * r + u)
                            if g < 7:
                                dve.wait_ge(sem("upd_ready"), grp * 28 + (g * 4 + u + 1))
                                for d in range(2):
                                    st = state[:, 2 * u + d, :]
                                    tot = etot[:, hf[d], bass.ds(h + (T * HD + d * H), 1)]
                                    upd = bank[2 * u + d][:, (2 + d) * P:(3 + d) * P]
                                    if g == 0:
                                        m = v.tensor_copy(st, upd)
                                    else:
                                        m = stt(st, st, tot, upd, ALU.mult, ALU.add)
                                    m.then_inc(sem("state_done"), 1)
                        if q:
                            for u in range(4):
                                oa = o_acc[:, 2 * u + t, :]
                                dve.wait_ge(sem("av_ready"), grp * 16 + ((g - 4) * 4 + u + 1))
                                if g == 7:
                                    dve.wait_ge(sem("o_added"), grp * 32 + (24 + u + 1))
                                tt(oa, bank[2 * u + 1][:, P:2 * P], oa, ALU.add).then_inc(sem("o_added"), 1)
                    dve.wait_ge(sem("o_ss"), grp * 9 + 9)
                    v.reciprocal(o_ss, o_ss).then_inc(sem("o_rstd"), 1)
                    dve.wait_ge(sem("o_rstd"), grp + 1)
                    for u in range(4):
                        for t in range(2):
                            oa = o_acc[:, 2 * u + t, :]
                            ts(oa, oa, o_ss[:, 2 * u + t:2 * u + t + 1], None, ALU.mult).then_inc(sem("o_normed"), 1)
                    for u in range(4):
                        h = i * 8 + (4 * r + u)
                        dve.wait_ge(sem("o_turned"), 1 + grp * 4 + (u + 1))
                        z_ = zsT[:, bass.ds(h, 1), :].rearrange("p o (c n) -> p (o c) n", c=NCH)
                        for t, zz in ((0, z_[:, 0::3, :]), (1, z_[:, 1:3, :])):
                            m = stt(zz, bank[2 * u + 1][:, (2 + t) * P:(3 + t) * P].rearrange("p (c n) -> p c n", c=2), dn_nw[:, 0:1], zz,
                                    ALU.mult, ALU.mult)
                        m.then_inc(sem("o_merged"), 1)
            with dve.Fori(0, 4) as i:
                for j in range(4):
                    x = mods.rearrange("p s n -> p (s n)")[:, bass.ds(i * D + j * N1, N1)].rearrange("p (k n) -> p k n", k=4)
                    tt(x, const("ident").unsqueeze(1).broadcast_to([P, 4, P]),
                       adac[:, bass.ds(i * 16 + 4 * j, 4)].unsqueeze(2).broadcast_to([P, 4, P]), ALU.mult
                       ).then_inc(sem("mods_diag"), 1)
            dve.sem_inc(sem("br_used"), 4)
            with dve.Fori(0, 8) as i:
                for j in range(2):
                    ct = i * 2 + j
                    g1_, g2_ = gT[:, bass.ds(ct, 1), :], gT[:, bass.ds(ct + 16, 1), :]
                    dve.wait_ge(sem("br_proj"), 4 + i * 4 + 2 * j + 1)
                    tt(g1_, bank[2 * j][:, 0:SEQ].unsqueeze(1), g1_, ALU.mult).then_inc(sem("br_used"), 1)
                    dve.wait_ge(sem("br_proj"), 4 + i * 4 + 2 * j + 2)
                    tmp = tmp_g[:, j:j + 1, :]
                    tt(tmp, bank[2 * j + 1][:, 0:SEQ].unsqueeze(1), g2_, ALU.mult).then_inc(sem("br_used"), 1)
                    dve.wait_ge(sem("br_used"), 4 + i * 4 + 2 * j + 2)
                    tt(g1_, g1_, tmp, ALU.add).then_inc(sem("merged"), 1)
            dve.wait_ge(sem("xres_in"), 16)
            dve.wait_ge(sem("mods_done"), 4 + 16)
            dve.wait_ge(sem("ln1_in"), 32)
            stt(h2[:, 0, :], mods[:, 2, :], 1.0, lnp[:, 1, :], ALU.add, ALU.mult)
            stt(mods[:, 2, :], mods[:, 2, :], 1.0, lnp[:, 0, :], ALU.add, ALU.mult).then_inc(sem("h2_scaled"), 1)
            dve.wait_ge(sem("h2_scaled"), 1)
            tt(mods[:, 1, :], mods[:, 1, :], h2[:, 0, :], ALU.add)
            with dve.Fori(0, 4) as i:
                dve.wait_ge(sem("wo_used"), 2 + 2 * i + 2)
                for t in range(2):
                    tt(tmp_m[:, t:t + 1, :], bank[4 + t][:, :].unsqueeze(1), mods[:, 0:1, bass.ds(i * N1, N1)], ALU.mult
                       ).then_inc(sem("mix_scaled"), 1)
                for t in range(2):
                    dve.wait_ge(sem("mix_scaled"), 2 * i + t + 1)
                    x = xn[:, t:t + 1, bass.ds(i * N1, N1)]
                    stt(x, x, ALPHA, tmp_m[:, t:t + 1, :], ALU.mult, ALU.add).then_inc(sem("mix_added"), 1)

            lns = 0

            def chain(ins):
                nonlocal lns
                lns += 1
                ins.then_inc(sem("ln_step"), 1)
                dve.wait_ge(sem("ln_step"), lns)

            def standardize(first, t, x):
                for k in range(4):
                    m = v.bn_stats(stats[:, t, 6 * k:6 * k + 6], x[:, k * N1:(k + 1) * N1])
                chain(m)
                v.bn_aggr(aggr[:, t, :], stats[:, t, :]).then_inc(sem("var_done"), 1)
                dve.wait_ge(sem("std_done"), 2 * first + t + 1)
                chain(v.reciprocal(rstd[:, t:t + 1], rstd[:, t:t + 1]))
                chain(ts(x, x, aggr[:, t, 0:1], rstd[:, t:t + 1], ALU.subtract, ALU.mult))

            def scale_shift(x):
                chain(tt(x, x, lnp[:, 0, :], ALU.mult))
                chain(tt(x, x, lnp[:, 1, :], ALU.add))

            dve.wait_ge(sem("mix_added"), 9)
            for t in range(2):
                standardize(0, t, xn[:, t, :])
                tt(h2[:, t, :], xn[:, t, :], mods[:, 2, :], ALU.mult).then_inc(sem("h2_scaled"), 1)
                dve.wait_ge(sem("h2_scaled"), 2 + t)
                tt(h2[:, t, :], h2[:, t, :], mods[:, 1, :], ALU.add).then_inc(sem("h2_done"), 1)
            for t in range(2):
                scale_shift(xn[:, t, :])
            dve.sem_inc(sem("xn_done"), 1)
            NEG = -3.0e38
            u32 = lambda x: x.bitcast(U32)
            done = 0

            def top16(rows, vals, inds, src, rep):
                nonlocal done
                ops = (lambda r: v.max(vals(r)[:, 0:8], src(r)),
                       lambda r: v.max_index(u32(inds(r)[:, 0:8]), vals(r)[:, 0:8], src(r)),
                       lambda r: v.match_replace(rep(r), vals(r)[:, 0:8], src(r), NEG),
                       lambda r: v.max(vals(r)[:, 8:16], rep(r)),
                       lambda r: v.max_index(u32(inds(r)[:, 8:16]), vals(r)[:, 8:16], rep(r)))
                for op in ops:
                    for r in rows:
                        m = op(r)
                    done += 1
                    m.then_inc(sem("topk_step"), 1)
                    dve.wait_ge(sem("topk_step"), done)

            def step(ins):
                nonlocal done
                done += 1
                ins.then_inc(sem("topk_step"), 1)
                dve.wait_ge(sem("topk_step"), done)

            def candidates(t, h0):
                for h in (0, 1):
                    c = 2 * (h0 + h)
                    m = tt(cand[:, h, :].rearrange("p (a b) -> p a b", a=TOPK),
                           tv[:, t, c, :].unsqueeze(2).broadcast_to([P, TOPK, TOPK]),
                           tv[:, t, c + 1, :].unsqueeze(1).broadcast_to([P, TOPK, TOPK]), ALU.add)
                step(m)
                top16((0, 1), lambda h: bv[:, t, (h0 + h) * TOPK:(h0 + h + 1) * TOPK], lambda h: bj[:, t, (h0 + h) * TOPK:(h0 + h + 1) * TOPK],
                      lambda h: cand[:, h, :], lambda h: cand2[:, h, :])

            def choose(t, h0):
                at = slice(h0 * TOPK, (h0 + 2) * TOPK)
                for part, ix in ((0, i0), (1, i1)):
                    if part == 0:
                        step(ts(u32(bhi[:, 0, at]), u32(bj[:, t, at]), 4, None, ALU.logical_shift_right))
                    else:
                        step(ts(u32(bhi[:, 0, at]), u32(bj[:, t, at]), 15, None, ALU.bitwise_and))
                    step(v.tensor_copy(bhi[:, 1, at], u32(bhi[:, 0, at])))
                    step(tt(onehot, bhi[:, 1, at].unsqueeze(2).broadcast_to([P, 2 * TOPK, TOPK]),
                            const("iota16").unsqueeze(1).broadcast_to([P, 2 * TOPK, TOPK]), ALU.is_equal))
                    o4 = onehot.rearrange("p (h k) m -> p h k m", h=2)
                    lists = tf[:, t, 2 * h0 + part:2 * h0 + 4:2, :]
                    step(tt(o4, o4, lists.unsqueeze(2).broadcast_to([P, 2, TOPK, TOPK]), ALU.mult))
                    step(v.tensor_reduce(ix[:, at], onehot, AX.X, ALU.add))
                step(stt(u32(idx[:, t, at]), i0[:, at], float(NKEYS), i1[:, at], ALU.mult, ALU.add))

            def softmax(t):
                b3 = bv[:, t, :].rearrange("p (h k) -> p h k", h=PH)
                g3 = gate[:, t, :].rearrange("p (h k) -> p h k", h=PH)
                tt(g3, b3, b3[:, :, 0:1].broadcast_to([P, PH, TOPK]), ALU.subtract).then_inc(sem("bdiff"), 1)
                dve.wait_ge(sem("bexp"), t + 1)
                step(v.tensor_reduce(esum, g3, AX.X, ALU.add))
                step(v.reciprocal(esum, esum))
                step(tt(g3, g3, esum.unsqueeze(2).broadcast_to([P, PH, TOPK]), ALU.mult))

            def set_idx(t, b, dst, name):
                v.tensor_copy(u32(dst), u32(idx_all[:, bass.ds(b * TOPK + t * SLOTS, TOPK)])).then_inc(sem(name), 1)

            for g in range(0, KT, 4):
                dve.wait_ge(sem("sc_copied"), 1 + g + 4)
                if g == KT - 4:
                    dve.sem_inc(sem("ring_used"), 7)
                    set_idx(0, 0, idx_u, "idxu_set")
                top16([(t, c) for c in range(g, g + 4) for t in range(2)], lambda r: tv[:, r[0], r[1], :], lambda r: ti[:, r[0], r[1], :],
                      lambda r: sc[:, r[0], r[1], :], lambda r: sc2[:, r[0], r[1], :])
                step(v.tensor_copy(tf[:, :, g:g + 4, :], u32(ti[:, :, g:g + 4, :])))
                for t in range(2):
                    candidates(t, g // 2)
                    choose(t, g // 2)

            def row_wait(t, n, e):
                dve.wait_ge(sem(f"row_in{e % 8}"), n * 2 + (t * 512 + (e // 8 + 1) * 16))

            def dot_batch(t, b, n):
                dve.wait_ge(sem("gelu_done"), b + t * PH)
                for e in range(TOPK):
                    row_wait(t, n, e)
                    dve.wait_ge(sem("ring_used"), n + (7 + t * 256 + e))
                    v.tensor_tensor_reduce(junk, ring[:, e % 8, :], h2[:, t, :], 1.0, 0.0, ALU.mult, ALU.add, dots[:, e:e + 1]
                                           ).then_inc(sem("ring_used"), 1)

            def add_batch(t, n):
                for e in range(TOPK):
                    row_wait(t, n, e)
                    dve.wait_ge(sem("ring_used"), n + (7 + t * 256 + e))
                    stt(y_acc[:, t, :], ring[:, e % 8, :], coef[:, e:e + 1], y_acc[:, t, :], ALU.mult, ALU.add
                        ).then_inc(sem("ring_used"), 1)

            def make_coef(t, b, n):
                dve.wait_ge(sem("gelu_done"), b + t * PH + 1)
                dve.wait_ge(sem("ring_used"), n + (7 + t * 256))
                tt(coef, gelu, gate[:, t, bass.ds(b * TOPK, TOPK)], ALU.mult).then_inc(sem("coef_done"), 1)
                dve.wait_ge(sem("coef_done"), b + t * PH + 1)

            v.memset(idx_all[:, 2 * SLOTS:], 0.0)
            step(v.memset(y_acc, 0.0))
            for t in range(2):
                softmax(t)

            def residual(t):
                dve.wait_ge(sem("ring_used"), 7 + 256 + (16 if t == 0 else 256))
                step(tt(y_acc[:, t, :], y_acc[:, t, :], mods[:, 3, :], ALU.mult))
                step(stt(xn[:, t, :], xn[:, t, :], ALPHA, y_acc[:, t, :], ALU.mult, ALU.add))
                dve.wait_ge(sem("ln2_in"), 32)
                standardize(1, t, xn[:, t, :])
                scale_shift(xn[:, t, :])
                dve.sem_inc(sem("result"), 1)

            def both(t, b):
                dot_batch(t, b, b * 32 - 16)
                set_idx(t, b + 1, idx_u, "idxu_set")
                add_batch(t, b * 32)
                set_idx(t, b, idx_v, "idxv_set")
                make_coef(t, b, b * 32 + 16)

            for t in range(2):
                dot_batch(t, 0, 0 if t == 0 else -16)
                set_idx(t, 1, idx_u, "idxu_set")
                if t:
                    add_batch(0, 256)
                set_idx(t, 0, idx_v, "idxv_set")
                make_coef(t, 0, 16)
                if t:
                    residual(0)
                with dve.Fori(1, PH) as b:
                    both(t, b)
            add_batch(1, 240)
            residual(1)

        @block.gpsimd
        def _(pool):
            pool.wait_ge(sem("gating_step"), 7)
            for s in range(2):
                pool.dma_start(beta_scr[s], xm.rearrange("p h i -> p (h i)")[0:HD, s * SEQ:(s + 1) * SEQ]
                               ).then_inc(sem("beta_out"), 16)
            pool.wait_ge(sem("beta_out"), 32)
            pool.sem_inc(sem("stored"), 1)

            def ada_load(h):
                for e in range(4):
                    pool.wait_ge(sem("ada2_used"), h * 4 + (e + 1))
                    pool.dma_start(wring[:, 3].rearrange("p k n -> p (k n)"), a["w_ada2"][bass.ds(h * 4 + e, 1)].rearrange("o p n -> p (o n)")
                                   ).then_inc(sem("ada_tile_in"), 16)

            def store(h):
                pool.wait_ge(sem("gram_used"), 1 + 4 * h + 2)
                for d in range(2):
                    for s in range(2):
                        dst = mix_scr[s].rearrange("(d h c) (a b) -> d h (c a) b", d=2, h=H, b=CH)[d, bass.ds(h, 1)]
                        dst = dst.rearrange("o (t p) b -> p (o t) b", p=P)
                        pool.dma_start(dst, mt[:, d, 2 * s:2 * s + 2, :]).then_inc(sem("mt_out"), 16)
                pool.wait_ge(sem("gram_used"), 1 + 4 * h + 4)
                pool.wait_ge(sem("k_copied"), 1 + h + 1)
                pool.wait_ge(sem("v_copied"), 1 + h + 1)
                pool.dma_start(rec_scr[bass.ds(h, 1)].rearrange("o p n -> p (o n)"), rec).then_inc(sem("rec_out"), 16)
                pool.wait_ge(sem("mt_out"), 64 * h + 64)
                pool.wait_ge(sem("rec_out"), 16 * h + 16)
                pool.sem_inc(sem("stored"), 1)

            pool.wait_ge(sem("zg_proj"), 4 + 16)
            ada_load(0)
            with pool.Fori(1, H) as h:
                ada_load(h)
                store(h - 1)
            store(H - 1)
            pool.sem_inc(sem("inv_stored"), 1)
            for n, q in enumerate((1, 0)):
                pool.dma_start(sol[:, n * CH:(n + 1) * CH, :].rearrange("p a b -> p (a b)"), mix_scr[q]).then_inc(sem("mix_in"), 16)
                pool.dma_start(sol_b[:, n, :], beta_scr[q].rearrange("h (c i) -> (h c) i", i=CH)).then_inc(sem("mix_in"), 16)
                pool.wait_ge(sem("mix_in"), 32 * n + 32)
            for n, q in enumerate((1, 0)):
                pool.wait_ge(sem("solved"), n + 1)
                pool.dma_start(inv_scr[q], sol_o.rearrange("p a b -> p (a b)")).then_inc(sem("inv_out"), 16)
                pool.wait_ge(sem("inv_out"), 16 * n + 16)
                pool.sem_inc(sem("inv_stored"), 1)
            pool.wait_ge(sem("solved"), 2)
            nc.gpsimd.memset(invs[0], 0.0).then_inc(sem("bd_zero"), 1)
            pool.wait_ge(sem("hy_tap"), 22 + 3 * 48)
            pool.wait_ge(sem("hy_tcopied"), 4 + 32)
            nc.gpsimd.memset(att, 0.0).then_inc(sem("bd_zero"), 1)
            pool.wait_ge(sem("inv_used"), 25)
            nc.gpsimd.memset(invs[1], 0.0).then_inc(sem("bd_zero"), 1)

            def gather(t, n, table, ids):
                for e in range(TOPK):
                    pool.wait_ge(sem("ring_used"), n + (t * 256 + e))
                    pool.sem_inc(sem("pool_passed"), 1)
                    pool.indirect_dma_start(ring[:, e % 8, :], None, a[table],
                                            bass.IndirectOffsetOnAxis(ap=ids[:, e:e + 1].bitcast(U32), axis=0)
                                            ).then_inc(sem(f"row_in{e % 8}"), 16)

            for t in range(2):
                pool.wait_ge(sem("idxu_set"), t * PH + 1)
                gather(t, 0 if t == 0 else -16, "peer_u", idx_u)
                if t:
                    pool.wait_ge(sem("idxv_set"), PH)
                    gather(0, 256, "peer_v", idx_v)
                with pool.Fori(1, PH) as b:
                    pool.wait_ge(sem("idxu_set"), b + (t * PH + 1))
                    gather(t, b * 32 - 16, "peer_u", idx_u)
                    pool.wait_ge(sem("idxv_set"), b + t * PH)
                    gather(t, b * 32, "peer_v", idx_v)
            pool.wait_ge(sem("idxv_set"), 2 * PH)
            gather(1, 240, "peer_v", idx_v)



def host_layout(i):
    f = lambda v: np.ascontiguousarray(v)
    x, ctx_, c, cc = i["x"][0], i["ctx"][0], i["c"][0], i["c_ctx"]
    w_in = i["w_in"][0]
    o = {}
    o["consts"] = constant_table()
    o["cond"] = f(np.stack([c.reshape(KT, P).T, cc.reshape(KT, P).T], -1))
    o["xcT"] = f(np.concatenate([x.T, ctx_.T], 1).reshape(KT, P, TOK).transpose(1, 0, 2))
    o["x"] = f(x)
    tiles = lambda w: w.reshape(KT, P, -1, P).transpose(2, 1, 0, 3)
    q, k, v, z = (tiles(w_in[:, n * D:(n + 1) * D]) for n in range(4))
    hy = tiles(w_in[:, 4 * D + 64:4 * D + 64 + 3 * D])
    gates = tiles(w_in[:, 7 * D + 64:])
    heads = np.stack([q, k, v], 1).reshape(3 * H, P, KT, P)
    o["w_in"] = f(np.concatenate([heads, z, gates, hy]))
    o["w_ab"] = f(w_in[:, 4 * D:4 * D + 64].reshape(KT, P, 64).transpose(1, 0, 2))
    o["dn_a_log"] = f(i["dn_a_log"][0].reshape(-1))
    o["dn_dt_bias"] = f(i["dn_dt_bias"][0].reshape(-1))
    o["dn_conv"] = f(i["dn_conv_w"][0].reshape(TAPS, 3, H, P).transpose(3, 2, 1, 0).reshape(P, 48, TAPS))
    o["hy_conv"] = f(i["hy_conv_w"][0].reshape(HTAPS, 48, P).transpose(2, 1, 0))
    o["dn_norm_w"] = f(i["dn_norm_w"][0].reshape(P, 1))
    n = SEQ
    t = np.linspace(0.0, 1.0, n, dtype=np.float32)
    bands = np.linspace(1e-4, 15, 16, dtype=np.float32)
    angle = np.float32(2.0 * np.pi / n) * np.arange(n, dtype=np.float32)[:, None] * bands[None, :]
    o["hy_z"] = f(np.concatenate([t[:, None], np.cos(angle), -np.sin(angle)], 1).T.astype(np.float32))
    delta = np.abs(np.linspace(np.log(1e-2) / 1.5, np.log(1e-2) / 0.3, D, dtype=np.float32))
    window = np.exp(-t[:, None] * delta[None, :]).astype(np.float32)
    o["hy_win"] = f(window.reshape(2, P, 4, N1).transpose(2, 1, 0, 3))
    o["hy_w1"] = f(i["hy_w1"][0])
    o["hy_w2"] = f(i["hy_w2"][0])
    o["hy_cols"] = f(np.stack([i["hy_b1"][0], i["hy_b2"][0], i["hy_freq"][0]], 1))
    w3 = np.concatenate([i["hy_w3"][0], i["hy_b3"][0][None, :]], 0)
    o["hy_w3"] = f(w3.reshape(65, 4, 4, N1).transpose(2, 0, 1, 3))
    o["hy_skip"] = f(i["hy_skip"][0].reshape(2, 4, N1).transpose(1, 0, 2))
    o["w_branch"] = f(np.stack([tiles(i["w_branch_dn"][0]), tiles(i["w_branch_hy"][0])], 1).reshape(32, P, KT, P))
    w_ada, b_ada = i["w_ada"][0], i["b_ada"][0]
    o["w_ada1"] = f(w_ada[:, :2 * D].reshape(2, 8, P, 2, 4, N1).transpose(4, 3, 0, 2, 1, 5).reshape(16, P, 8, N1))
    o["b_ada1"] = f(b_ada[:2 * D].reshape(2, 4, N1).transpose(1, 0, 2).reshape(-1))
    o["w_ada2"] = f(w_ada[:, 2 * D:].T.reshape(64, P, D))
    o["b_ada2"] = f(b_ada[2 * D:].reshape(64, P).T)
    o["c_row"] = f(c)
    o["w_out"] = f(i["w_out"][0].reshape(2, 8, P, 4, N1).transpose(3, 0, 2, 1, 4).reshape(8, P, 8, N1))
    o["w_q"] = f(tiles(i["peer_wq"][0]))
    o["subkeys"] = f(i["peer_subkeys"][0].reshape(KT, NKEYS, P).transpose(2, 0, 1))
    for name in ("ln1_g", "ln1_b", "ln2_g", "ln2_b", "peer_u", "peer_v"):
        o[name] = f(i[name][0])
    return o


def kernel(**inputs):
    import concourse.bacc as bacc
    from concourse.bass_utils import run_bass_kernel_spmd

    arrays = host_layout({n: np.asarray(v) for n, v in inputs.items()})
    nc = bacc.Bacc("TRN2", target_bir_lowering=False, num_devices=1)
    a = {n: nc.dram_tensor(n + "_in", v.shape, F32, kind="ExternalInput").ap() for n, v in arrays.items()}
    out = nc.dram_tensor("out_0_dram", (1, SEQ, D), F32, kind="ExternalOutput").ap()
    build(nc, a, out.rearrange("b n d -> (b n) d"))
    r = run_bass_kernel_spmd(nc, [{n + "_in": v for n, v in arrays.items()}], core_ids=[0])
    return r.results[0]["out_0_dram"]
```
